# Optimizing a Trainium2 kernel written in Bass

```python
import jax
import jax.numpy as jnp
from jax import lax
import numpy as np

D_MODEL = 1024
BATCH = 1
SEQ = 256
DEPTH = 1

GRID_W = 64
CTX_LEN = 256

A_HEADS = 8
A_HEAD_DIM = 64
D_A = A_HEADS * A_HEAD_DIM
LORA_W = 64
LORA_A = 64
LORA_G = 128

B_HEADS = 8
B_HEAD_DIM = 64
D_B = B_HEADS * B_HEAD_DIM
WIN_H = 8
WIN_W = 16

N_EXPERTS = 16
N_GROUPS = 4
EXPERTS_PER_GROUP = N_EXPERTS // N_GROUPS
TOP_K = 2
D_EXPERT = 512

RMS_EPS = 1e-6
GN_EPS = 64e-5

IN_SPLITS = (D_A, D_A, D_A, 2 * LORA_W, 2 * LORA_A, LORA_G, D_B, D_B, D_B, D_MODEL, D_MODEL)
IN_COLS = sum(IN_SPLITS)
IN_OFFSETS = tuple(int(o) for o in np.cumsum(IN_SPLITS)[:-1])


def rms_norm(x, g):
    xf = x.astype(jnp.float32)
    y = xf * lax.rsqrt(jnp.mean(xf * xf, axis=-1, keepdims=True) + RMS_EPS)
    return (y * g.astype(jnp.float32)).astype(x.dtype)

def modulate(h, shift, scale):
    return h * (1.0 + scale) + shift

def split_cols(z):
    return jnp.split(z, IN_OFFSETS, axis=-1)

def rwkv_prep(z, w0, w_lora_b, a0, a_lora_b, k_k, k_a):
    f = jnp.float32
    k, v, lw, la = z[1].astype(f), z[2].astype(f), z[3].astype(f), z[4].astype(f)
    bsz, t = k.shape[:2]
    heads = lambda u: u.reshape(bsz, t, A_HEADS, A_HEAD_DIM)
    lw = jnp.tanh(lw).reshape(bsz, t, 2, LORA_W)
    wl = w0.astype(f) + jnp.einsum('btzr,zrc->btzc', lw, w_lora_b.astype(f))
    decay = jnp.exp(-jnp.exp(-jax.nn.softplus(-wl) - 0.5))
    la = la.reshape(bsz, t, 2, LORA_A)
    a = jax.nn.sigmoid(a0.astype(f) + jnp.einsum('btzr,zrc->btzc', la, a_lora_b.astype(f)))
    kk = heads(k * k_k.astype(f))
    kk = kk * lax.rsqrt(jnp.maximum(jnp.sum(kk * kk, axis=-1, keepdims=True), 1e-12))
    k_dir = k[:, :, None, :] * (1.0 + (a - 1.0) * k_a.astype(f))
    per_dir = [(heads(decay[:, :, d]), heads(k_dir[:, :, d]), heads(a[:, :, d])) for d in range(2)]
    return heads(k), heads(v), kk, per_dir

def rwkv_scan(s0, r, decay, k, v, kk, a, reverse, emit):
    def step(s, inp):
        w_t, k_t, v_t, kk_t, a_t = inp[:5]
        s_kk = jnp.einsum('bhvk,bhk->bhv', s, kk_t)
        s = (s * w_t[:, :, None, :]
             - s_kk[..., None] * (kk_t * a_t)[:, :, None, :]
             + v_t[..., None] * k_t[:, :, None, :])
        y = jnp.einsum('bhvk,bhk->bhv', s, inp[5]) if emit else None
        return s, y
    seq = (decay, k, v, kk, a) + ((r,) if emit else ())
    xs = tuple(jnp.moveaxis(u, 1, 0) for u in seq)
    s_final, ys = lax.scan(step, s0, xs, reverse=reverse)
    return s_final, (jnp.moveaxis(ys, 0, 1) if emit else None)

def rwkv_out(y, r, k, v, lg, r_k, g_lora_b, ln_g, ln_b, out_dtype):
    f = jnp.float32
    bsz, t = y.shape[:2]
    mu = jnp.mean(y, axis=-1, keepdims=True)
    var = jnp.mean(jnp.square(y - mu), axis=-1, keepdims=True)
    yn = ((y - mu) * lax.rsqrt(var + GN_EPS)).reshape(bsz, t, D_A) * ln_g.astype(f) + ln_b.astype(f)
    bonus = (jnp.sum(r * k * r_k.astype(f), axis=-1, keepdims=True) * v).reshape(bsz, t, D_A)
    g = jax.nn.sigmoid(lg.astype(f)) @ g_lora_b.astype(f)
    return ((yn + bonus) * g).astype(out_dtype)

def rwkv_mixer(z_c, z_x, w0, w_lora_b, a0, a_lora_b, g_lora_b, k_k, k_a, r_k, ln_g, ln_b, emit_ctx):
    f = jnp.float32
    k_c, v_c, kk_c, dir_c = rwkv_prep(z_c, w0, w_lora_b, a0, a_lora_b, k_k, k_a)
    k_x, v_x, kk_x, dir_x = rwkv_prep(z_x, w0, w_lora_b, a0, a_lora_b, k_k, k_a)
    bsz, seq = z_x[0].shape[:2]
    r_x = z_x[0].astype(f).reshape(bsz, seq, A_HEADS, A_HEAD_DIM)
    r_c = z_c[0].astype(f).reshape(bsz, z_c[0].shape[1], A_HEADS, A_HEAD_DIM) if emit_ctx else None
    y_x, y_c = 0.0, 0.0
    for d in range(2):
        rev = d == 1
        s0 = jnp.zeros((bsz, A_HEADS, A_HEAD_DIM, A_HEAD_DIM), f)
        w_c, kd_c, a_c = dir_c[d]
        s_c, yc_d = rwkv_scan(s0, r_c, w_c, kd_c, v_c, kk_c, a_c, rev, emit_ctx)
        w_x, kd_x, a_x = dir_x[d]
        _, yx_d = rwkv_scan(s_c, r_x, w_x, kd_x, v_x, kk_x, a_x, rev, True)
        y_x = y_x + yx_d
        if emit_ctx:
            y_c = y_c + yc_d
    out_x = rwkv_out(y_x, r_x, k_x, v_x, z_x[5], r_k, g_lora_b, ln_g, ln_b, z_x[0].dtype)
    out_c = rwkv_out(y_c, r_c, k_c, v_c, z_c[5], r_k, g_lora_b, ln_g, ln_b, z_c[0].dtype) if emit_ctx else None
    return out_c, out_x

def na_mixer(z_c, z_x, q_g, k_g, rpb, need_ctx):
    f = jnp.float32
    scale = B_HEAD_DIM ** -0.5

    def heads(u):
        bsz, t = u.shape[:2]
        return u.reshape(bsz, t, B_HEADS, B_HEAD_DIM).transpose(0, 2, 1, 3)

    k_c, v_c = rms_norm(heads(z_c[7]), k_g), heads(z_c[8])
    q_x = rms_norm(heads(z_x[6]), q_g) * scale
    k_x, v_x = rms_norm(heads(z_x[7]), k_g), heads(z_x[8])
    bsz, _, seq, _ = q_x.shape
    rows = seq // GRID_W
    kh = min(WIN_H, rows)
    kw = WIN_W
    grid = lambda u: u.reshape(bsz, B_HEADS, rows, GRID_W, B_HEAD_DIM)
    q_grid, k_grid, v_grid = grid(q_x), grid(k_x), grid(v_x)

    i = jnp.arange(rows)
    key_rows = jnp.clip(i - kh // 2, 0, rows - kh)[:, None] + jnp.arange(kh)[None, :]
    k_blk = k_grid[:, :, key_rows]
    v_blk = v_grid[:, :, key_rows]
    s_lat = jnp.einsum('bhiqd,bhiakd->bhiqak', q_grid, k_blk).astype(f)

    j = jnp.arange(GRID_W)
    col_start = jnp.clip(j - kw // 2, 0, GRID_W - kw)
    in_win = (j[None, :] >= col_start[:, None]) & (j[None, :] < col_start[:, None] + kw)
    d_row = key_rows - i[:, None] + (WIN_H - 1)
    d_col = jnp.clip(j[None, :] - j[:, None], -(WIN_W - 1), WIN_W - 1) + (WIN_W - 1)
    bias = rpb[:, d_row[:, None, :, None], d_col[None, :, None, :]].astype(f)
    s_lat = jnp.where(in_win[:, None, :], s_lat + bias[None], -jnp.inf)

    s_ctx = jnp.einsum('bhiqd,bhcd->bhiqc', q_grid, k_c).astype(f)
    n_lat = kh * GRID_W
    logits = jnp.concatenate([s_lat.reshape(bsz, B_HEADS, rows, GRID_W, n_lat), s_ctx], axis=-1)
    p = jax.nn.softmax(logits, axis=-1).astype(v_x.dtype)
    p_lat = p[..., :n_lat].reshape(bsz, B_HEADS, rows, GRID_W, kh, GRID_W)
    o = (jnp.einsum('bhiqak,bhiakd->bhiqd', p_lat, v_blk)
         + jnp.einsum('bhiqc,bhcd->bhiqd', p[..., n_lat:], v_c))
    y_x = o.transpose(0, 2, 3, 1, 4).reshape(bsz, seq, D_B)

    y_c = None
    if need_ctx:
        q_c = rms_norm(heads(z_c[6]), q_g) * scale
        p_c = jax.nn.softmax(jnp.einsum('bhqd,bhkd->bhqk', q_c, k_c).astype(f), axis=-1).astype(v_c.dtype)
        y_c = jnp.einsum('bhqk,bhkd->bhqd', p_c, v_c).transpose(0, 2, 1, 3).reshape(bsz, -1, D_B)
    return y_c, y_x

def branch_merge(gate_a, gate_b, y_a, y_b, proj_a, proj_b, w_out):
    merged = jax.nn.sigmoid(gate_a) * (y_a @ proj_a) + jax.nn.sigmoid(gate_b) * (y_b @ proj_b)
    return merged @ w_out

def moe(h, router_w, router_bias, w1, w3, w2):
    f = jnp.float32
    shp = h.shape
    t = h.reshape(-1, shp[-1])
    n = t.shape[0]
    scores = jax.nn.sigmoid(t.astype(f) @ router_w.astype(f))
    sel = scores + router_bias.astype(f)
    grp_score = lax.top_k(sel.reshape(n, N_GROUPS, EXPERTS_PER_GROUP), TOP_K)[0].sum(-1)
    best = jnp.argmax(grp_score, axis=-1)
    in_group = (jnp.arange(N_EXPERTS) // EXPERTS_PER_GROUP)[None, :] == best[:, None]
    _, top_idx = lax.top_k(jnp.where(in_group, sel, -jnp.inf), TOP_K)
    top_s = jnp.take_along_axis(scores, top_idx, axis=-1)
    wts = top_s / jnp.sum(top_s, axis=-1, keepdims=True)
    gate = jnp.sum(jax.nn.one_hot(top_idx, N_EXPERTS, dtype=f) * wts[..., None], axis=1).astype(t.dtype)
    out = jnp.zeros_like(t)
    for e in range(N_EXPERTS):
        hid = jax.nn.silu(t @ w1[e]) * (t @ w3[e])
        out = out + gate[:, e:e + 1] * (hid @ w2[e])
    return out.reshape(shp)

def first_inputs(seed: int = 0) -> dict:
    key = jax.random.key(seed)
    ks = iter(jax.random.split(key, 40))
    D = D_MODEL

    def nrm(shape, s):
        return jax.random.normal(next(ks), shape, jnp.float32) * s

    inp = {}
    inp['x'] = nrm((BATCH, SEQ, D), 1.0)
    inp['c'] = nrm((BATCH, D), 1.0)
    inp['ctx'] = nrm((BATCH, CTX_LEN, D), 1.0)
    inp['c_ctx'] = nrm((D,), 1.0)
    inp['mod_w'] = nrm((DEPTH, D, 6 * D), 0.5 * D ** -0.5)
    inp['mod_b'] = nrm((DEPTH, 6 * D), 0.02)
    inp['norm1_g'] = 1.0 + nrm((DEPTH, D), 0.05)
    inp['norm2_g'] = 1.0 + nrm((DEPTH, D), 0.05)
    inp['w_in'] = nrm((DEPTH, D, IN_COLS), D ** -0.5)
    inp['rw_w0'] = jax.random.uniform(next(ks), (DEPTH, 2, D_A), jnp.float32, -6.0, 1.0)
    inp['rw_w_lora_b'] = nrm((DEPTH, 2, LORA_W, D_A), 0.5 * LORA_W ** -0.5)
    inp['rw_a0'] = nrm((DEPTH, 2, D_A), 0.5)
    inp['rw_a_lora_b'] = nrm((DEPTH, 2, LORA_A, D_A), 0.5 * LORA_A ** -0.5)
    inp['rw_g_lora_b'] = nrm((DEPTH, LORA_G, D_A), LORA_G ** -0.5)
    inp['rw_k_k'] = 0.85 + nrm((DEPTH, D_A), 0.05)
    inp['rw_k_a'] = 1.0 + nrm((DEPTH, D_A), 0.05)
    inp['rw_r_k'] = nrm((DEPTH, A_HEADS, A_HEAD_DIM), 0.1)
    inp['rw_ln_g'] = 1.0 + nrm((DEPTH, D_A), 0.05)
    inp['rw_ln_b'] = nrm((DEPTH, D_A), 0.02)
    inp['na_q_g'] = 1.0 + nrm((DEPTH, B_HEAD_DIM), 0.1)
    inp['na_k_g'] = 1.0 + nrm((DEPTH, B_HEAD_DIM), 0.1)
    inp['na_rpb'] = nrm((DEPTH, B_HEADS, 2 * WIN_H - 1, 2 * WIN_W - 1), 0.5)
    inp['proj_a'] = nrm((DEPTH, D_A, D), D_A ** -0.5)
    inp['proj_b'] = nrm((DEPTH, D_B, D), D_B ** -0.5)
    inp['w_out'] = nrm((DEPTH, D, D), D ** -0.5)
    inp['router_w'] = nrm((D, N_EXPERTS), D ** -0.5)
    inp['router_bias'] = nrm((N_EXPERTS,), 0.01)
    inp['moe_w1'] = nrm((DEPTH, N_EXPERTS, D, D_EXPERT), D ** -0.5)
    inp['moe_w3'] = nrm((DEPTH, N_EXPERTS, D, D_EXPERT), D ** -0.5)
    inp['moe_w2'] = nrm((DEPTH, N_EXPERTS, D_EXPERT, D), D_EXPERT ** -0.5)
    return inp

def first_block(x, c, ctx, c_ctx, mod_w, mod_b, norm1_g, norm2_g, w_in,
              rw_w0, rw_w_lora_b, rw_a0, rw_a_lora_b, rw_g_lora_b, rw_k_k, rw_k_a, rw_r_k,
              rw_ln_g, rw_ln_b, na_q_g, na_k_g, na_rpb, proj_a, proj_b, w_out,
              router_w, router_bias, moe_w1, moe_w3, moe_w2):
    for l in range(DEPTH):
        last = l == DEPTH - 1
        m_x = [m[:, None, :] for m in jnp.split(jax.nn.silu(c) @ mod_w[l] + mod_b[l], 6, axis=-1)]
        m_c = jnp.split(jax.nn.silu(c_ctx) @ mod_w[l] + mod_b[l], 6, axis=-1)

        h_x = modulate(rms_norm(x, norm1_g[l]), m_x[0], m_x[1])
        h_c = modulate(rms_norm(ctx, norm1_g[l]), m_c[0], m_c[1])
        z_x = split_cols(h_x @ w_in[l])
        z_c = split_cols(h_c @ w_in[l])
        ya_c, ya_x = rwkv_mixer(z_c, z_x, rw_w0[l], rw_w_lora_b[l], rw_a0[l], rw_a_lora_b[l],
                                rw_g_lora_b[l], rw_k_k[l], rw_k_a[l], rw_r_k[l], rw_ln_g[l], rw_ln_b[l],
                                emit_ctx=not last)
        yb_c, yb_x = na_mixer(z_c, z_x, na_q_g[l], na_k_g[l], na_rpb[l], need_ctx=not last)
        x = x + m_x[2] * branch_merge(z_x[9], z_x[10], ya_x, yb_x, proj_a[l], proj_b[l], w_out[l])

        h2_x = modulate(rms_norm(x, norm2_g[l]), m_x[3], m_x[4])
        x = x + m_x[5] * moe(h2_x, router_w, router_bias, moe_w1[l], moe_w3[l], moe_w2[l])

        if not last:
            ctx = ctx + m_c[2] * branch_merge(z_c[9], z_c[10], ya_c, yb_c, proj_a[l], proj_b[l], w_out[l])
            h2_c = modulate(rms_norm(ctx, norm2_g[l]), m_c[3], m_c[4])
            ctx = ctx + m_c[5] * moe(h2_c, router_w, router_bias, moe_w1[l], moe_w3[l], moe_w2[l])
    return x


DEPTH_2 = 2

HEAD_DIM = 64
Q_BLOCK = 128
MIX_W = 256
N_BRANCH = 4
SB_HEADS = 4
NSA_HEADS = 4
NSA_GATES = 3
CMP_LEN = 32
CMP_STRIDE = 16
SEL_LEN = 64
SEL_TOPK = 16
WINDOW = 512
RET_HEADS = 4
RET_CHUNK = 128
GLA_HEADS = 4
GLA_DK = 32
GLA_DV = 64
GLA_LOWRANK = 16
GLA_TAU = 16.0
GLA_CHUNK = 64
PEER_HEADS = 8
N_KEYS = 128
N_EXPERTS_2 = N_KEYS * N_KEYS
PEER_TOPK = 16
PEER_QDIM = 256
PEER_BLOCK = 128
DN_ALPHA = (2 * DEPTH_2) ** 0.25
DN_BETA = (8 * DEPTH_2) ** -0.25
LN_EPS = 1e-5
NEG = -1e30

IN_WIDTHS = (
    MIX_W, MIX_W, MIX_W,
    NSA_HEADS * HEAD_DIM,
    HEAD_DIM, HEAD_DIM, HEAD_DIM, HEAD_DIM, HEAD_DIM, HEAD_DIM,
    NSA_HEADS * NSA_GATES,
    MIX_W, MIX_W, MIX_W, MIX_W,
    GLA_HEADS * GLA_DK, GLA_HEADS * GLA_DK,
    GLA_HEADS * GLA_DV, GLA_HEADS * GLA_DV,
    GLA_LOWRANK,
    N_BRANCH * D_MODEL,
)
IN_TOTAL = sum(IN_WIDTHS)


def _layer_norm(x, g, b):
    xf = x.astype(jnp.float32)
    mu = jnp.mean(xf, axis=-1, keepdims=True)
    var = jnp.mean(jnp.square(xf - mu), axis=-1, keepdims=True)
    return ((xf - mu) * lax.rsqrt(var + LN_EPS) * g + b).astype(x.dtype)

def _split(h, widths):
    cuts = [int(c) for c in np.cumsum(widths)[:-1]]
    return jnp.split(h, cuts, axis=-1)

def _heads(t, n):
    B, S, _ = t.shape
    return t.reshape(B, S, n, -1).transpose(0, 2, 1, 3)

def _merge_heads(t):
    B, H, S, d = t.shape
    return t.transpose(0, 2, 1, 3).reshape(B, S, H * d)

def _alibi_slopes(n):
    return 2.0 ** (-8.0 * jnp.arange(1, n + 1, dtype=jnp.float32) / n)

def _masked_softmax(s, mask):
    return jax.nn.softmax(jnp.where(mask, s, NEG), axis=-1)

def _band(t, n_prev):
    B, S, D = t.shape
    nb = S // Q_BLOCK
    tp = jnp.pad(t, ((0, 0), (n_prev * Q_BLOCK, 0), (0, 0))).reshape(B, nb + n_prev, Q_BLOCK, D)
    return jnp.concatenate([tp[:, j:j + nb] for j in range(n_prev + 1)], axis=2)

def stick_breaking_attention(q, k, v):
    B, H, S, Dh = q.shape
    nb = S // Q_BLOCK
    scale = Dh ** -0.5
    s_pos = jnp.arange(S)
    qb = q.reshape(B, H, nb, Q_BLOCK, Dh).transpose(2, 0, 1, 3, 4)

    def one_block(args):
        qi, i = args
        z = jnp.einsum('bhqd,bhsd->bhqs', qi, k).astype(jnp.float32) * scale
        t_pos = i * Q_BLOCK + jnp.arange(Q_BLOCK)
        causal = s_pos[None, :] < t_pos[:, None]
        log_1mb = jnp.where(causal, jax.nn.log_sigmoid(-z), 0.0)
        between = lax.cumsum(log_1mb, axis=3, reverse=True) - log_1mb
        w = jnp.where(causal, jnp.exp(jax.nn.log_sigmoid(z) + between), 0.0)
        return jnp.einsum('bhqs,bhsd->bhqd', w.astype(v.dtype), v)

    o = lax.map(one_block, (qb, jnp.arange(nb)))
    return o.transpose(1, 2, 0, 3, 4).reshape(B, H, S, Dh)

def nsa_attention(q, k_cmp, v_cmp, k_slc, v_slc, k_win, v_win, gate_logits, cmp_pos, cmp_wk, cmp_wv):
    B, H, S, Dh = q.shape
    f32 = jnp.float32
    scale = Dh ** -0.5
    slopes = _alibi_slopes(H)[None, :, None, None]
    t_pos = jnp.arange(S)
    nb = S // Q_BLOCK
    t_blk = t_pos.reshape(nb, Q_BLOCK)

    n_cmp = (S - CMP_LEN) // CMP_STRIDE + 1
    tok = jnp.arange(n_cmp)[:, None] * CMP_STRIDE + jnp.arange(CMP_LEN)[None, :]

    def compress(kv, w):
        blk = kv[:, tok] + cmp_pos
        return blk.reshape(B, n_cmp, CMP_LEN * Dh) @ w

    kc = compress(k_cmp, cmp_wk)
    vc = compress(v_cmp, cmp_wv)
    cmp_end = jnp.arange(n_cmp) * CMP_STRIDE + CMP_LEN - 1
    d_c = (t_pos[:, None] - cmp_end[None, :]).astype(f32)
    s_c = jnp.einsum('bhtd,bcd->bhtc', q, kc).astype(f32) * scale - slopes * d_c
    any_c = (t_pos >= CMP_LEN - 1).astype(f32)[:, None]
    p_c = _masked_softmax(s_c, d_c >= 0) * any_c
    o_cmp = jnp.einsum('bhtc,bcd->bhtd', p_c.astype(vc.dtype), vc)

    n_sel = S // SEL_LEN
    c_start = jnp.arange(n_cmp) * CMP_STRIDE
    sel_start = jnp.arange(n_sel) * SEL_LEN
    overlap = ((c_start[:, None] < sel_start[None, :] + SEL_LEN)
               & (c_start[:, None] + CMP_LEN > sel_start[None, :])).astype(f32)
    imp = jnp.einsum('bhtc,cn->btn', p_c, overlap)
    imp = jnp.where(sel_start[None, :] > t_pos[:, None], NEG, imp)
    imp = jnp.where(jnp.arange(n_sel)[None, :] == (t_pos // SEL_LEN)[:, None], -NEG, imp)
    n_top = min(SEL_TOPK, n_sel)
    _, sel_idx = lax.top_k(imp, n_top)

    qb = q.reshape(B, H, nb, Q_BLOCK, Dh).transpose(2, 0, 1, 3, 4)
    ib = sel_idx.reshape(B, nb, Q_BLOCK, n_top).transpose(1, 0, 2, 3)
    b_ix = jnp.arange(B)[:, None, None]

    def sel_block(args):
        qi, ii, ti = args
        pos = (ii[..., None] * SEL_LEN + jnp.arange(SEL_LEN)).reshape(B, Q_BLOCK, n_top * SEL_LEN)
        kk = k_slc[b_ix, pos]
        vv = v_slc[b_ix, pos]
        dist = (ti[None, :, None] - pos).astype(f32)
        s = jnp.einsum('bhqd,bqld->bhql', qi, kk).astype(f32) * scale - slopes * dist[:, None]
        p = _masked_softmax(s, (dist >= 0)[:, None])
        return jnp.einsum('bhql,bqld->bhqd', p.astype(vv.dtype), vv)

    o_slc = lax.map(sel_block, (qb, ib, t_blk)).transpose(1, 2, 0, 3, 4).reshape(B, H, S, Dh)

    n_prev = WINDOW // Q_BLOCK
    Lw = (n_prev + 1) * Q_BLOCK
    kw = _band(k_win, n_prev)
    vw = _band(v_win, n_prev)
    key_pos = (jnp.arange(nb)[:, None] - n_prev) * Q_BLOCK + jnp.arange(Lw)[None, :]
    dist_w = t_blk[:, :, None] - key_pos[:, None, :]
    mask_w = (dist_w >= 0) & (dist_w < WINDOW) & (key_pos[:, None, :] >= 0)
    s_w = (jnp.einsum('bhnqd,bnld->bhnql', q.reshape(B, H, nb, Q_BLOCK, Dh), kw).astype(f32) * scale
           - slopes[..., None] * dist_w.astype(f32))
    p_w = _masked_softmax(s_w, mask_w)
    o_win = jnp.einsum('bhnql,bnld->bhnqd', p_w.astype(vw.dtype), vw).reshape(B, H, S, Dh)

    g = jax.nn.sigmoid(gate_logits.astype(f32)).reshape(B, S, H, NSA_GATES).transpose(0, 2, 1, 3).astype(q.dtype)
    return g[..., 0:1] * o_cmp + g[..., 1:2] * o_slc + g[..., 2:3] * o_win

def retention_block(q, k, v, gate, gn_g, gn_b):
    B, S, _ = q.shape
    H = RET_HEADS
    Dh = MIX_W // H
    C = RET_CHUNK
    n = S // C
    f32 = jnp.float32
    log_g = jnp.log1p(-(2.0 ** (-5.0 - jnp.arange(H, dtype=f32))))
    idx = jnp.arange(C, dtype=f32)
    diff = idx[:, None] - idx[None, :]
    decay_in = jnp.where(diff >= 0, jnp.exp(log_g[:, None, None] * jnp.maximum(diff, 0.0)), 0.0)
    q_decay = jnp.exp(log_g[:, None] * (idx + 1.0))[None, :, :, None]
    k_decay = jnp.exp(log_g[:, None] * (C - 1.0 - idx))[None, :, :, None]
    chunk_decay = jnp.exp(log_g * C)[None, :, None, None]

    def chunks(t):
        return t.reshape(B, H, n, C, Dh).transpose(2, 0, 1, 3, 4).astype(f32)

    qc = chunks(_heads(q, H))
    kc = chunks(_heads(k, H) * Dh ** -0.5)
    vc = chunks(_heads(v, H))

    def step(R, inp):
        qi, ki, vi = inp
        att = jnp.einsum('bhid,bhjd->bhij', qi, ki) * decay_in
        o = jnp.einsum('bhij,bhjd->bhid', att, vi) + jnp.einsum('bhid,bhde->bhie', qi, R) * q_decay
        R = chunk_decay * R + jnp.einsum('bhjd,bhje->bhde', ki * k_decay, vi)
        return R, o

    _, o = lax.scan(step, jnp.zeros((B, H, Dh, Dh), f32), (qc, kc, vc))
    o = o.transpose(1, 2, 0, 3, 4).reshape(B, H, S, Dh)
    mu = jnp.mean(o, axis=-1, keepdims=True)
    var = jnp.mean(jnp.square(o - mu), axis=-1, keepdims=True)
    o = _merge_heads((o - mu) * lax.rsqrt(var + LN_EPS)) * gn_g + gn_b
    return (jax.nn.silu(gate.astype(f32)) * o).astype(q.dtype)

def gla_block(q, k, v, r, lr, w_alpha, b_alpha, norm_g):
    B, S, _ = q.shape
    H = GLA_HEADS
    C = GLA_CHUNK
    n = S // C
    f32 = jnp.float32
    log_a = jax.nn.log_sigmoid((lr @ w_alpha + b_alpha).astype(f32)) / GLA_TAU

    def chunks(t, d):
        return t.reshape(B, n, C, H, d).transpose(1, 0, 3, 2, 4).astype(f32)

    qc = chunks(q * GLA_DK ** -0.5, GLA_DK)
    kc = chunks(k, GLA_DK)
    vc = chunks(v, GLA_DV)
    ac = chunks(log_a, GLA_DK)
    causal = jnp.tril(jnp.ones((C, C), dtype=bool))[:, :, None]

    def step(St, inp):
        qi, ki, vi, ai = inp
        b = jnp.cumsum(ai, axis=2)
        inter = jnp.einsum('bhtk,bhkv->bhtv', qi * jnp.exp(b), St)
        diff = b[:, :, :, None, :] - b[:, :, None, :, :]
        decay = jnp.where(causal, jnp.exp(jnp.where(causal, diff, 0.0)), 0.0)
        att = jnp.einsum('bhtk,bhsk,bhtsk->bhts', qi, ki, decay)
        intra = jnp.einsum('bhts,bhsv->bhtv', att, vi)
        b_last = b[:, :, -1, :]
        St = jnp.exp(b_last)[..., None] * St + jnp.einsum('bhsk,bhsv->bhkv', ki * jnp.exp(b_last[:, :, None, :] - b), vi)
        return St, inter + intra

    _, o = lax.scan(step, jnp.zeros((B, H, GLA_DK, GLA_DV), f32), (qc, kc, vc, ac))
    o = o.transpose(1, 0, 3, 2, 4).reshape(B, S, H, GLA_DV)
    o = (o * lax.rsqrt(jnp.mean(jnp.square(o), axis=-1, keepdims=True) + LN_EPS)).reshape(B, S, H * GLA_DV) * norm_g
    return (jax.nn.silu(r.astype(f32)) * o).astype(q.dtype)

def peer_ffn(x, wq, sub_keys, u_tab, v_tab):
    B, S, D = x.shape
    nb = S // PEER_BLOCK
    half = PEER_QDIM // 2
    K = PEER_TOPK
    xb = x.reshape(B, nb, PEER_BLOCK, D).transpose(1, 0, 2, 3)

    def block(xi):
        qv = (xi @ wq).reshape(B, PEER_BLOCK, PEER_HEADS, 2, half)
        s = jnp.einsum('bthpc,hpnc->bthpn', qv, sub_keys).astype(jnp.float32)
        top_s, top_i = lax.top_k(s, K)
        cand_s = (top_s[..., 0, :, None] + top_s[..., 1, None, :]).reshape(B, PEER_BLOCK, PEER_HEADS, K * K)
        cand_i = (top_i[..., 0, :, None] * N_KEYS + top_i[..., 1, None, :]).reshape(B, PEER_BLOCK, PEER_HEADS, K * K)
        best_s, best_j = lax.top_k(cand_s, K)
        expert = jnp.take_along_axis(cand_i, best_j, axis=-1)
        gate = jax.nn.softmax(best_s, axis=-1)
        act = jax.nn.gelu(jnp.einsum('btd,bthkd->bthk', xi, u_tab[expert]).astype(jnp.float32), approximate=False)
        return jnp.einsum('bthk,bthkd->btd', (gate * act).astype(xi.dtype), v_tab[expert])

    return lax.map(block, xb).transpose(1, 0, 2, 3).reshape(B, S, D)

def hybrid_layer(x, w_in, cmp_pos, cmp_wk, cmp_wv, ret_gn_g, ret_gn_b, gla_w_alpha, gla_b_alpha,
                 gla_norm_g, w_branch, w_out, ln1_g, ln1_b, peer_wq, peer_keys, peer_u, peer_v, ln2_g, ln2_b):
    B, S, D = x.shape
    f32 = jnp.float32
    (sb_q, sb_k, sb_v, n_q, n_kc, n_vc, n_ks, n_vs, n_kw, n_vw, n_g,
     r_q, r_k, r_v, r_g, g_q, g_k, g_v, g_r, g_lr, m_g) = _split(x @ w_in, IN_WIDTHS)

    o_a = _merge_heads(stick_breaking_attention(_heads(sb_q, SB_HEADS), _heads(sb_k, SB_HEADS), _heads(sb_v, SB_HEADS)))
    o_b = _merge_heads(nsa_attention(_heads(n_q, NSA_HEADS), n_kc, n_vc, n_ks, n_vs, n_kw, n_vw, n_g,
                                     cmp_pos, cmp_wk, cmp_wv))
    o_c = retention_block(r_q, r_k, r_v, r_g, ret_gn_g, ret_gn_b)
    o_d = gla_block(g_q, g_k, g_v, g_r, g_lr, gla_w_alpha, gla_b_alpha, gla_norm_g)

    branches = jnp.stack([o_a, o_b, o_c, o_d], axis=2)
    proj = jnp.einsum('bsnc,ncd->bsnd', branches, w_branch)
    gates = jax.nn.sigmoid(m_g.astype(f32)).reshape(B, S, N_BRANCH, D).astype(x.dtype)
    mix = jnp.sum(gates * proj, axis=2) @ w_out
    x = _layer_norm(DN_ALPHA * x + mix, ln1_g, ln1_b)
    x = _layer_norm(DN_ALPHA * x + peer_ffn(x, peer_wq, peer_keys, peer_u, peer_v), ln2_g, ln2_b)
    return x

def second_inputs(seed: int = 0) -> dict:
    key = jax.random.key(seed)
    ks = jax.random.split(key, 24)
    f32 = jnp.float32
    L = DEPTH_2

    def nrm(k, shape, scale):
        return jax.random.normal(k, shape, f32) * scale

    return {
        'x': nrm(ks[0], (BATCH, SEQ, D_MODEL), 1.0),
        'ln_in_g': 1.0 + nrm(ks[1], (D_MODEL,), 0.02),
        'ln_in_b': nrm(ks[2], (D_MODEL,), 0.02),
        'w_in': nrm(ks[3], (L, D_MODEL, IN_TOTAL), D_MODEL ** -0.5),
        'nsa_cmp_pos': nrm(ks[4], (L, CMP_LEN, HEAD_DIM), 0.1),
        'nsa_cmp_wk': nrm(ks[5], (L, CMP_LEN * HEAD_DIM, HEAD_DIM), (CMP_LEN * HEAD_DIM) ** -0.5),
        'nsa_cmp_wv': nrm(ks[6], (L, CMP_LEN * HEAD_DIM, HEAD_DIM), (CMP_LEN * HEAD_DIM) ** -0.5),
        'ret_gn_g': 1.0 + nrm(ks[7], (L, MIX_W), 0.02),
        'ret_gn_b': nrm(ks[8], (L, MIX_W), 0.02),
        'gla_w_alpha': nrm(ks[9], (L, GLA_LOWRANK, GLA_HEADS * GLA_DK), GLA_LOWRANK ** -0.5),
        'gla_b_alpha': nrm(ks[10], (L, GLA_HEADS * GLA_DK), 0.1),
        'gla_norm_g': 1.0 + nrm(ks[11], (L, GLA_HEADS * GLA_DV), 0.02),
        'w_branch': nrm(ks[12], (L, N_BRANCH, MIX_W, D_MODEL), DN_BETA * MIX_W ** -0.5),
        'w_out': nrm(ks[13], (L, D_MODEL, D_MODEL), DN_BETA * D_MODEL ** -0.5),
        'ln1_g': 1.0 + nrm(ks[14], (L, D_MODEL), 0.02),
        'ln1_b': nrm(ks[15], (L, D_MODEL), 0.02),
        'peer_wq': nrm(ks[16], (L, D_MODEL, PEER_HEADS * PEER_QDIM), D_MODEL ** -0.5),
        'peer_keys': nrm(ks[17], (L, PEER_HEADS, 2, N_KEYS, PEER_QDIM // 2), (PEER_QDIM // 2) ** -0.5),
        'peer_u': nrm(ks[18], (L, N_EXPERTS_2, D_MODEL), D_MODEL ** -0.5),
        'peer_v': nrm(ks[19], (L, N_EXPERTS_2, D_MODEL), DN_BETA * PEER_HEADS ** -0.5),
        'ln2_g': 1.0 + nrm(ks[20], (L, D_MODEL), 0.02),
        'ln2_b': nrm(ks[21], (L, D_MODEL), 0.02),
    }

def second_block(x, ln_in_g, ln_in_b, w_in, nsa_cmp_pos, nsa_cmp_wk, nsa_cmp_wv, ret_gn_g, ret_gn_b,
              gla_w_alpha, gla_b_alpha, gla_norm_g, w_branch, w_out, ln1_g, ln1_b,
              peer_wq, peer_keys, peer_u, peer_v, ln2_g, ln2_b):
    h = _layer_norm(x, ln_in_g, ln_in_b)
    for l in range(DEPTH_2):
        h = hybrid_layer(h, w_in[l], nsa_cmp_pos[l], nsa_cmp_wk[l], nsa_cmp_wv[l], ret_gn_g[l], ret_gn_b[l],
                         gla_w_alpha[l], gla_b_alpha[l], gla_norm_g[l], w_branch[l], w_out[l],
                         ln1_g[l], ln1_b[l], peer_wq[l], peer_keys[l], peer_u[l], peer_v[l],
                         ln2_g[l], ln2_b[l])
    return h


def setup_inputs(seed=0):
    out = dict(first_inputs(seed))
    for name, value in second_inputs(seed + 1).items():
        if name != "x":
            out[name + "_2"] = value
    return out


def reference(
    x, c, ctx, c_ctx, mod_w, mod_b, norm1_g, norm2_g, w_in, rw_w0, rw_w_lora_b, rw_a0,
    rw_a_lora_b, rw_g_lora_b, rw_k_k, rw_k_a, rw_r_k, rw_ln_g, rw_ln_b, na_q_g, na_k_g, na_rpb,
    proj_a, proj_b, w_out, router_w, router_bias, moe_w1, moe_w3, moe_w2, ln_in_g_2, ln_in_b_2,
    w_in_2, nsa_cmp_pos_2, nsa_cmp_wk_2, nsa_cmp_wv_2, ret_gn_g_2, ret_gn_b_2, gla_w_alpha_2,
    gla_b_alpha_2, gla_norm_g_2, w_branch_2, w_out_2, ln1_g_2, ln1_b_2, peer_wq_2, peer_keys_2,
    peer_u_2, peer_v_2, ln2_g_2, ln2_b_2,
):
    x = first_block(
        x, c, ctx, c_ctx, mod_w, mod_b, norm1_g, norm2_g, w_in, rw_w0, rw_w_lora_b, rw_a0,
        rw_a_lora_b, rw_g_lora_b, rw_k_k, rw_k_a, rw_r_k, rw_ln_g, rw_ln_b, na_q_g, na_k_g,
        na_rpb, proj_a, proj_b, w_out, router_w, router_bias, moe_w1, moe_w3, moe_w2,
    )
    return second_block(
        x, ln_in_g_2, ln_in_b_2, w_in_2, nsa_cmp_pos_2, nsa_cmp_wk_2, nsa_cmp_wv_2, ret_gn_g_2,
        ret_gn_b_2, gla_w_alpha_2, gla_b_alpha_2, gla_norm_g_2, w_branch_2, w_out_2, ln1_g_2,
        ln1_b_2, peer_wq_2, peer_keys_2, peer_u_2, peer_v_2, ln2_g_2, ln2_b_2,
    )


_drawn_inputs = setup_inputs


def setup_inputs(seed=0):
    import zlib

    import numpy as np

    out = dict(_drawn_inputs(seed))
    spreads = {}
    factors = {'rw_w_lora_b': 4.612,
     'rw_k_a': 3.291,
     'rw_ln_g': 3.457,
     'rw_ln_b': 5.805,
     'na_q_g': 6.798,
     'na_k_g': 8.0,
     'na_rpb': 3.301,
     'nsa_cmp_pos_2': 5.32,
     'ret_gn_g_2': 26.851,
     'ret_gn_b_2': 25.591,
     'gla_w_alpha_2': 4.84,
     'gla_b_alpha_2': 8.0,
     'gla_norm_g_2': 24.931,
     'nsa_cmp_wk_2': 3.187}
    for name, (base, spread) in spreads.items():
        noise = np.random.default_rng([zlib.crc32(name.encode()), seed]).standard_normal(out[name].shape)
        drawn = base * np.exp(spread * noise) if base else spread * noise
        out[name] = jnp.asarray(drawn.astype(out[name].dtype))
    for name, factor in factors.items():
        out[name] = (out[name] * factor).astype(out[name].dtype)
    return out
```

```python
from contextlib import ExitStack

import numpy as np

import concourse.bass as bass
from concourse import mybir

F32 = mybir.dt.float32
F32R = mybir.dt.float32r
U32 = mybir.dt.uint32
I32 = mybir.dt.int32
ALU = mybir.AluOpType
ACT = mybir.ActivationFunctionType
AX = mybir.AxisListType.X

P = 128
D = 1024
KT = D // P
SEQ = 256
CTX = 256
ALL = CTX + SEQ
TT = SEQ // P
TILE = 2048
RING = 6
NH = 8
HD = 64
PAIRS = NH // 2
CH = 64
RMS_EPS = 1e-6
GN_EPS = 64e-5
LN_EPS = 1e-5
N_EXP = 16
D_EXP = 512
DECAY = float(np.exp(-0.5))
NEG = -1e30


class Stage:

    def __init__(self, nc, name):
        self.nc, self.name, self.sems, self.count = nc, name, {}, {}

    def __getitem__(self, what):
        if what not in self.sems:
            self.sems[what] = self.nc.alloc_semaphore(f"{self.name}_{what}")
            self.count[what] = 0
        return self.sems[what]

    def wait(self, eng, what, n):
        if n > 0:
            eng.wait_ge(self[what], n)

    def link(self, eng, ins, what):
        ins.then_inc(self[what], 1)
        self.count[what] += 1
        eng.wait_ge(self[what], self.count[what])

    def close(self):
        self.nc.clear_and_free_semaphores(list(self.sems.values()))
        self.nc.all_engine_barrier()


class Core:

    def __init__(self, nc, ctx):
        self.nc, self.ctx = nc, ctx
        self.bank = [ctx.enter_context(nc.psum_tensor(f"bank{i}", [P, 512], F32)) for i in range(8)]
        self.ring = ctx.enter_context(nc.sbuf_tensor("ring", [P, RING, TILE], F32))

    def keep(self, name, shape, dt=F32):
        return self.ctx.enter_context(self.nc.sbuf_tensor(name, shape, dt))


def constants_square():
    i, j = np.arange(P)[:, None], np.arange(P)[None, :]
    same = (i // CH) == (j // CH)
    out = {}
    out["ident"] = (i == j)
    out["ones"] = np.ones((P, P))
    out["head_ones"] = same
    out["fwd_in"] = -DECAY * (same & (i <= j))
    out["fwd_ex"] = -DECAY * (same & (i < j))
    out["bwd_in"] = -DECAY * (same & (i >= j))
    out["bwd_ex"] = -DECAY * (same & (i > j))
    out["m_fwd_ex"] = same & (i < j)
    out["m_fwd_in"] = same & (i <= j)
    out["m_bwd_ex"] = same & (i > j)
    out["m_bwd_in"] = same & (i >= j)
    out["lt"] = i < j
    out["neg_ge"] = -1.0 * (i >= j)
    out["neg_ones"] = -np.ones((P, P))
    mid = same & ((i % CH) <= CH // 2 - 1)
    tau = 16.0
    out["gla_in"] = (same & (i <= j)) / tau
    out["gla_mid"] = ((same & (i <= j)) * 1.0 - mid) / tau
    out["gla_tail"] = (same & (i > j)) / tau
    return {k: v.astype(np.float32) for k, v in out.items()}


SQUARE = list(constants_square())
EPS = [RMS_EPS, GN_EPS, LN_EPS, 1.0]


def square_array():
    c = constants_square()
    return np.ascontiguousarray(np.stack([c[k] for k in SQUARE], 1))


def eps_array():
    return np.ascontiguousarray(np.tile(np.array(EPS, np.float32)[None], (P, 1)))


def load_all(nc, name, pairs):
    S = Stage(nc, name)
    with nc.Block() as block:
        @block.sync
        def _(sp):
            for dst, src in pairs:
                sp.dma_start(dst, src).then_inc(S["loaded"], 16)
            sp.wait_ge(S["loaded"], 16 * len(pairs))
    S.close()


def product(pe, out, terms):
    for n, (lhsT, rhs) in enumerate(terms):
        ins = pe.matmul(out, lhsT, rhs, start=(n == 0), stop=(n == len(terms) - 1))
    return ins


def split_product(pe, out, a, b, first, last):
    pe.matmul(out, a[0], b[0], start=first, stop=False)
    pe.matmul(out, a[0], b[1], start=False, stop=False)
    return pe.matmul(out, a[1], b[0], start=False, stop=last)


def split(C, name, pairs):
    S = Stage(C.nc, name)
    with C.nc.Block() as block:
        @block.scalar
        def _(act):
            for src, high, low in pairs:
                act.activation(high, src, ACT.Copy).then_inc(S["high"], 1)

        @block.vector
        def _(dve):
            for n, (src, high, low) in enumerate(pairs):
                dve.wait_ge(S["high"], n + 1)
                dve.tensor_tensor(low, src, high.bitcast(F32), ALU.subtract).then_inc(S["low"], 1)
    S.close()


def linear(C, name, tiles, jobs, kt=KT, extra=None):
    nc = C.nc
    S = Stage(nc, name)
    by = []
    for j, job in enumerate(jobs):
        by.append("v" if job[9] is not None or (job[8] is None and j % 2) else "a")
    upto = {e: [sum(b == e for b in by[:j + 1]) for j in range(len(jobs))] for e in "av"}
    last = {job[0]: j + 1 for j, job in enumerate(jobs)}
    of_tile = [[j for j, job in enumerate(jobs) if job[0] == n] for n in range(len(tiles))]
    halves = [any(isinstance(jobs[j][4], tuple) for j in of_tile[n]) for n in range(len(tiles))]
    plain = [any(not isinstance(jobs[j][4], tuple) for j in of_tile[n]) for n in range(len(tiles))]
    nth = [sum(halves[:n]) for n in range(len(tiles))]
    split_at = [n for n in range(len(tiles)) if halves[n]]
    out_of = {"a": "taken_by_act", "v": "taken_by_dve"}
    NB = 8

    def where(j):
        _, _, cols, turned, _, _, n, _, _, _ = jobs[j]
        return C.bank[j % NB][0:cols if turned else n, 0:n if turned else cols]

    with ExitStack() as local:
        w2 = local.enter_context(nc.sbuf_tensor(name + "_halves", [P, 2, 2, TILE], F32R)) if any(halves) else None
        with nc.Block() as block:
            @block.sync
            def _(sp):
                for n, src in enumerate(tiles):
                    old = n - RING
                    if old >= 0:
                        if halves[old]:
                            S.wait(sp, "low", nth[old] + 1)
                        if plain[old]:
                            S.wait(sp, "product", last[old])
                    sp.dma_start(C.ring[:, n % RING, :], src).then_inc(S[f"loaded{n % RING}"], 16)

            @block.tensor
            def _(pe):
                at = -1
                for j, (tile, c0, cols, turned, acts, t0, n, _, _, _) in enumerate(jobs):
                    if tile != at:
                        at = tile
                        pe.wait_ge(S[f"loaded{tile % RING}"], 16 * (tile // RING + 1))
                        if halves[tile]:
                            pe.wait_ge(S["low"], nth[tile] + 1)
                    if j >= NB:
                        S.wait(pe, out_of[by[j - NB]], upto[by[j - NB]][j - NB])
                    for k in range(kt):
                        if isinstance(acts, tuple):
                            w = [w2[:, nth[tile] % 2, i, :].rearrange("p (k c) -> p k c", k=kt)[:, k, c0:c0 + cols]
                                 for i in range(2)]
                            x = [acts[i][:, k, t0:t0 + n] for i in range(2)]
                            a, b = (w, x) if turned else (x, w)
                            ins = split_product(pe, where(j), a, b, k == 0, k == kt - 1)
                        else:
                            w = C.ring[:, tile % RING, :].rearrange("p (k c) -> p k c", k=kt)[:, k, c0:c0 + cols]
                            x = acts[:, k, t0:t0 + n]
                            a, b = (w, x) if turned else (x, w)
                            ins = pe.matmul(where(j), a, b, start=(k == 0), stop=(k == kt - 1))
                    ins.then_inc(S["product"], 1)

            @block.scalar
            def _(act):
                def high(i):
                    n = split_at[i]
                    act.wait_ge(S[f"loaded{n % RING}"], 16 * (n // RING + 1))
                    if i >= 2:
                        act.wait_ge(S["product"], last[split_at[i - 2]])
                    act.activation(w2[:, i % 2, 0, :], C.ring[:, n % RING, :], ACT.Copy).then_inc(S["high"], 1)

                if split_at:
                    high(0)
                for n in range(len(tiles)):
                    if halves[n] and nth[n] + 1 < len(split_at):
                        high(nth[n] + 1)
                    for j in of_tile[n]:
                        if by[j] == "a":
                            act.wait_ge(S["product"], j + 1)
                            act.activation(jobs[j][7], where(j), jobs[j][8] or ACT.Copy).then_inc(S["taken_by_act"], 1)

            @block.vector
            def _(dve):
                def low(i):
                    n = split_at[i]
                    dve.wait_ge(S["high"], i + 1)
                    dve.tensor_tensor(w2[:, i % 2, 1, :], C.ring[:, n % RING, :], w2[:, i % 2, 0, :].bitcast(F32),
                                      ALU.subtract).then_inc(S["low"], 1)

                if split_at:
                    low(0)
                for n in range(len(tiles)):
                    if halves[n] and nth[n] + 1 < len(split_at):
                        low(nth[n] + 1)
                    for j in of_tile[n]:
                        if by[j] == "v":
                            dve.wait_ge(S["product"], j + 1)
                            if jobs[j][9] is None:
                                ins = dve.tensor_copy(jobs[j][7], where(j))
                            else:
                                ins = dve.tensor_tensor(jobs[j][7], where(j), jobs[j][9], ALU.mult)
                            ins.then_inc(S["taken_by_dve"], 1)
                if extra is not None:
                    S.wait(dve, "taken_by_act", upto["a"][-1])
                    S.wait(dve, "taken_by_dve", upto["v"][-1])
                    extra(S, dve)
    S.close()


def norm(C, name, rows, eps, centred=False):
    nc = C.nc
    S = Stage(nc, name)
    n = rows[0][4]
    with ExitStack() as local:
        work = local.enter_context(nc.sbuf_tensor(name + "_work", [P, KT, n], F32))
        cent = local.enter_context(nc.sbuf_tensor(name + "_cent", [P, KT, n], F32)) if centred else None
        mean = local.enter_context(nc.sbuf_tensor(name + "_mean", [P, n], F32))
        rstd = local.enter_context(nc.sbuf_tensor(name + "_rstd", [P, n], F32))
        with nc.Block() as block:
            @block.tensor
            def _(pe):
                for i, (src, dst, gain, shift, n) in enumerate(rows):
                    if centred:
                        S.wait(pe, "mean", i)
                        product(pe, C.bank[0][:, 0:n], [(C.sq["ones"], src[:, k, :]) for k in range(KT)])\
                            .then_inc(S["sum"], 1)
                    pe.wait_ge(S["squares"], i + 1)
                    S.wait(pe, "root", i)
                    product(pe, C.bank[1][:, 0:n], [(C.sq["ones"], work[:, k, :]) for k in range(KT)])\
                        .then_inc(S["square_sum"], 1)

            @block.scalar
            def _(act):
                for i, (src, dst, gain, shift, n) in enumerate(rows):
                    if centred:
                        act.wait_ge(S["sum"], i + 1)
                        act.activation(mean[:, :], C.bank[0][:, 0:n], ACT.Copy, scale=1.0 / D)\
                           .then_inc(S["mean"], 1)
                        act.wait_ge(S["centred"], i + 1)
                        src = cent[:, :, :]
                    S.wait(act, "square_sum", i)
                    act.activation(work[:, :, :], src, ACT.Square).then_inc(S["squares"], 1)
                    act.wait_ge(S["square_sum"], i + 1)
                    S.wait(act, "out", i * KT * 2)
                    act.activation(rstd[:, :], C.bank[1][:, 0:n], ACT.Sqrt, scale=1.0 / D,
                                   bias=C.eps[eps]).then_inc(S["root"], 1)

            @block.vector
            def _(dve):
                for i, (src, dst, gain, shift, n) in enumerate(rows):
                    if centred:
                        dve.wait_ge(S["mean"], i + 1)
                        S.link(dve, dve.tensor_tensor(cent[:, :, :], src, mean[:, :].unsqueeze(1).broadcast_to([P, KT, n]),
                                                      ALU.subtract), "centred")
                        src = cent
                    dve.wait_ge(S["root"], i + 1)
                    S.link(dve, dve.reciprocal(rstd[:, :], rstd[:, :]), "inverse")
                    for k in range(KT):
                        dve.scalar_tensor_tensor(out=dst[:, k, :], in0=src[:, k, :], scalar=gain[:, k:k + 1],
                                                 in1=rstd[:, :], op0=ALU.mult, op1=ALU.mult)\
                           .then_inc(S["out"], 1)
                    dve.wait_ge(S["out"], i * KT * 2 + KT)
                    for k in range(KT):
                        sh = 0.0 if shift is None else shift[:, k:k + 1]
                        dve.tensor_scalar(dst[:, k, :], dst[:, k, :], sh, None, ALU.add)\
                           .then_inc(S["out"], 1)
        S.close()


def modulation(C, A, mod):
    nc = C.nc
    S = Stage(nc, "modulation")
    tiles = 6 * D // 256
    with ExitStack() as local:
        c = local.enter_context(nc.sbuf_tensor("cond", [P, KT, 2], F32))
        bias = local.enter_context(nc.sbuf_tensor("mod_bias", [P, 6 * KT], F32))
        row = local.enter_context(nc.sbuf_tensor("mod_rows", [2, 6 * D], F32))
        with nc.Block() as block:
            @block.sync
            def _(sp):
                sp.dma_start(c[:, :, :], A["cond"]).then_inc(S["small"], 16)
                sp.dma_start(bias[:, :], A["mod_b"]).then_inc(S["small"], 16)
                for n in range(tiles):
                    S.wait(sp, "product", n - RING + 1)
                    sp.dma_start(C.ring[:, n % RING, :], A["mod_w"][n]).then_inc(S[f"loaded{n % RING}"], 16)

            @block.scalar
            def _(act):
                act.wait_ge(S["small"], 32)
                act.activation(c[:, :, :], c[:, :, :], ACT.Silu).then_inc(S["silu"], 1)
                for n in range(tiles):
                    act.wait_ge(S["product"], n + 1)
                    act.activation(row[:, n * 256:(n + 1) * 256], C.bank[n % 4][0:2, 0:256], ACT.Copy)\
                       .then_inc(S["row"], 1)

            @block.tensor
            def _(pe):
                pe.wait_ge(S["silu"], 1)
                for n in range(tiles):
                    pe.wait_ge(S[f"loaded{n % RING}"], 16 * (n // RING + 1))
                    S.wait(pe, "row", n - 3)
                    w = C.ring[:, n % RING, :].rearrange("p (k c) -> p k c", k=KT)
                    product(pe, C.bank[n % 4][0:2, 0:256], [(c[:, k, :], w[:, k, :]) for k in range(KT)])\
                        .then_inc(S["product"], 1)
                for m in range(6 * KT):
                    pe.wait_ge(S["row"], m // 2 + 1)
                    ins = pe.transpose(C.bank[4][:, 2 * m:2 * m + 2], row[:, m * P:(m + 1) * P],
                                       C.sq["ident"][0:2, 0:2])
                ins.then_inc(S["turned"], 1)

            @block.vector
            def _(dve):
                dve.wait_ge(S["small"], 32)
                dve.wait_ge(S["turned"], 1)
                S.link(dve, dve.tensor_tensor(mod[:, :, :], C.bank[4][:, 0:12 * KT].rearrange("p (m c) -> p m c", c=2),
                                              bias[:, :].unsqueeze(2).broadcast_to([P, 6 * KT, 2]), ALU.add), "mod")
        S.close()


def gains(C, name, rows):
    nc = C.nc
    S = Stage(nc, name)
    with nc.Block() as block:
        @block.vector
        def _(dve):
            for out, gain, scale in rows:
                S.link(dve, dve.scalar_tensor_tensor(out=out, in0=scale, scalar=1.0, in1=gain,
                                                     op0=ALU.add, op1=ALU.mult), "gain")
    S.close()


def rwkv_prep(C, Z, W):
    nc = C.nc
    S = Stage(nc, "rwkv_prep")
    kT, kk = Z["k"], W["kk"]
    with ExitStack() as local:
        sq = local.enter_context(nc.sbuf_tensor("kk_sq", [P, PAIRS, ALL], F32))
        nrm = local.enter_context(nc.sbuf_tensor("kk_norm", [P, PAIRS, ALL], F32))
        with nc.Block() as block:
            @block.tensor
            def _(pe):
                pe.wait_ge(S["squares"], 1)
                for p in range(PAIRS):
                    product(pe, C.bank[p][:, :], [(C.sq["head_ones"], sq[:, p, :])]).then_inc(S["norm"], 1)

            @block.scalar
            def _(act):
                act.wait_ge(S["scaled"], PAIRS)
                act.activation(sq[:, :, :], kk[:, :, :], ACT.Square).then_inc(S["squares"], 1)
                for p in range(PAIRS):
                    act.wait_ge(S["clamped"], p + 1)
                    act.activation(nrm[:, p, :], nrm[:, p, :], ACT.Sqrt).then_inc(S["root"], 1)

            @block.vector
            def _(dve):
                for p in range(PAIRS):
                    dve.tensor_scalar(kk[:, p, :], kT[:, p, :], C.v["k_k"][:, p:p + 1], None, ALU.mult)\
                       .then_inc(S["scaled"], 1)
                for p in range(PAIRS):
                    dve.wait_ge(S["norm"], p + 1)
                    dve.tensor_scalar(nrm[:, p, :], C.bank[p][:, :], 1e-12, None, ALU.max)\
                       .then_inc(S["clamped"], 1)
                dve.wait_ge(S["scaled"], PAIRS)
                for p in range(PAIRS):
                    dve.wait_ge(S["root"], p + 1)
                    S.link(dve, dve.reciprocal(nrm[:, p, :], nrm[:, p, :]), "inverse")
                S.link(dve, dve.tensor_tensor(kk[:, :, :], kk[:, :, :], nrm[:, :, :], ALU.mult), "kk")
        S.close()


SIDES = ("fwd", "bwd")


def rwkv_tile(C, Z, W, step, B):
    nc = C.nc
    latent = step >= 2
    tile = [step, (1, 0, 3, 2)[step]]
    NCOL = 512 if latent else 256
    S = Stage(nc, f"delta{step}")

    def tok(d):
        return slice(P * tile[d], P * tile[d] + P)

    def lat(d):
        return slice(P * tile[d] - CTX, P * tile[d] - CTX + P)

    def rows(h):
        return slice(HD * (h % 2), HD * (h % 2) + HD)

    qr, bb, kn, btok, ktok = B["qr"], B["bb"], B["kn"], B["btok"], B["ktok"]
    ein, eex, eneg, tmp = B["ein"], B["eex"], B["eneg"], B["tmp"]
    X, PT, M = B["X"], B["PT"], B["M"]
    with nc.Block() as block:
        @block.tensor
        def _(pe):
            for d in range(2):
                r = slice(64 * d, 64 * d + 64)
                product(pe, C.bank[2 + d][:, :], [(Z["lw"][r, tok(d)], W["wb"][r, :]),
                                                  (C.sq["ones"][r, :], W["w0"][r, :])]).then_inc(S["wl"], 1)
                for p in range(PAIRS):
                    ins = product(pe, C.bank[6 + d][:, p * P:(p + 1) * P],
                                  [(W["ab"][r, p * P:(p + 1) * P], Z["la"][r, tok(d)])])
                ins.then_inc(S["al"], 1)
            for d, side in enumerate(SIDES):
                pe.wait_ge(S["sig"], d + 1)
                if d:
                    pe.wait_ge(S["decays"], 3 * d)
                for p in range(PAIRS):
                    out = C.bank[p // 2][:, (p % 2) * 256:(p % 2) * 256 + 256]
                    lhsT = W["sig"][:, d, p * P:(p + 1) * P]
                    pe.matmul(out[:, 0:P], lhsT, C.sq[side + "_in"], start=True, stop=True)
                    ins = pe.matmul(out[:, P:2 * P], lhsT, C.sq[side + "_ex"], start=True, stop=True)
                ins.then_inc(S["logs"], 1)
            for d in range(2):
                pe.wait_ge(S["operands"], d + 1)
                if d:
                    pe.wait_ge(S["tok"], 2 * d)
                for p in range(PAIRS):
                    pe.transpose(C.bank[4][:, p * P:(p + 1) * P], bb[:, d, p, :], C.sq["ident"])
                    ins = pe.transpose(C.bank[5][:, p * P:(p + 1) * P], kn[:, d, p, :], C.sq["ident"])
                ins.then_inc(S["turned"], 1)

        @block.scalar
        def _(act):
            for d in range(2):
                act.wait_ge(S["wl"], d + 1)
                act.activation(W["sig"][:, d, :], C.bank[2 + d][:, :], ACT.Sigmoid).then_inc(S["sig"], 1)
                act.wait_ge(S["al"], d + 1)
                for p in range(PAIRS):
                    ins = act.activation(W["a"][:, d, p, :], C.bank[6 + d][:, p * P:(p + 1) * P], ACT.Sigmoid,
                                         bias=C.v["a0"][:, 4 * d + p:4 * d + p + 1])
                ins.then_inc(S["a"], 1)
            for d in range(2):
                act.wait_ge(S["logs"], d + 1)
                for i, (dst, scale, half) in enumerate(((ein, 1.0, 0), (eneg, -1.0, 0), (eex, 1.0, 1))):
                    for q in range(2):
                        src = C.bank[q][:, :].rearrange("p (a c) -> p a c", a=2)[:, :, half * P:half * P + P]
                        ins = act.activation(dst[:, d, 2 * q:2 * q + 2, :], src, ACT.Exp, scale=scale)
                    ins.then_inc(S["decays"], 1)
            for d in range(2):
                act.wait_ge(S["turned"], d + 1)
                for dst, bank in ((btok, 4), (ktok, 5)):
                    act.activation(dst[:, d, :], C.bank[bank][:, :], ACT.Copy).then_inc(S["tok"], 1)

        @block.vector
        def _(dve):
            for d in range(2):
                a = W["a"][:, d, :, :]
                dve.wait_ge(S["a"], d + 1)
                kk = W["kk"][:, :, tok(d)]
                for p in range(PAIRS):
                    dve.tensor_scalar(tmp[:, d, p, :], a[:, p, :], C.v["k_a"][:, p:p + 1],
                                      C.v["one_minus_k_a"][:, p:p + 1], ALU.mult, ALU.add).then_inc(S["rate"], 1)
                dve.wait_ge(S["rate"], PAIRS * (d + 1))
                S.link(dve, dve.tensor_tensor(kn[:, d, :, :], tmp[:, d, :, :], Z["k"][:, :, tok(d)], ALU.mult), "kdir")
                S.link(dve, dve.tensor_tensor(bb[:, d, :, :], a, kk, ALU.mult), "kka")
                dve.wait_ge(S["decays"], 3 * d + 3)
                dve.tensor_tensor(qr[:, d, :, 0:P], kk, eex[:, d, :, :], ALU.mult).then_inc(S["q"], 1)
                if latent:
                    dve.tensor_tensor(qr[:, d, :, P:2 * P], Z["r"][:, :, lat(d)], ein[:, d, :, :], ALU.mult)\
                       .then_inc(S["r"], 1)
                dve.tensor_tensor(kn[:, d, :, :], kn[:, d, :, :], eneg[:, d, :, :], ALU.mult).then_inc(S["k"], 1)
                dve.wait_ge(S["k"], d + 1)
                dve.wait_ge(S["q"], d + 1)
                S.link(dve, dve.tensor_tensor(bb[:, d, :, :], bb[:, d, :, :], eneg[:, d, :, :], ALU.mult), "operands")
    S.close()

    S = Stage(nc, f"inverse{step}")
    UN = 2 * NH
    SQ = 5
    with nc.Block() as block:
        @block.tensor
        def _(pe):
            for u in range(UN):
                d, h = u // NH, u % NH
                r, p = rows(h), h // 2
                if u >= 3:
                    pe.wait_ge(S["masked"], u - 2)
                b1, b2 = C.bank[2 * (u % 3)], C.bank[2 * (u % 3) + 1]
                w = 2 * P if latent else P
                pe.matmul(b1[:, 0:w], bb[r, d, p, :], qr[r, d, p, 0:w], start=True, stop=True)
                pe.matmul(b1[:, 256:256 + w], kn[r, d, p, :], qr[r, d, p, 0:w], start=True, stop=True)
                pe.matmul(b2[:, 0:P], qr[r, d, p, 0:P], bb[r, d, p, :], start=True, stop=True)\
                  .then_inc(S["pairs"], 1)
            pe.wait_ge(S["masked"], UN)
            for s in range(SQ + 1):
                for u in range(UN):
                    n = s * UN + u
                    if s == 0:
                        pe.wait_ge(S["first"], u + 1)
                    else:
                        pe.wait_ge(S["power"], n - UN + 1)
                    m, mt = M[:, u, 0:P], M[:, u, P:2 * P]
                    if s >= 1:
                        q = n - UN
                        S.wait(pe, "summed", max(q - 3, q - UN + 1))
                        pe.matmul(C.bank[4 + q % 4][:, 0:P], m, PT[:, u, :], start=True, stop=True)\
                          .then_inc(S["corrected"], 1)
                    if s < SQ:
                        S.wait(pe, "power", n - 3)
                        pe.matmul(C.bank[n % 4][:, 0:P], mt, m, start=True, stop=True)
                        pe.matmul(C.bank[n % 4][:, P:2 * P], m, mt, start=True, stop=True)\
                          .then_inc(S["squared"], 1)

        @block.scalar
        def _(act):
            for s in range(SQ):
                for u in range(UN):
                    n = s * UN + u
                    act.wait_ge(S["squared"], n + 1)
                    act.activation(M[:, u, :], C.bank[n % 4][:, 0:2 * P], ACT.Copy).then_inc(S["power"], 1)

        @block.vector
        def _(dve):
            for u in range(UN):
                d = u // NH
                dve.wait_ge(S["pairs"], u + 1)
                mask = C.mask4[:, d, :] if latent else C.mask4[:, d, :].rearrange("p (a c) -> p a c", a=2)[:, :, 0:P]
                b1, b2 = C.bank[2 * (u % 3)], C.bank[2 * (u % 3) + 1]
                x = X[:, u, :].rearrange("p (a c) -> p a c", a=2)
                if latent:
                    dve.tensor_tensor(X[:, u, :], b1[:, :], mask, ALU.mult).then_inc(S["x"], 1)
                else:
                    dve.tensor_tensor(x[:, :, 0:P], b1[:, :].rearrange("p (a c) -> p a c", a=2)[:, :, 0:P], mask,
                                      ALU.mult).then_inc(S["x"], 1)
                dve.tensor_tensor(M[:, u, 0:P], b2[:, 0:P], C.sq["m_" + SIDES[1 - d] + "_ex"], ALU.mult)\
                   .then_inc(S["masked"], 1)
            for u in range(UN):
                dve.wait_ge(S["x"], u + 1)
                dve.tensor_tensor(PT[:, u, :], C.sq["ident"], X[:, u, 0:P], ALU.subtract).then_inc(S["start"], 1)
                dve.tensor_copy(M[:, u, P:2 * P], X[:, u, 0:P]).then_inc(S["first"], 1)
            for q in range(SQ * UN):
                u = q % UN
                dve.wait_ge(S["corrected"], q + 1)
                if q < UN:
                    dve.wait_ge(S["start"], u + 1)
                else:
                    dve.wait_ge(S["summed"], q - UN + 1)
                dve.tensor_tensor(PT[:, u, :], PT[:, u, :], C.bank[4 + q % 4][:, 0:P], ALU.add)\
                   .then_inc(S["summed"], 1)
    S.close()

    S = Stage(nc, f"chain{step}")
    R, nU, S0, SW, yT, V = B["R"], B["nU"], W["S0"], B["SW"], W["y"], Z["v"]
    units = [(c, d) for c in range(2) for d in range(2)]

    def chunk(c, d):
        a = CH * (c if d == 0 else 1 - c)
        return slice(a, a + CH)

    def cols(h):
        return slice(HD * h, HD * h + HD)

    with nc.Block() as block:
        @block.tensor
        def _(pe):
            for n, (c, d) in enumerate(units):
                t, B0 = chunk(c, d), 4 * d
                if c:
                    pe.wait_ge(S["state"], n - 1)
                for p in range(PAIRS):
                    pe.matmul(C.bank[B0][t, p * P:(p + 1) * P], qr[:, d, p, t], S0[:, d, p, :],
                              start=True, stop=False, skip_group_check=True)
                    for h in (2 * p, 2 * p + 1):
                        ins = pe.matmul(C.bank[B0][t, cols(h)], X[:, d * NH + h, 256 + t.start:256 + t.stop],
                                        V[:, tile[d], cols(h)], start=False, stop=True, skip_group_check=True)
                ins.then_inc(S["right_side"], 1)
                pe.wait_ge(S["right"], n + 1)
                for h in range(NH):
                    ins = pe.matmul(C.bank[B0 + 1][t, cols(h)], PT[:, d * NH + h, t], R[:, d, cols(h)],
                                    start=True, stop=True)
                ins.then_inc(S["solved"], 1)
                pe.wait_ge(S["u"], n + 1)
                for p in range(PAIRS):
                    c2 = slice(p * P, (p + 1) * P)
                    pe.matmul(C.bank[B0 + 2][:, c2], btok[t, d, c2], nU[t, d, c2], start=True, stop=False)
                    ins = pe.matmul(C.bank[B0 + 2][:, c2], ktok[t, d, c2], V[t, tile[d], c2], start=False, stop=True)
                ins.then_inc(S["update"], 1)
                if latent:
                    if c:
                        pe.wait_ge(S["y"], n - 1)
                    for p in range(PAIRS):
                        out = C.bank[B0 + 3][:, p * CH:(p + 1) * CH]
                        pe.matmul(out, S0[:, d, p, :], qr[:, d, p, P + t.start:P + t.stop], start=True, stop=False,
                                  skip_group_check=True)
                        for h in (2 * p, 2 * p + 1):
                            r, u = rows(h), d * NH + h
                            out = C.bank[B0 + 3][r, p * CH:(p + 1) * CH]
                            pe.matmul(out, nU[:, d, cols(h)], X[:, u, P + t.start:P + t.stop], start=False, stop=False,
                                      skip_group_check=True)
                            ins = pe.matmul(out, V[:, tile[d], cols(h)], X[:, u, 384 + t.start:384 + t.stop],
                                            start=False, stop=True, skip_group_check=True)
                    ins.then_inc(S["y_product"], 1)

        @block.scalar
        def _(act):
            for n, (c, d) in enumerate(units):
                t, B0 = chunk(c, d), 4 * d
                act.wait_ge(S["right_side"], n + 1)
                act.activation(R[t, d, :], C.bank[B0][t, :], ACT.Copy).then_inc(S["right"], 1)
                act.wait_ge(S["solved"], n + 1)
                act.activation(nU[t, d, :], C.bank[B0 + 1][t, :], ACT.Copy, scale=-1.0).then_inc(S["u"], 1)

        @block.vector
        def _(dve):
            for n, (c, d) in enumerate(units):
                t, B0 = chunk(c, d), 4 * d
                last = t.stop - 1 if d == 0 else t.start
                for p in range(PAIRS):
                    dve.tensor_scalar(SW[:, p, :], C.sq["head_ones"], ein[:, d, p, last:last + 1], None, ALU.mult)\
                       .then_inc(S["whole"], 1)
                dve.wait_ge(S["whole"], PAIRS * (n + 1))
                dve.wait_ge(S["update"], n + 1)
                if latent:
                    dve.wait_ge(S["y_product"], n + 1)
                S.link(dve, dve.tensor_tensor(S0[:, d, :, :], S0[:, d, :, :], C.bank[B0 + 2][:, :].rearrange(
                    "p (a c) -> p a c", a=PAIRS), ALU.add), "sum")
                S.link(dve, dve.tensor_tensor(S0[:, d, :, :], S0[:, d, :, :], SW[:, :, :], ALU.mult), "state")
                if latent:
                    at = P * tile[d] - CTX + t.start
                    out = yT[:, d, :, at:at + CH]
                    dve.tensor_copy(out, C.bank[B0 + 3][:, 0:256].rearrange("p (a c) -> p a c", a=PAIRS))\
                       .then_inc(S["y"], 1)
    S.close()


def head_norm(C, name, src, dst, eps, gain, shift, centred, nt=PAIRS, cols=SEQ):
    nc = C.nc
    S = Stage(nc, name)
    half = nt * cols // 512
    with ExitStack() as local:
        work = local.enter_context(nc.sbuf_tensor(name + "_w", [P, nt * cols], F32))
        root = local.enter_context(nc.sbuf_tensor(name + "_r", [P, nt * cols], F32))
        s2 = src[:, :, :].rearrange("p a c -> p (a c)")
        d2 = dst[:, :, :].rearrange("p a c -> p (a c)")
        with nc.Block() as block:
            @block.tensor
            def _(pe):
                if centred:
                    for i in range(half):
                        ins = product(pe, C.bank[i][:, :], [(C.sq["head_ones"], s2[:, i * 512:(i + 1) * 512])])
                    ins.then_inc(S["sum"], 1)
                pe.wait_ge(S["squares"], 1)
                for i in range(half):
                    ins = product(pe, C.bank[4 + i][:, :], [(C.sq["head_ones"], work[:, i * 512:(i + 1) * 512])])
                ins.then_inc(S["square_sum"], 1)

            @block.scalar
            def _(act):
                if centred:
                    act.wait_ge(S["centred"], half)
                act.activation(work[:, :], d2 if centred else s2, ACT.Square).then_inc(S["squares"], 1)
                act.wait_ge(S["square_sum"], 1)
                for i in range(half):
                    act.activation(root[:, i * 512:(i + 1) * 512], C.bank[4 + i][:, :], ACT.Sqrt, scale=1.0 / HD,
                                   bias=C.eps[eps]).then_inc(S["root"], 1)

            @block.vector
            def _(dve):
                if centred:
                    dve.wait_ge(S["sum"], 1)
                    for i in range(half):
                        c = slice(i * 512, (i + 1) * 512)
                        dve.scalar_tensor_tensor(out=d2[:, c], in0=C.bank[i][:, :], scalar=-1.0 / HD, in1=s2[:, c],
                                                 op0=ALU.mult, op1=ALU.add).then_inc(S["centred"], 1)
                dve.wait_ge(S["root"], half)
                S.link(dve, dve.reciprocal(root[:, :], root[:, :]), "inverse")
                S.link(dve, dve.tensor_tensor(d2, d2 if centred else s2, root[:, :], ALU.mult), "scaled")
                for p in range(nt):
                    dve.tensor_scalar(dst[:, p, :], dst[:, p, :], gain[:, p:p + 1],
                                      0.0 if shift is None else shift[:, p:p + 1], ALU.mult, ALU.add)\
                       .then_inc(S["out"], 1)
        S.close()


def rwkv_bonus(C, A, Z, W, ya):
    nc = C.nc
    S = Stage(nc, "bonus")
    with ExitStack() as local:
        rk = local.enter_context(nc.sbuf_tensor("rk", [P, PAIRS, SEQ], F32))
        vT = local.enter_context(nc.sbuf_tensor("vT", [P, PAIRS, SEQ], F32))
        gb = local.enter_context(nc.sbuf_tensor("g_lora", [P, NH * HD], F32))
        flat = rk[:, :, :].rearrange("p a c -> p (a c)")
        with nc.Block() as block:
            @block.sync
            def _(sp):
                sp.dma_start(gb[:, :], A["rw_g_lora_b"]).then_inc(S["lora"], 16)

            @block.tensor
            def _(pe):
                for p in range(PAIRS):
                    for t in range(TT):
                        ins = pe.transpose(C.bank[p // 2][:, (p % 2) * SEQ + t * P:(p % 2) * SEQ + (t + 1) * P],
                                           Z["v"][:, TT + t, p * P:(p + 1) * P], C.sq["ident"])
                ins.then_inc(S["v_turned"], 1)
                pe.wait_ge(S["lora"], 16)
                for p in range(PAIRS):
                    ins = product(pe, C.bank[2 + p // 2][:, (p % 2) * SEQ:(p % 2) * SEQ + SEQ],
                                  [(gb[:, p * P:(p + 1) * P], Z["lg"][:, :])])
                ins.then_inc(S["gate"], 1)
                pe.wait_ge(S["rk"], PAIRS)
                for i in range(2):
                    ins = product(pe, C.bank[4 + i][:, :], [(C.sq["head_ones"], flat[:, i * 512:(i + 1) * 512])])
                ins.then_inc(S["rk_sum"], 1)

            @block.scalar
            def _(act):
                act.wait_ge(S["v_turned"], 1)
                for i in range(2):
                    act.activation(vT[:, 2 * i:2 * i + 2, :], C.bank[i][:, :].rearrange("p (a c) -> p a c", a=2),
                                   ACT.Copy).then_inc(S["v"], 1)

            @block.vector
            def _(dve):
                for p in range(PAIRS):
                    dve.scalar_tensor_tensor(out=rk[:, p, :], in0=Z["r"][:, p, :], scalar=C.v["r_k"][:, p:p + 1],
                                             in1=Z["k"][:, p, CTX:ALL], op0=ALU.mult, op1=ALU.mult)\
                       .then_inc(S["rk"], 1)
                dve.wait_ge(S["v"], 2)
                dve.wait_ge(S["rk_sum"], 1)
                for i in range(2):
                    c = slice(2 * i, 2 * i + 2)
                    S.link(dve, dve.tensor_tensor(vT[:, c, :], vT[:, c, :], C.bank[4 + i][:, :].rearrange(
                        "p (a c) -> p a c", a=2), ALU.mult), "bonus")
                S.link(dve, dve.tensor_tensor(ya[:, :, :], ya[:, :, :], vT[:, :, :], ALU.add), "added")
                dve.wait_ge(S["gate"], 1)
                for i in range(2):
                    c = slice(2 * i, 2 * i + 2)
                    S.link(dve, dve.tensor_tensor(ya[:, c, :], ya[:, c, :], C.bank[2 + i][:, :].rearrange(
                        "p (a c) -> p a c", a=2), ALU.mult), "gated")
        S.close()


def na_attention(C, A, Z, qn, kn, yb):
    nc = C.nc
    S = Stage(nc, "na")
    units = [(h, t) for h in range(NH) for t in range(TT)]
    N = len(units)
    scale = HD ** -0.5
    with ExitStack() as local:
        sb = lambda name, shape: local.enter_context(nc.sbuf_tensor(name, shape, F32))
        bias = sb("na_bias", [P, 3, SEQ])
        mask = sb("na_mask", [P, TT, SEQ])
        sc = sb("na_scores", [P, 2, ALL])
        pT = sb("na_probsT", [P, 2, ALL])
        mx = sb("na_max", [P, N])
        rs = sb("na_sum", [P, N])
        with nc.Block() as block:
            @block.sync
            def _(sp):
                sp.dma_start(mask[:, :, :], A["na_mask"]).then_inc(S["mask"], 16)
                for n, (h, t) in enumerate(units):
                    S.wait(sp, "biased", n - 2)
                    sp.dma_start(bias[:, n % 3, :], A["na_bias"][h, t]).then_inc(S[f"bias{n % 3}"], 16)

            @block.gpsimd
            def _(pool):
                pool.wait_ge(S["mask"], 16)
                for n, (h, t) in enumerate(units):
                    pool.wait_ge(S[f"bias{n % 3}"], 16 * (n // 3 + 1))
                    pool.tensor_tensor(bias[:, n % 3, :], bias[:, n % 3, :], mask[:, t, :], ALU.add)\
                        .then_inc(S["bias_masked"], 1)

            @block.tensor
            def _(pe):
                def scores(n):
                    h, t = units[n]
                    r, p = slice(HD * (h % 2), HD * (h % 2) + HD), h // 2
                    if n >= 2:
                        pe.wait_ge(S["biased"], n - 1)
                    pe.matmul(C.bank[n % 2][:, :], qn[r, p, t * P:(t + 1) * P], kn[r, p, :],
                              start=True, stop=True).then_inc(S["scores"], 1)

                scores(0)
                for n, (h, t) in enumerate(units):
                    r, p = slice(HD * (h % 2), HD * (h % 2) + HD), h // 2
                    if n + 1 < N:
                        scores(n + 1)
                    pe.wait_ge(S["probs"], n + 1)
                    if n >= 2:
                        pe.wait_ge(S["turned_out"], n - 1)
                    for k in range(4):
                        ins = pe.transpose(C.bank[2 + n % 2][:, k * P:(k + 1) * P],
                                           sc[:, n % 2, k * P:(k + 1) * P], C.sq["ident"])
                    ins.then_inc(S["turned"], 1)
                    pe.wait_ge(S["turned_out"], n + 1)
                    if n >= 2:
                        pe.wait_ge(S["out"], n - 1)
                    product(pe, C.bank[4 + n % 2][r, 0:P],
                            [(Z["vb"][:, k, h * HD:(h + 1) * HD], pT[:, n % 2, k * P:(k + 1) * P])
                             for k in range(4)]).then_inc(S["mixed"], 1)

            @block.scalar
            def _(act):
                for n in range(N):
                    act.wait_ge(S["max"], n + 1)
                    act.activation(sc[:, n % 2, :], sc[:, n % 2, :], ACT.Exp, bias=mx[:, n:n + 1],
                                   accum_out=rs[:, n:n + 1]).then_inc(S["exp"], 1)
                    act.wait_ge(S["turned"], n + 1)
                    S.wait(act, "mixed", n - 1)
                    act.activation(pT[:, n % 2, :], C.bank[2 + n % 2][:, :], ACT.Copy).then_inc(S["turned_out"], 1)

            @block.vector
            def _(dve):
                def begin(n):
                    h, t = units[n]
                    dve.wait_ge(S["scores"], n + 1)
                    S.wait(dve, "turned", n - 1)
                    dve.wait_ge(S["bias_masked"], n + 1)
                    dve.tensor_scalar(sc[:, n % 2, 0:CTX], C.bank[n % 2][:, 0:CTX], scale, None, ALU.mult)\
                       .then_inc(S["ctx_scores"], 1)
                    S.link(dve, dve.scalar_tensor_tensor(out=sc[:, n % 2, CTX:ALL], in0=C.bank[n % 2][:, CTX:ALL],
                                                         scalar=scale, in1=bias[:, n % 3, :], op0=ALU.mult,
                                                         op1=ALU.add), "biased")
                    S.link(dve, dve.tensor_reduce(mx[:, n:n + 1], sc[:, n % 2, :], AX, ALU.max), "reduced")
                    dve.tensor_scalar(mx[:, n:n + 1], mx[:, n:n + 1], -1.0, None, ALU.mult).then_inc(S["max"], 1)

                begin(0)
                for n, (h, t) in enumerate(units):
                    if n + 1 < N:
                        begin(n + 1)
                    dve.wait_ge(S["exp"], n + 1)
                    S.link(dve, dve.reciprocal(rs[:, n:n + 1], rs[:, n:n + 1]), "inverse")
                    dve.tensor_scalar(sc[:, n % 2, :], sc[:, n % 2, :], rs[:, n:n + 1], None, ALU.mult)\
                       .then_inc(S["probs"], 1)
                    dve.wait_ge(S["mixed"], n + 1)
                    r, p = slice(HD * (h % 2), HD * (h % 2) + HD), h // 2
                    dve.tensor_copy(yb[r, p, t * P:(t + 1) * P], C.bank[4 + n % 2][r, 0:P]).then_inc(S["out"], 1)
        S.close()


def router(C, A, h2, gate_all):
    nc = C.nc
    S = Stage(nc, "router")
    with ExitStack() as local:
        sb = lambda name, shape: local.enter_context(nc.sbuf_tensor(name, shape, F32))
        rw = sb("router_w", [P, KT, N_EXP])
        rb = sb("router_b", [P, N_EXP])
        pick = sb("pick", [N_EXP, N_EXP, P])
        sc = sb("r_scores", [P, TT, N_EXP])
        sel = sb("r_sel", [P, TT, N_EXP])
        pair = sb("r_pair", [P, TT, 4, 6])
        grp = sb("r_grp", [P, TT, 4])
        top = sb("r_top", [P, TT, 8])
        den = sb("r_den", [P, TT])
        gT = sb("r_gateT", [N_EXP, SEQ])
        with nc.Block() as block:
            @block.sync
            def _(sp):
                for dst, src in ((rw[:, :, :], "router_w"), (rb[:, :], "router_bias"), (pick[:, :, :], "pick")):
                    sp.dma_start(dst, A[src]).then_inc(S["loaded"], 16)

            @block.tensor
            def _(pe):
                pe.wait_ge(S["loaded"], 48)
                for t in range(TT):
                    ins = product(pe, C.bank[0][:, t * N_EXP:(t + 1) * N_EXP],
                                  [(h2[:, k, t * P:(t + 1) * P], rw[:, k, :]) for k in range(KT)])
                ins.then_inc(S["logits"], 1)
                pe.wait_ge(S["gates"], TT)
                for t in range(TT):
                    ins = pe.transpose(C.bank[1][0:N_EXP, t * P:(t + 1) * P], sel[:, t, :], C.sq["ident"])
                ins.then_inc(S["turned"], 1)
                pe.wait_ge(S["gateT"], 1)
                for e in range(N_EXP):
                    if e >= 4:
                        pe.wait_ge(S["spread_out"], e - 3)
                    pe.matmul(C.bank[2 + e % 4][:, 0:SEQ], pick[:, e, :], gT[:, :], start=True, stop=True)\
                      .then_inc(S["spread"], 1)

            @block.scalar
            def _(act):
                act.wait_ge(S["logits"], 1)
                act.activation(sc[:, :, :], C.bank[0][:, 0:TT * N_EXP].rearrange("p (t e) -> p t e", t=TT),
                               ACT.Sigmoid).then_inc(S["scores"], 1)
                act.wait_ge(S["turned"], 1)
                act.activation(gT[:, :], C.bank[1][0:N_EXP, 0:SEQ], ACT.Copy).then_inc(S["gateT"], 1)
                for e in range(N_EXP):
                    act.wait_ge(S["spread"], e + 1)
                    act.activation(gate_all[:, e, :], C.bank[2 + e % 4][:, 0:SEQ], ACT.Copy)\
                       .then_inc(S["spread_out"], 1)

            @block.vector
            def _(dve):
                L = lambda ins: S.link(dve, ins, "vector")
                dve.wait_ge(S["loaded"], 48)
                dve.wait_ge(S["scores"], 1)
                L(dve.tensor_tensor(sel[:, :, :], sc[:, :, :], rb[:, :].unsqueeze(1).broadcast_to([P, TT, N_EXP]), ALU.add))
                for t in range(TT):
                    s = sel[:, t, :].rearrange("p (g e) -> p g e", g=4)
                    at = 0
                    for gap in (1, 2, 3):
                        L(dve.tensor_tensor(pair[:, t, :, at:at + 4 - gap], s[:, :, 0:4 - gap], s[:, :, gap:4], ALU.add))
                        at += 4 - gap
                    L(dve.tensor_reduce(grp[:, t, :], pair[:, t, :, :], AX, ALU.max))
                    L(dve.tensor_reduce(den[:, t:t + 1], grp[:, t, :], AX, ALU.max))
                    L(dve.tensor_scalar(grp[:, t, :], grp[:, t, :], den[:, t:t + 1], None, ALU.is_ge))
                    g = grp[:, t, :].unsqueeze(2).broadcast_to([P, 4, 4])
                    L(dve.tensor_tensor(s, s, g, ALU.mult))
                    L(dve.tensor_scalar(grp[:, t, :], grp[:, t, :], 1.0, -NEG, ALU.subtract, ALU.mult))
                    L(dve.tensor_tensor(s, s, g, ALU.add))
                    L(dve.max(top[:, t, :], sel[:, t, :]))
                    L(dve.tensor_scalar(sel[:, t, :], sel[:, t, :], top[:, t, 1:2], None, ALU.is_ge))
                    L(dve.tensor_tensor(sel[:, t, :], sel[:, t, :], sc[:, t, :], ALU.mult))
                    L(dve.tensor_reduce(den[:, t:t + 1], sel[:, t, :], AX, ALU.add))
                    L(dve.reciprocal(den[:, t:t + 1], den[:, t:t + 1]))
                    S.link(dve, dve.tensor_scalar(sel[:, t, :], sel[:, t, :], den[:, t:t + 1], None, ALU.mult), "gates")
        S.close()


def experts(C, A, h2, gate_all, xT, m5):
    nc = C.nc
    S = Stage(nc, "experts")
    HT = D_EXP // P
    NT = 6
    FIRST_UP = 4
    with ExitStack() as local:
        act_h = local.enter_context(nc.sbuf_tensor("silu_h", [P, HT, SEQ], F32))
        hid = local.enter_context(nc.sbuf_tensor("hid", [P, 2, HT, SEQ], F32R))
        w2 = local.enter_context(nc.sbuf_tensor("moe_halves", [P, 2, 2, TILE], F32R))
        zero = local.enter_context(nc.sbuf_tensor("zero_row", [1, 512], F32))
        up = lambda m: C.bank[m]
        body = ("up0", "down0", "down1", "up1", "up2", "up3")

        def number(e, i):
            return FIRST_UP + NT * (e - 1) + i

        def arrivals(e, i):
            return 16 * (e - 1) + 16 * ((FIRST_UP + i) // NT + 1)

        with nc.Block() as block:
            @block.sync
            def _(sp):
                for n in range(NT):
                    sp.dma_start(C.ring[:, n, :], A["moe"][n, :, :]).then_inc(S[f"loaded{n}"], 16)
                with sp.Fori(1, N_EXP) as e:
                    for i in range(NT):
                        sp.wait_ge(S["low"], NT * (e - 1) + i + 1)
                        sp.dma_start(C.ring[:, i, :], A["moe"][NT * e + i, :, :]).then_inc(S[f"loaded{i}"], 16)

            @block.tensor
            def _(pe):
                def halves(n2, k):
                    return [w2[:, n2, i, :].rearrange("p (k c) -> p k c", k=k) for i in range(2)]

                def up_tile(m, n2):
                    w = halves(n2, KT)
                    for i in range(2):
                        for k in range(KT):
                            ins = split_product(pe, up(m)[:, i * SEQ:(i + 1) * SEQ],
                                                [x[:, k, i * P:(i + 1) * P] for x in w],
                                                [x[:, k, :] for x in h2], k == 0, k == KT - 1)
                    ins.then_inc(S["tile"], 1)

                def down_tile(j, n2):
                    w = halves(n2, HT)
                    for q in range(4):
                        dt = 4 * j + q
                        out = C.bank[4 + dt // 2][:, (dt % 2) * SEQ:(dt % 2) * SEQ + SEQ]
                        for m in range(HT):
                            a = [x[:, m, q * P:(q + 1) * P] for x in w]
                            b = [hid[:, i, m, :] for i in range(2)]
                            for x, y in ((a[0], b[0]), (a[0], b[1]), (a[1], b[0])):
                                ins = pe.matmul(out, x, y, start=False, stop=False, skip_group_check=True)
                    ins.then_inc(S["tile"], 1)

                pe.wait_ge(S["zero"], 1)
                for b in range(4):
                    pe.matmul(C.bank[4 + b][:, :], zero[:, 0:P], zero[:, :], start=True, stop=False,
                              skip_group_check=True)
                for m in range(HT):
                    pe.wait_ge(S["low"], m + 1)
                    up_tile(m, m % 2)
                with pe.Fori(1, N_EXP) as e:
                    for i, what in enumerate(body):
                        if what == "down0":
                            pe.wait_ge(S["hid"], e * HT)
                        pe.wait_ge(S["low"], number(e, i) + 1)
                        if what.startswith("up"):
                            up_tile(int(what[-1]), i % 2)
                        else:
                            down_tile(int(what[-1]), i % 2)
                pe.wait_ge(S["hid"], N_EXP * HT)
                for j in range(2):
                    pe.wait_ge(S["low"], N_EXP * NT - 1 + j)
                    down_tile(j, j % 2)
                pe.matmul(C.bank[4][:, 0:P], zero[:, 0:P], zero[:, 0:P], start=False, stop=True,
                          skip_group_check=True).then_inc(S["done"], 1)

            @block.scalar
            def _(act):
                def high(slot, arrived, n2, used):
                    act.wait_ge(S[f"loaded{slot}"], arrived)
                    if used is not None:
                        act.wait_ge(S["tile"], used)
                    act.activation(w2[:, n2, 0, :], C.ring[:, slot, :], ACT.Copy).then_inc(S["high"], 1)

                def silu(m, n):
                    act.wait_ge(S["tile"], n + 1)
                    act.activation(act_h[:, m, :], up(m)[:, 0:SEQ], ACT.Silu).then_inc(S["silu"], 1)

                def hidden_high(m, count):
                    act.wait_ge(S["hidden"], count)
                    act.activation(hid[:, 0, m, :], act_h[:, m, :], ACT.Copy).then_inc(S["hid_high"], 1)

                high(0, 16, 0, None)
                for m in range(HT):
                    high(m + 1, 16, (m + 1) % 2, m if m else None)
                    silu(m, m)
                    hidden_high(m, m + 1)
                with act.Fori(1, N_EXP) as e:
                    for i in range(NT):
                        high((FIRST_UP + i + 1) % NT, arrivals(e, i + 1), (i + 1) % 2, number(e, i))
                        if i == 2:
                            silu(0, number(e, 0))
                            act.wait_ge(S["tile"], number(e, 2) + 1)
                            hidden_high(0, e * HT + 1)
                        elif i > 2:
                            silu(i - 2, number(e, i))
                            hidden_high(i - 2, e * HT + i - 1)
                high(5, 16 * N_EXP, 1, N_EXP * NT - 2)

            @block.vector
            def _(dve):
                def low(slot, n2, n):
                    dve.wait_ge(S["high"], n + 1)
                    dve.tensor_tensor(w2[:, n2, 1, :], C.ring[:, slot, :], w2[:, n2, 0, :].bitcast(F32), ALU.subtract)\
                       .then_inc(S["low"], 1)

                def hidden(m, e, count):
                    dve.wait_ge(S["silu"], count)
                    dve.tensor_tensor(act_h[:, m, :], act_h[:, m, :], gate_all[:, e, :], ALU.mult)\
                       .then_inc(S["gated"], 1)
                    dve.wait_ge(S["gated"], count)
                    dve.tensor_tensor(act_h[:, m, :], act_h[:, m, :], up(m)[:, SEQ:2 * SEQ], ALU.mult)\
                       .then_inc(S["hidden"], 1)
                    dve.wait_ge(S["hid_high"], count)
                    dve.tensor_tensor(hid[:, 1, m, :], act_h[:, m, :], hid[:, 0, m, :].bitcast(F32), ALU.subtract)\
                       .then_inc(S["hid"], 1)

                dve.memset(zero[:, :], 0.0).then_inc(S["zero"], 1)
                low(0, 0, 0)
                for m in range(HT):
                    low(m + 1, (m + 1) % 2, m + 1)
                    hidden(m, 0, m + 1)
                with dve.Fori(1, N_EXP) as e:
                    for i in range(NT):
                        low((FIRST_UP + i + 1) % NT, (i + 1) % 2, number(e, i + 1))
                        if i == 2:
                            hidden(0, e, e * HT + 1)
                        elif i > 2:
                            hidden(i - 2, e, e * HT + i - 1)
                low(5, 1, N_EXP * NT - 1)
                dve.wait_ge(S["done"], 1)
                for k in range(KT):
                    S.link(dve, dve.scalar_tensor_tensor(
                        out=xT[:, k, :], in0=C.bank[4 + k // 2][:, (k % 2) * SEQ:(k % 2) * SEQ + SEQ],
                        scalar=m5[:, k:k + 1], in1=xT[:, k, :], op0=ALU.mult, op1=ALU.add), "x")
        S.close()


def first_block(C, A, xT):
    nc = C.nc
    with ExitStack() as outer:
        sb = lambda name, shape: outer.enter_context(nc.sbuf_tensor(name, shape, F32))
        mod = sb("mod", [P, 6 * KT, 2])
        g1 = sb("gain_x", [P, KT])
        gc = sb("gain_c", [P, KT])
        g2 = sb("gain_2", [P, KT])
        modulation(C, A, mod)
        gains(C, "gains", [(g1[:, :], C.v["norm1_g"], mod[:, KT:2 * KT, 0]),
                           (gc[:, :], C.v["norm1_g"], mod[:, KT:2 * KT, 1]),
                           (g2[:, :], C.v["norm2_g"], mod[:, 4 * KT:5 * KT, 0])])
        upper = outer.enter_context(ExitStack())
        su = lambda name, shape: upper.enter_context(nc.sbuf_tensor(name, shape, F32))
        gates = su("gates", [P, 2 * KT, SEQ])
        yab = su("yab", [P, 2 * PAIRS, SEQ])
        ya, yb = yab[:, 0:PAIRS, :], yab[:, PAIRS:2 * PAIRS, :]
        with ExitStack() as mid:
            sm = lambda name, shape: mid.enter_context(nc.sbuf_tensor(name, shape, F32))
            Z = {"r": sm("z_r", [P, PAIRS, SEQ]), "k": sm("z_k", [P, PAIRS, ALL]),
                 "v": sm("z_v", [P, 4, NH * HD]), "lw": sm("z_lw", [P, ALL]), "la": sm("z_la", [P, ALL]),
                 "lg": sm("z_lg", [P, SEQ]), "q": sm("z_q", [P, PAIRS, SEQ]), "kb": sm("z_kb", [P, PAIRS, ALL]),
                 "vb": sm("z_vb", [P, 4, NH * HD])}
            with ExitStack() as local:
                hs = local.enter_context(nc.sbuf_tensor("h1_halves", [P, 2, KT, ALL], F32R))
                h = (hs[:, 0, :, :], hs[:, 1, :, :])
                h1 = C.ring[:, 0:2, :].rearrange("p a (b c) -> p (a b) c", c=ALL)
                xc = C.ring[:, 2, :].rearrange("p (b c) -> p b c", c=CTX)
                load_all(nc, "context", [(xc, A["ctxT"])])
                norm(C, "norm1", [(xc, h1[:, :, 0:CTX], gc, mod[:, 0:KT, 1], CTX),
                                  (xT[:, :, :], h1[:, :, CTX:ALL], g1, mod[:, 0:KT, 0], SEQ)], 0)
                split(C, "split1", [(h1[:, k, :], h[0][:, k, :], h[1][:, k, :]) for k in range(KT)])
                jobs = []

                def turned(col, n, dst, lo, func=None):
                    for m in range(n // P):
                        c = col + m * P
                        jobs.append((c // 256, c % 256, P, True, h, lo, ALL - lo, dst[m], func, None))

                def straight(col, n, dst):
                    for m in range(n // 256):
                        for t in range(ALL // P):
                            jobs.append(((col + m * 256) // 256, 0, 256, False, h, t * P, P,
                                         dst[:, t, m * 256:(m + 1) * 256], None, None))

                per = lambda t, n: [t[:, i, :] for i in range(n)]
                turned(0, 512, per(Z["r"], PAIRS), CTX)
                turned(512, 512, per(Z["k"], PAIRS), 0)
                straight(1024, 512, Z["v"])
                turned(1536, 128, [Z["lw"][:, :]], 0, ACT.Tanh)
                turned(1664, 128, [Z["la"][:, :]], 0)
                turned(1792, 128, [Z["lg"][:, :]], CTX, ACT.Sigmoid)
                turned(2048, 512, per(Z["q"], PAIRS), CTX)
                turned(2560, 512, per(Z["kb"], PAIRS), 0)
                straight(3072, 512, Z["vb"])
                turned(3584, 2048, per(gates, 2 * KT), CTX, ACT.Sigmoid)
                linear(C, "w_in", [A["w_in"][i] for i in range(22)], jobs)
            head_norm(C, "q_norm", Z["q"], Z["q"], 0, C.v["q_g"], None, False)
            head_norm(C, "k_norm", Z["kb"], Z["kb"], 0, C.v["k_g"], None, False, cols=ALL)
            na_attention(C, A, Z, Z["q"], Z["kb"], yb)
            with ExitStack() as local:
                sl = lambda name, shape: local.enter_context(nc.sbuf_tensor(name, shape, F32))
                W = {"kk": Z["kb"], "a": sl("w_a", [P, 2, PAIRS, P]), "sig": sl("w_sig", [P, 2, NH * HD]),
                     "S0": sl("w_S0", [P, 2, PAIRS, P]),
                     "y": Z["vb"][:, :, :].rearrange("p a (b c) -> p (a b) c", c=SEQ)
                                          .rearrange("p (d a) c -> p d a c", d=2),
                     "wb": sl("lora_w", [P, NH * HD]), "ab": sl("lora_a", [P, NH * HD]),
                     "w0": sl("w0", [P, NH * HD])}
                load_all(nc, "lora", [(W["wb"][:, :], A["rw_w_lora_b"]), (W["ab"][:, :], A["rw_a_lora_b"]),
                                      (W["w0"][:, :], A["rw_w0"])])
                rwkv_prep(C, Z, W)
                with ExitStack() as inner:
                    si = lambda name, shape: inner.enter_context(nc.sbuf_tensor(name, shape, F32))
                    B = {"qr": si("b_qr", [P, 2, PAIRS, 2 * P]), "bb": C.ring[:, 5, 0:8 * P].rearrange("p (d a c) -> p d a c", d=2, a=PAIRS),
                         "kn": C.ring[:, 5, 8 * P:16 * P].rearrange("p (d a c) -> p d a c", d=2, a=PAIRS), "btok": si("b_btok", [P, 2, NH * HD]),
                         "ktok": si("b_ktok", [P, 2, NH * HD]), "ein": si("b_ein", [P, 2, PAIRS, P]),
                         "eex": si("b_eex", [P, 2, PAIRS, P]), "eneg": si("b_eneg", [P, 2, PAIRS, P]),
                         "tmp": Z["q"][:, :, :].rearrange("p a (d c) -> p d a c", d=2),
                         "X": C.ring[:, 0:4, :].rearrange("p a (b c) -> p (a b) c", c=4 * P),
                         "PT": C.ring[:, 4, :].rearrange("p (b c) -> p b c", c=P),
                         "M": si("b_m", [P, 2 * NH, 2 * P])}
                    B["R"] = B["eex"][:, :, :, :].rearrange("p d a c -> p d (a c)")
                    B["nU"] = B["eneg"][:, :, :, :].rearrange("p d a c -> p d (a c)")
                    B["SW"] = si("b_sw", [P, PAIRS, P])
                    S = Stage(nc, "delta")
                    with nc.Block() as block:
                        @block.vector
                        def _(dve):
                            S.link(dve, dve.memset(W["S0"][:, :, :, :], 0.0), "state")
                    S.close()
                    for step in range(4):
                        rwkv_tile(C, Z, W, step, B)
                S = Stage(nc, "directions")
                with nc.Block() as block:
                    @block.vector
                    def _(dve):
                        S.link(dve, dve.tensor_tensor(ya[:, :, :], W["y"][:, 0, :, :], W["y"][:, 1, :, :], ALU.add), "y")
                S.close()
            head_norm(C, "y_norm", ya, ya, 1, C.v["ln_g"], C.v["ln_b"], True)
            rwkv_bonus(C, A, Z, None, ya)
        with ExitStack() as local:
            sl = lambda name, shape, dt=F32: local.enter_context(nc.sbuf_tensor(name, shape, dt))
            pab = sl("p_ab", [P, 2 * KT, SEQ])
            ys = sl("y_halves", [P, 2, KT, SEQ], F32R)
            split(C, "split_y", [(yab[:, :, :], ys[:, 0, :, :], ys[:, 1, :, :])])
            jobs = []
            for i in range(2):
                y = (ys[:, 0, i * PAIRS:(i + 1) * PAIRS, :], ys[:, 1, i * PAIRS:(i + 1) * PAIRS, :])
                for m in range(KT):
                    jobs.append((2 * i + m // 4, P * (m % 4), P, True, y, 0, SEQ,
                                 pab[:, i * KT + m, :], None, gates[:, i * KT + m, :]))

            def merge(S, dve):
                S.link(dve, dve.tensor_tensor(pab[:, 0:KT, :], pab[:, 0:KT, :], pab[:, KT:2 * KT, :], ALU.add), "merged")

            linear(C, "proj", [A["proj_ab"][i] for i in range(4)], jobs, kt=4, extra=merge)
            split(C, "split_p", [(pab[:, 0:KT, :], ys[:, 0, :, :], ys[:, 1, :, :])])
            jobs = [(m // 2, P * (m % 2), P, True, (ys[:, 0, :, :], ys[:, 1, :, :]), 0, SEQ, pab[:, KT + m, :], None,
                     None) for m in range(KT)]

            def residual(S, dve):
                for k in range(KT):
                    S.link(dve, dve.scalar_tensor_tensor(out=xT[:, k, :], in0=pab[:, KT + k, :],
                                                         scalar=mod[:, 2 * KT + k:2 * KT + k + 1, 0],
                                                         in1=xT[:, k, :], op0=ALU.mult, op1=ALU.add), "x")
            linear(C, "w_out", [A["w_out"][i] for i in range(4)], jobs, extra=residual)
        upper.close()
        with ExitStack() as local:
            sl = lambda name, shape, dt=F32: local.enter_context(nc.sbuf_tensor(name, shape, dt))
            h2 = sl("h2", [P, KT, SEQ])
            hs = sl("h2_halves", [P, 2, KT, SEQ], F32R)
            gate_all = sl("gate_all", [P, N_EXP, SEQ])
            m5 = sl("m5", [P, KT])
            norm(C, "norm2", [(xT[:, :, :], h2[:, :, :], g2, mod[:, 3 * KT:4 * KT, 0], SEQ)], 0)
            split(C, "split2", [(h2[:, :, :], hs[:, 0, :, :], hs[:, 1, :, :])])
            S = Stage(nc, "m5")
            with nc.Block() as block:
                @block.vector
                def _(dve):
                    S.link(dve, dve.tensor_copy(m5[:, :], mod[:, 5 * KT:6 * KT, 0]), "m5")
            S.close()
            router(C, A, h2, gate_all)
            experts(C, A, (hs[:, 0, :, :], hs[:, 1, :, :]), gate_all, xT, m5)


H4 = 4
MIX = H4 * HD
N_CMP = (SEQ - 32) // 16 + 1
GATHERED = 8
TOPK = 16
PH = 8
KEYS = 128
DN_ALPHA = 4.0 ** 0.25
TILES2 = 29


def stick_breaking(C, A, Z, out):
    nc = C.nc
    S = Stage(nc, "stick")
    scale = HD ** -0.5
    with ExitStack() as local:
        sb = lambda name: local.enter_context(nc.sbuf_tensor(name, [P, H4, TT * SEQ], F32))
        z, l = sb("sb_z"), sb("sb_l")
        mask = local.enter_context(nc.sbuf_tensor("sb_mask", [P, TT * SEQ], F32))
        with nc.Block() as block:
            @block.sync
            def _(sp):
                sp.dma_start(mask[:, :], A["causal"]).then_inc(S["mask"], 16)

            @block.tensor
            def _(pe):
                for h in range(H4):
                    r, p = slice(HD * (h % 2), HD * (h % 2) + HD), h // 2
                    for s in range(TT):
                        ins = pe.matmul(C.bank[h][:, s * SEQ:(s + 1) * SEQ], Z["sk"][r, p, s * P:(s + 1) * P],
                                        Z["sq"][r, p, :], start=True, stop=True)
                    ins.then_inc(S["z"], 1)
                for h in range(H4):
                    pe.wait_ge(S["softplus"], h + 1)
                    lo, hi = l[:, h, 0:SEQ], l[:, h, SEQ:2 * SEQ]
                    product(pe, C.bank[4 + h][:, 0:SEQ], [(C.sq["neg_ge"], lo), (C.sq["neg_ones"], hi)])
                    product(pe, C.bank[4 + h][:, SEQ:2 * SEQ], [(C.sq["neg_ge"], hi)]).then_inc(S["sums"], 1)
                for h in range(H4):
                    pe.wait_ge(S["weights"], h + 1)
                    r = slice(HD * (h % 2), HD * (h % 2) + HD)
                    product(pe, C.bank[h][r, 0:SEQ], [(Z["sv"][:, s, h * HD:(h + 1) * HD],
                                                       l[:, h, s * SEQ:(s + 1) * SEQ]) for s in range(TT)])\
                        .then_inc(S["o"], 1)

            @block.scalar
            def _(act):
                for h in range(H4):
                    act.wait_ge(S["z"], h + 1)
                    act.activation(z[:, h, :], C.bank[h][:, :], ACT.Copy, scale=scale).then_inc(S["z_out"], 1)
                    S.link(act, act.activation(l[:, h, :], C.bank[h][:, :], ACT.Abs, scale=scale), "abs")
                for h in range(H4):
                    S.link(act, act.activation(l[:, h, :], l[:, h, :], ACT.Exp, scale=-1.0), "exp")
                for h in range(H4):
                    act.activation(l[:, h, :], l[:, h, :], ACT.Ln, bias=C.eps[3]).then_inc(S["log"], 1)
                for h in range(H4):
                    act.wait_ge(S["log_w"], h + 1)
                    act.activation(l[:, h, :], z[:, h, :], ACT.Exp).then_inc(S["w"], 1)
                for h in range(H4):
                    r, p = slice(HD * (h % 2), HD * (h % 2) + HD), h // 2
                    act.wait_ge(S["o"], h + 1)
                    act.activation(out[r, p, :], C.bank[h][r, 0:SEQ], ACT.Copy).then_inc(S["out"], 1)

            @block.vector
            def _(dve):
                dve.wait_ge(S["mask"], 16)
                for h in range(H4):
                    dve.wait_ge(S["log"], h + 1)
                    S.link(dve, dve.scalar_tensor_tensor(out=l[:, h, :], in0=z[:, h, :], scalar=0.0, in1=l[:, h, :],
                                                         op0=ALU.max, op1=ALU.add), "sp")
                    dve.tensor_tensor(l[:, h, :], l[:, h, :], mask[:, :], ALU.mult).then_inc(S["softplus"], 1)
                for h in range(H4):
                    dve.wait_ge(S["sums"], h + 1)
                    S.link(dve, dve.tensor_tensor(z[:, h, :], z[:, h, :], C.bank[4 + h][:, :], ALU.add), "added")
                    dve.tensor_scalar(z[:, h, :], z[:, h, :], 0.0, None, ALU.min).then_inc(S["log_w"], 1)
                for h in range(H4):
                    dve.wait_ge(S["w"], h + 1)
                    dve.tensor_tensor(l[:, h, :], l[:, h, :], mask[:, :], ALU.mult).then_inc(S["weights"], 1)
        S.close()


def nsa(C, A, l_, Z, out):
    nc = C.nc
    S = Stage(nc, "nsa")
    scale = HD ** -0.5
    units = [(t, h) for t in range(TT) for h in range(H4)]
    N = len(units)
    NC = N_CMP
    with ExitStack() as local:
        sb = lambda name, shape: local.enter_context(nc.sbuf_tensor(name, shape, F32))
        wkv = sb("cmp_w", [HD, 2, 32, HD])
        pos = sb("cmp_pos", [HD, 32])
        blk = sb("cmp_blocks", [HD, 2, 32, NC])
        kc = sb("cmp_k", [HD, NC])
        vc = sb("cmp_v", [NC, HD])
        cb = sb("cmp_bias", [P, N, NC])
        seen = sb("cmp_seen", [P, TT])
        lb = sb("lin_bias", [P, N, SEQ])
        pc = sb("cmp_p", [P, N, NC])
        cm = sb("cmp_max", [P, N])
        pcT = sb("cmp_pT", [NC, N * P])
        sc = sb("nsa_s", [P, 2, 2 * SEQ])
        pT = sb("nsa_pT", [P, 2, 4 * P])
        mx = sb("nsa_max", [P, N, 2])
        rs = sb("nsa_sum", [P, N, 2])
        with nc.Block() as block:
            @block.sync
            def _(sp):
                for dst, src in ((wkv[:, :, :, :], A["cmp_w"][l_, :, :, :, :]), (pos[:, :], A["cmp_pos"][l_, :, :]),
                                 (cb[:, :, :], A["cmp_bias"]), (seen[:, :], A["cmp_seen"]), (lb[:, :, :], A["lin_bias"])):
                    sp.dma_start(dst, src).then_inc(S["loaded"], 16)

            @block.tensor
            def _(pe):
                pe.wait_ge(S["loaded"], 80)
                pe.wait_ge(S["blocks"], 4)
                product(pe, C.bank[6][0:HD, 0:NC], [(wkv[:, 0, i, :], blk[:, 0, i, :]) for i in range(32)])\
                    .then_inc(S["kc"], 1)
                product(pe, C.bank[7][0:NC, 0:HD], [(blk[:, 1, i, :], wkv[:, 1, i, :]) for i in range(32)])\
                    .then_inc(S["vc"], 1)
                pe.wait_ge(S["kv_out"], 2)
                for n, (t, h) in enumerate(units):
                    ins = pe.matmul(C.bank[6][:, n * NC:(n + 1) * NC], Z["nq"][:, h, t * P:(t + 1) * P], kc[:, :],
                                    start=True, stop=True)
                ins.then_inc(S["cmp_scores"], 1)
                pe.wait_ge(S["cmp_p"], 1)
                for n in range(N):
                    ins = pe.transpose(C.bank[6 + n // 4][0:NC, (n % 4) * P:(n % 4) * P + P], pc[:, n, :], C.sq["ident"])
                ins.then_inc(S["cmp_turned"], 1)
                pe.wait_ge(S["cmp_pT"], 1)

                def scores(n):
                    t, h = units[n]
                    if n >= 2:
                        pe.wait_ge(S["biased"], n - 1)
                    for b in range(2):
                        ins = pe.matmul(C.bank[n % 2][:, b * SEQ:(b + 1) * SEQ], Z["nq"][:, h, t * P:(t + 1) * P],
                                        Z["nk"][:, b, :], start=True, stop=True)
                    ins.then_inc(S["scores"], 1)

                scores(0)
                for n, (t, h) in enumerate(units):
                    r = slice(HD * (h % 2), HD * (h % 2) + HD)
                    if n + 1 < N:
                        scores(n + 1)
                    pe.wait_ge(S["probs"], 2 * n + 2)
                    if n >= 2:
                        pe.wait_ge(S["turned_out"], n - 1)
                    for k in range(4):
                        ins = pe.transpose(C.bank[2 + n % 2][:, k * P:(k + 1) * P], sc[:, n % 2, k * P:(k + 1) * P],
                                           C.sq["ident"])
                    ins.then_inc(S["turned"], 1)
                    pe.wait_ge(S["turned_out"], n + 1)
                    if n >= 2:
                        pe.wait_ge(S["out"], n - 1)
                    product(pe, C.bank[4 + n % 2][r, 0:P],
                            [(vc[:, :], pcT[:, n * P:(n + 1) * P])] +
                            [(Z["nv"][:, k % 2, (k // 2) * HD:(k // 2 + 1) * HD], pT[:, n % 2, k * P:(k + 1) * P])
                             for k in range(4)]).then_inc(S["mixed"], 1)

            @block.scalar
            def _(act):
                act.wait_ge(S["kc"], 1)
                act.activation(kc[:, :], C.bank[6][0:HD, 0:NC], ACT.Copy).then_inc(S["kv_out"], 1)
                act.wait_ge(S["vc"], 1)
                act.activation(vc[:, :], C.bank[7][0:NC, 0:HD], ACT.Copy).then_inc(S["kv_out"], 1)
                act.wait_ge(S["cmp_s"], 1)
                act.activation(pc[:, :, :], pc[:, :, :], ACT.Exp).then_inc(S["cmp_exp"], 1)
                act.wait_ge(S["cmp_turned"], 1)
                for i in range(2):
                    ins = act.activation(pcT[:, i * 512:(i + 1) * 512], C.bank[6 + i][0:NC, :], ACT.Copy)
                ins.then_inc(S["cmp_pT"], 1)
                for n in range(N):
                    act.wait_ge(S["max"], n + 1)
                    for b in range(2):
                        half = sc[:, n % 2, b * SEQ:(b + 1) * SEQ]
                        ins = act.activation(half, half, ACT.Exp, bias=mx[:, n, b:b + 1], accum_out=rs[:, n, b:b + 1])
                    ins.then_inc(S["exp"], 1)
                    act.wait_ge(S["turned"], n + 1)
                    S.wait(act, "mixed", n - 1)
                    act.activation(pT[:, n % 2, :], C.bank[2 + n % 2][:, :], ACT.Copy).then_inc(S["turned_out"], 1)

            @block.vector
            def _(dve):
                L = lambda ins: S.link(dve, ins, "vector")
                dve.wait_ge(S["loaded"], 80)
                for b in range(2):
                    rows = Z["kcv"][:, b, :].rearrange("d (c i) -> d i c", i=16)
                    for a in range(2):
                        i = slice(16 * a, 16 * a + 16)
                        dve.tensor_tensor(blk[:, b, i, :], rows[:, :, a:a + NC],
                                          pos[:, i].unsqueeze(2).broadcast_to([HD, 16, NC]), ALU.add)\
                           .then_inc(S["blocks"], 1)
                dve.wait_ge(S["cmp_scores"], 1)
                wide = lambda a: a.unsqueeze(2).broadcast_to([P, N, NC])
                L(dve.scalar_tensor_tensor(out=pc[:, :, :].rearrange("p n c -> p (n c)"), in0=C.bank[6][:, 0:N * NC], scalar=scale, in1=cb[:, :, :].rearrange("p n c -> p (n c)"), op0=ALU.mult, op1=ALU.add))
                L(dve.tensor_reduce(cm[:, :], pc[:, :, :], AX, ALU.max))
                dve.tensor_tensor(pc[:, :, :], pc[:, :, :], wide(cm[:, :]), ALU.subtract).then_inc(S["cmp_s"], 1)
                dve.wait_ge(S["cmp_exp"], 1)
                L(dve.tensor_reduce(cm[:, :], pc[:, :, :], AX, ALU.add))
                L(dve.reciprocal(cm[:, :], cm[:, :]))
                for t in range(TT):
                    g = Z["ng"][:, t, 0:12].rearrange("p (h b) -> p h b", b=3)[:, :, 0]
                    c4 = cm[:, 4 * t:4 * t + 4]
                    L(dve.scalar_tensor_tensor(out=c4, in0=c4, scalar=seen[:, t:t + 1], in1=g, op0=ALU.mult, op1=ALU.mult))
                dve.tensor_tensor(pc[:, :, :], pc[:, :, :], wide(cm[:, :]), ALU.mult).then_inc(S["cmp_p"], 1)

                def begin(n):
                    dve.wait_ge(S["scores"], n + 1)
                    S.wait(dve, "turned", n - 1)
                    s2 = sc[:, n % 2, :].rearrange("p (b k) -> p b k", b=2)
                    S.link(dve, dve.scalar_tensor_tensor(
                        out=s2, in0=C.bank[n % 2][:, :].rearrange("p (b k) -> p b k", b=2), scalar=scale,
                        in1=lb[:, n, :].unsqueeze(1).broadcast_to([P, 2, SEQ]), op0=ALU.mult, op1=ALU.add), "biased")
                    S.link(dve, dve.tensor_reduce(mx[:, n, :], s2, AX, ALU.max), "reduced")
                    dve.tensor_scalar(mx[:, n, :], mx[:, n, :], -1.0, None, ALU.mult).then_inc(S["max"], 1)

                begin(0)
                for n, (t, h) in enumerate(units):
                    if n + 1 < N:
                        begin(n + 1)
                    dve.wait_ge(S["exp"], n + 1)
                    L(dve.reciprocal(rs[:, n, :], rs[:, n, :]))
                    L(dve.tensor_tensor(rs[:, n, :], rs[:, n, :], Z["ng"][:, t, 3 * h + 1:3 * h + 3], ALU.mult))
                    for b in range(2):
                        half = sc[:, n % 2, b * SEQ:(b + 1) * SEQ]
                        dve.tensor_scalar(half, half, rs[:, n, b:b + 1], None, ALU.mult).then_inc(S["probs"], 1)
                    dve.wait_ge(S["mixed"], n + 1)
                    r = slice(HD * (h % 2), HD * (h % 2) + HD)
                    dve.tensor_copy(out[r, h // 2, t * P:(t + 1) * P], C.bank[4 + n % 2][r, 0:P]).then_inc(S["out"], 1)
        S.close()


def retention(C, A, Z, out):
    nc = C.nc
    S = Stage(nc, "retention")
    with ExitStack() as local:
        dec = local.enter_context(nc.sbuf_tensor("ret_decay", [P, H4, TT * SEQ], F32))
        w = local.enter_context(nc.sbuf_tensor("ret_w", [P, H4, TT * SEQ], F32))
        with nc.Block() as block:
            @block.sync
            def _(sp):
                sp.dma_start(dec[:, :, :], A["ret_decay"]).then_inc(S["decay"], 16)

            @block.tensor
            def _(pe):
                for h in range(H4):
                    r, p = slice(HD * (h % 2), HD * (h % 2) + HD), h // 2
                    for s in range(TT):
                        ins = pe.matmul(C.bank[h][:, s * SEQ:(s + 1) * SEQ], Z["rk"][r, p, s * P:(s + 1) * P],
                                        Z["rq"][r, p, :], start=True, stop=True)
                    ins.then_inc(S["scores"], 1)
                for h in range(H4):
                    pe.wait_ge(S["weights"], h + 1)
                    r = slice(HD * (h % 2), HD * (h % 2) + HD)
                    product(pe, C.bank[4 + h][r, 0:SEQ], [(Z["rv"][:, s, h * HD:(h + 1) * HD],
                                                           w[:, h, s * SEQ:(s + 1) * SEQ]) for s in range(TT)])\
                        .then_inc(S["o"], 1)

            @block.vector
            def _(dve):
                dve.wait_ge(S["decay"], 16)
                for h in range(H4):
                    dve.wait_ge(S["scores"], h + 1)
                    dve.tensor_tensor(w[:, h, :], C.bank[h][:, :], dec[:, h, :], ALU.mult).then_inc(S["weights"], 1)

            @block.scalar
            def _(act):
                for h in range(H4):
                    r, p = slice(HD * (h % 2), HD * (h % 2) + HD), h // 2
                    act.wait_ge(S["o"], h + 1)
                    act.activation(out[r, p, :], C.bank[4 + h][r, 0:SEQ], ACT.Copy).then_inc(S["out"], 1)
        S.close()


def gla(C, A, l_, Z, out):
    nc = C.nc
    S = Stage(nc, "gla")
    NCH = SEQ // CH
    dk = 32
    with ExitStack() as local:
        sb = lambda name, shape: local.enter_context(nc.sbuf_tensor(name, shape, F32))
        wa = sb("gla_wa", [17, P])
        hm = sb("gla_heads", [P, H4])
        bd = sb("gla_blocks", [P, MIX])
        la = sb("gla_log", [P, TT, P])
        lt = sb("gla_tmp", [P, TT, P])
        e1, en, eb, et = (sb(f"gla_e{i}", [P, SEQ]) for i in range(4))
        k1 = sb("gla_k", [P, H4, SEQ])
        att = sb("gla_att", [P, TT, H4, P])
        st = sb("gla_state", [P, NCH, MIX])
        up = sb("gla_update", [P, MIX])
        with nc.Block() as block:
            @block.sync
            def _(sp):
                for dst, src in ((wa[:, :], A["gla_wa"][l_, :, :]), (hm[:, :], A["gla_heads"]), (bd[:, :], A["gla_blocks"])):
                    sp.dma_start(dst, src).then_inc(S["loaded"], 16)

            @block.tensor
            def _(pe):
                pe.wait_ge(S["loaded"], 48)
                for t in range(TT):
                    ins = pe.matmul(C.bank[0][:, t * P:(t + 1) * P], Z["lr"][0:17, t * P:(t + 1) * P], wa[:, :],
                                    start=True, stop=True)
                ins.then_inc(S["alpha"], 1)
                pe.wait_ge(S["log_a"], 1)
                for t in range(TT):
                    c = slice(t * P, (t + 1) * P)
                    pe.matmul(C.bank[1][:, c], la[:, t, :], C.sq["gla_mid"], start=True, stop=True)
                    pe.matmul(C.bank[2][:, c], la[:, t, :], C.sq["gla_in"], start=True, stop=True)
                    ins = pe.matmul(C.bank[3][:, c], C.sq["gla_tail"], la[:, t, :], start=True, stop=True)
                ins.then_inc(S["sums"], 1)
                pe.wait_ge(S["k1"], H4)
                for t in range(TT):
                    for h in range(H4):
                        ins = pe.matmul(C.bank[4 + t][:, h * P:(h + 1) * P], k1[:, h, t * P:(t + 1) * P],
                                        e1[:, t * P:(t + 1) * P], start=True, stop=True)
                ins.then_inc(S["pairs"], 1)
                for c in range(NCH - 1):
                    t, r = c // 2, slice(CH * (c % 2), CH * (c % 2) + CH)
                    if c >= 2:
                        pe.wait_ge(S["update"], c - 1)
                    pe.matmul(C.bank[6 + c % 2][:, 0:MIX], et[r, t * P:(t + 1) * P], Z["gv"][r, t, :],
                              start=True, stop=True).then_inc(S["outer"], 1)
                pe.wait_ge(S["att"], TT)
                for c in range(NCH):
                    t, off = c // 2, CH * (c % 2)
                    S.wait(pe, "state", c + 1)
                    for h in range(H4):
                        r, p = slice(HD * (h % 2), HD * (h % 2) + HD), h // 2
                        o = C.bank[0][r, p * SEQ + c * CH:p * SEQ + (c + 1) * CH]
                        ins = product(pe, o, [(st[:, c, h * HD:(h + 1) * HD], eb[:, c * CH:(c + 1) * CH]),
                                              (Z["gv"][:, t, h * HD:(h + 1) * HD], att[:, t, h, off:off + CH])])
                ins.then_inc(S["o"], 1)

            @block.scalar
            def _(act):
                flat = lt[:, :, :].rearrange("p t c -> p (t c)")
                act.wait_ge(S["alpha"], 1)
                S.link(act, act.activation(flat, C.bank[0][:, 0:SEQ], ACT.Abs), "a")
                S.link(act, act.activation(flat, flat, ACT.Exp, scale=-1.0), "a")
                act.activation(flat, flat, ACT.Ln, bias=C.eps[3]).then_inc(S["softplus"], 1)
                act.wait_ge(S["sums"], 1)
                for dst, b, scale in ((e1, 1, 1.0), (en, 1, -1.0), (eb, 2, 1.0), (et, 3, 1.0)):
                    act.activation(dst[:, :], C.bank[b][:, 0:SEQ], ACT.Exp, scale=scale).then_inc(S["exps"], 1)
                act.wait_ge(S["o"], 1)
                act.activation(out[:, :, :].rearrange("p a t -> p (a t)"), C.bank[0][:, :], ACT.Copy).then_inc(S["out"], 1)

            @block.vector
            def _(dve):
                L = lambda ins: S.link(dve, ins, "vector")
                flat = lambda a: a[:, :, :].rearrange("p t c -> p (t c)")
                L(dve.memset(st[:, 0, :], 0.0))
                dve.wait_ge(S["loaded"], 48)
                dve.wait_ge(S["softplus"], 1)
                dve.scalar_tensor_tensor(out=flat(la), in0=C.bank[0][:, 0:SEQ], scalar=0.0, in1=flat(lt),
                                         op0=ALU.min, op1=ALU.subtract).then_inc(S["log_a"], 1)
                dve.wait_ge(S["exps"], 4)
                L(dve.tensor_copy(lt[:, 0, 0:NCH], eb[:, CH - 1:SEQ:CH]))
                L(dve.tensor_tensor(en[:, :], en[:, :], Z["gk"][:, :], ALU.mult))
                L(dve.scalar_tensor_tensor(out=e1[:, :], in0=e1[:, :], scalar=dk ** -0.5, in1=Z["gq"][:, :],
                                           op0=ALU.mult, op1=ALU.mult))
                L(dve.scalar_tensor_tensor(out=eb[:, :], in0=eb[:, :], scalar=dk ** -0.5, in1=Z["gq"][:, :],
                                           op0=ALU.mult, op1=ALU.mult))
                L(dve.tensor_tensor(et[:, :], et[:, :], Z["gkt"][:, :, :].rearrange("p t c -> p (t c)"), ALU.mult))
                for h in range(H4):
                    dve.tensor_scalar(k1[:, h, :], en[:, :], hm[:, h:h + 1], None, ALU.mult).then_inc(S["k1"], 1)
                dve.wait_ge(S["pairs"], 1)
                for t in range(TT):
                    dve.tensor_tensor(att[:, t, :, :], C.bank[4 + t][:, :].rearrange("p (h c) -> p h c", h=H4),
                                      C.sq["m_fwd_in"].unsqueeze(1).broadcast_to([P, H4, P]), ALU.mult)\
                       .then_inc(S["att"], 1)
                S.link(dve, dve.tensor_copy(st[:, 0, :], st[:, 0, :]), "state")
                for c in range(NCH - 1):
                    dve.wait_ge(S["outer"], c + 1)
                    S.link(dve, dve.tensor_tensor(up[:, :], C.bank[6 + c % 2][:, 0:MIX], bd[:, :], ALU.mult), "update")
                    S.link(dve, dve.scalar_tensor_tensor(out=st[:, c + 1, :], in0=st[:, c, :], scalar=lt[:, 0, c:c + 1],
                                                         in1=up[:, :], op0=ALU.mult, op1=ALU.add), "state")
        S.close()


def times(C, name, rows):
    S = Stage(C.nc, name)
    with C.nc.Block() as block:
        @block.vector
        def _(dve):
            for a, b in rows:
                S.link(dve, dve.tensor_tensor(a, a, b, ALU.mult), "product")
    S.close()


def peer_search(C, A, l_, qv, x1, xtok, gate, index, offset):
    nc = C.nc
    S = Stage(nc, "search")
    U = TT * PH
    U2 = 2 * U
    with ExitStack() as local:
        sb = lambda name, shape, dt=F32: local.enter_context(nc.sbuf_tensor(name, shape, dt))
        keys = sb("peer_keys", [P, 2 * PH, KEYS])
        s = sb("peer_s", [P, U2, KEYS])
        top = sb("peer_top", [P, U2, TOPK])
        ti = sb("peer_ti", [P, U2, TOPK], U32)
        tf = sb("peer_tf", [P, U2, TOPK])
        cand = sb("peer_cand", [P, U, TOPK * TOPK])
        bi = sb("peer_bi", [P, U, TOPK], U32)
        part = sb("peer_part", [P, 2, U * TOPK], U32)
        pf = sb("peer_pf", [P, 2, U * TOPK])
        iota = sb("peer_iota", [P, TOPK])
        den = sb("peer_den", [P, U])
        with nc.Block() as block:
            @block.sync
            def _(sp):
                sp.dma_start(keys[:, :, :], A["peer_keys"][l_, :, :, :]).then_inc(S["keys"], 16)

            @block.gpsimd
            def _(pool):
                pool.iota(iota[:, :], pattern=[[1, TOPK]], base=0, channel_multiplier=0,
                          allow_small_or_imprecise_dtypes=True).then_inc(S["iota"], 1)

            @block.tensor
            def _(pe):
                for t in range(TT):
                    for k in range(KT):
                        ins = pe.transpose(C.bank[4 + 2 * t + k // 4][:, (k % 4) * P:(k % 4) * P + P],
                                           x1[:, k, t * P:(t + 1) * P], C.sq["ident"])
                ins.then_inc(S["x_turned"], 1)
                pe.wait_ge(S["keys"], 16)
                for g in range(U2 // 4):
                    if g >= 4:
                        pe.wait_ge(S["scores_out"], g - 3)
                    for i in range(4):
                        u = 4 * g + i
                        t, hp = u // (2 * PH), u % (2 * PH)
                        ins = pe.matmul(C.bank[g % 4][:, i * P:(i + 1) * P], qv[:, hp, t * P:(t + 1) * P],
                                        keys[:, hp, :], start=True, stop=True)
                    ins.then_inc(S["scores"], 1)

            @block.scalar
            def _(act):
                for g in range(U2 // 4):
                    act.wait_ge(S["scores"], g + 1)
                    act.activation(s[:, 4 * g:4 * g + 4, :].rearrange("p a c -> p (a c)"), C.bank[g % 4][:, :], ACT.Copy)\
                       .then_inc(S["scores_out"], 1)
                act.wait_ge(S["x_turned"], 1)
                for i in range(4):
                    act.activation(xtok[:, i // 2, (i % 2) * 512:(i % 2) * 512 + 512], C.bank[4 + i][:, :], ACT.Copy)\
                       .then_inc(S["x_out"], 1)
                act.wait_ge(S["relative"], 1)
                act.activation(gate[:, :, :], gate[:, :, :], ACT.Exp).then_inc(S["exp"], 1)

            @block.vector
            def _(dve):
                L = lambda ins: S.link(dve, ins, "vector")

                def best(n, score, value, where):
                    base = S.count.get("best", 0)
                    for step in range(5):
                        for u in range(n):
                            a, b = slice(0, 8), slice(8, 16)
                            if step:
                                dve.wait_ge(S["best"], base + (step - 1) * n + u + 1)
                            if step == 0:
                                ins = dve.max(value(u)[:, a], score(u))
                            elif step == 1:
                                ins = dve.max_index(where(u)[:, a], value(u)[:, a], score(u))
                            elif step == 2:
                                ins = dve.match_replace(score(u), value(u)[:, a], score(u), NEG)
                            elif step == 3:
                                ins = dve.max(value(u)[:, b], score(u))
                            else:
                                ins = dve.max_index(where(u)[:, b], value(u)[:, b], score(u))
                            ins.then_inc(S["best"], 1)
                    S.count["best"] = base + 5 * n
                    dve.wait_ge(S["best"], base + 5 * n)

                dve.wait_ge(S["scores_out"], U2 // 4)
                best(U2, lambda u: s[:, u, :], lambda u: top[:, u, :], lambda u: ti[:, u, :])
                L(dve.tensor_copy(tf[:, :, :], ti[:, :, :]))
                half = lambda a, p: a[:, :, :].rearrange("p (u q) k -> p u q k", q=2)[:, :, p, :]
                big = [P, U, TOPK, TOPK]
                c4 = cand[:, :, :].rearrange("p u (a b) -> p u a b", a=TOPK)
                L(dve.tensor_tensor(c4, half(top, 0).unsqueeze(3).broadcast_to(big),
                                    half(top, 1).unsqueeze(2).broadcast_to(big), ALU.add))
                best(U, lambda u: cand[:, u, :], lambda u: gate[:, u, :], lambda u: bi[:, u, :])
                flat = bi[:, :, :].rearrange("p u k -> p (u k)")
                L(dve.tensor_scalar(part[:, 0, :], flat, 4, None, ALU.logical_shift_right))
                L(dve.tensor_scalar(part[:, 1, :], flat, 15, None, ALU.bitwise_and))
                L(dve.tensor_copy(pf[:, :, :], part[:, :, :]))
                dve.wait_ge(S["iota"], 1)
                wide = [P, U * TOPK, TOPK]
                eq = cand[:, :, :].rearrange("p u (a b) -> p (u a) b", a=TOPK)
                for q in range(2):
                    L(dve.tensor_tensor(eq, pf[:, q, :].unsqueeze(2).broadcast_to(wide),
                                        iota[:, :].unsqueeze(1).broadcast_to(wide), ALU.is_equal))
                    L(dve.tensor_tensor(c4, c4, half(tf, q).unsqueeze(2).broadcast_to(big), ALU.mult))
                    L(dve.tensor_reduce(pf[:, q, :], eq, AX, ALU.add))
                L(dve.scalar_tensor_tensor(out=pf[:, 0, :], in0=pf[:, 0, :], scalar=float(KEYS), in1=pf[:, 1, :],
                                           op0=ALU.mult, op1=ALU.add))
                L(dve.tensor_scalar(pf[:, 0, :], pf[:, 0, :], offset, None, ALU.add))
                L(dve.tensor_copy(index[:, :, :].rearrange("p u k -> p (u k)"), pf[:, 0, :]))
                L(dve.tensor_copy(den[:, :], gate[:, :, 0]))
                w3 = [P, U, TOPK]
                dve.tensor_tensor(gate[:, :, :], gate[:, :, :], den[:, :].unsqueeze(2).broadcast_to(w3), ALU.subtract)\
                   .then_inc(S["relative"], 1)
                dve.wait_ge(S["exp"], 1)
                L(dve.tensor_reduce(den[:, :], gate[:, :, :], AX, ALU.add))
                L(dve.reciprocal(den[:, :], den[:, :]))
                L(dve.tensor_tensor(gate[:, :, :], gate[:, :, :], den[:, :].unsqueeze(2).broadcast_to(w3), ALU.mult))
        S.close()


def peer_experts(C, A, xtok, gate, index, x1):
    nc = C.nc
    NG = GATHERED
    with ExitStack() as local:
        sb = lambda name, shape, dt=F32: local.enter_context(nc.sbuf_tensor(name, shape, dt))
        ub = sb("u_rows", [P, NG, D])
        vb = sb("v_rows", [P, NG, D])
        junk = sb("u_junk", [P, D])
        y = sb("peer_y", [P, TT, D])
        acts = sb("peer_act", [P, 2, TOPK])
        wts = sb("peer_wts", [P, TOPK])
        gi = sb("peer_gi", [P, 2, TOPK], U32)
        idle = sb("gather_idle", [1, 1 + 2 * TOPK])
        S = Stage(nc, "gather")
        PER = TOPK // NG
        with nc.Block() as block:
            @block.gpsimd
            def _(pool):
                def gather(name, table, rows, done, g, i, k, first):
                    slot = k % NG
                    if not (first and k < NG):
                        pool.wait_ge(S[done], TOPK * g + (k - NG + 1))
                        cell = 1 + k + (TOPK if name == "v" else 0)
                        pool.tensor_tensor(idle[:, cell:cell + 1], idle[:, 0:1], idle[:, 0:1], ALU.mult)
                    pool.indirect_dma_start(
                        out=rows[:, slot, :], out_offset=None, in_=table,
                        in_offset=bass.IndirectOffsetOnAxis(ap=gi[:, i, k:k + 1], axis=0))\
                        .then_inc(S[f"{name}{slot}"], 16)

                def head(g, i, first):
                    pool.tensor_copy(gi[:, i, :], index[:, g, :]).then_inc(S["index"], 1)
                    pool.wait_ge(S["index"], g + 1)
                    for k in range(TOPK):
                        gather("u", A["peer_u"], ub, "dots", g, i, k, first)
                    for k in range(TOPK):
                        gather("v", A["peer_v"], vb, "sums", g, i, k, first)

                S.link(pool, pool.memset(idle[:, :], 0.0), "idle")
                head(0, 0, True)
                head(1, 1, False)
                with pool.Fori(1, TT * PH // 2) as m:
                    head(2 * m, 0, False)
                    head(2 * m + 1, 1, False)

            @block.scalar
            def _(act):
                with act.Fori(0, TT * PH) as g:
                    act.wait_ge(S["dots"], TOPK * g + TOPK)
                    act.activation(acts[:, 1, :], acts[:, 0, :], ACT.Gelu).then_inc(S["gelu"], 1)

            @block.vector
            def _(dve):
                S.link(dve, dve.memset(y[:, :, :], 0.0), "zero")
                for t in range(TT):
                    with dve.Fori(t * PH, (t + 1) * PH) as g:
                        for k in range(TOPK):
                            dve.wait_ge(S[f"u{k % NG}"], PER * 16 * g + 16 * (k // NG + 1))
                            if k:
                                dve.wait_ge(S["dots"], TOPK * g + k)
                            dve.tensor_tensor_reduce(junk[:, :], ub[:, k % NG, :], xtok[:, t, :], 1.0, 0.0, ALU.mult,
                                                     ALU.add, acts[:, 0, k:k + 1]).then_inc(S["dots"], 1)
                        dve.wait_ge(S["gelu"], g + 1)
                        dve.tensor_tensor(wts[:, :], acts[:, 1, :], gate[:, g, :], ALU.mult).then_inc(S["weights"], 1)
                        dve.wait_ge(S["weights"], g + 1)
                        for k in range(TOPK):
                            dve.wait_ge(S[f"v{k % NG}"], PER * 16 * g + 16 * (k // NG + 1))
                            if k:
                                dve.wait_ge(S["sums"], TOPK * g + k)
                            dve.scalar_tensor_tensor(out=y[:, t, :], in0=vb[:, k % NG, :], scalar=wts[:, k:k + 1],
                                                     in1=y[:, t, :], op0=ALU.mult, op1=ALU.add).then_inc(S["sums"], 1)
        S.close()
        S = Stage(nc, "peer_out")
        with nc.Block() as block:
            @block.tensor
            def _(pe):
                for k in range(KT):
                    for t in range(TT):
                        ins = pe.transpose(C.bank[k // 2][:, (k % 2) * SEQ + t * P:(k % 2) * SEQ + (t + 1) * P],
                                           y[:, t, k * P:(k + 1) * P], C.sq["ident"])
                ins.then_inc(S["turned"], 1)

            @block.vector
            def _(dve):
                dve.wait_ge(S["turned"], 1)
                for i in range(4):
                    c = slice(2 * i, 2 * i + 2)
                    S.link(dve, dve.scalar_tensor_tensor(out=x1[:, c, :], in0=x1[:, c, :], scalar=DN_ALPHA,
                                                         in1=C.bank[i][:, :].rearrange("p (a c) -> p a c", a=2),
                                                         op0=ALU.mult, op1=ALU.add), "x")
        S.close()


def layer(C, A, l_, xT):
    nc = C.nc
    with ExitStack() as outer:
        so = lambda name, shape: outer.enter_context(nc.sbuf_tensor(name, shape, F32))
        v2 = so("vec2", [P, VEC2_COLS])
        x1 = so("x1", [P, KT, SEQ])
        V = {name: v2[:, at:at + n] for name, (at, n) in VEC2_AT.items()}
        load_all(nc, "vec2", [(v2[:, :], A["vec2"][l_, :, :])])
        with ExitStack() as mid:
            sm = lambda name, shape: mid.enter_context(nc.sbuf_tensor(name, shape, F32))
            mg = sm("z_mg", [P, 4 * KT, SEQ])
            o = sm("z_o", [P, 8, SEQ])
            branch = [o[:, 2 * i:2 * i + 2, :] for i in range(4)]
            with ExitStack() as local:
                sl = lambda name, shape: local.enter_context(nc.sbuf_tensor(name, shape, F32))
                Z = {n: sl("z2_" + n, [P, 2, SEQ]) for n in ("sq", "sk", "sv", "rq", "rk", "rv", "rg", "gv", "gr")}
                Z["nq"], Z["kcv"], Z["nk"] = sl("z2_nq", [HD, 4, SEQ]), sl("z2_kcv", [HD, 2, SEQ]), sl("z2_nk", [HD, 2, SEQ])
                Z["nv"], Z["ng"], Z["lr"] = sl("z2_nv", [P, 2, P]), sl("z2_ng", [P, 2, 12]), sl("z2_lr", [32, SEQ])
                Z["gq"], Z["gk"], Z["gkt"] = sl("z2_gq", [P, SEQ]), sl("z2_gk", [P, SEQ]), sl("z2_gkt", [P, 2, P])
                S = Stage(nc, "lr_ones")
                with nc.Block() as block:
                    @block.vector
                    def _(dve):
                        S.link(dve, dve.memset(Z["lr"][:, :], 1.0), "ones")
                S.close()
                hv = local.enter_context(ExitStack())
                xh = hv.enter_context(nc.sbuf_tensor("x_halves", [P, 2, KT, SEQ], F32R))
                xs = (xh[:, 0, :, :], xh[:, 1, :, :])
                split(C, "split_x", [(xT[:, :, :], *xs)])
                jobs = []

                def turned(tile, dst, func=None, width=P, at=0):
                    for i, d in enumerate(dst):
                        acts = xs if width == P else xT
                        jobs.append((tile, at + i * width, width, True, acts, 0, SEQ, d, func, None))

                def straight(tile, dst, width, at=0, func=None):
                    for t in range(TT):
                        jobs.append((tile, at, width, False, xs, t * P, P, dst[:, t, 0:width], func, None))

                two = lambda a: [a[:, 0, :], a[:, 1, :]]
                turned(0, two(Z["sq"]))
                turned(1, two(Z["sk"]))
                straight(2, Z["sv"], 256)
                turned(3, [Z["nq"][:, i, :] for i in range(4)], width=HD)
                turned(4, two(Z["kcv"]) + two(Z["nk"]), width=HD)
                straight(5, Z["nv"], 128)
                straight(5, Z["ng"], 12, 128, ACT.Sigmoid)
                turned(5, [Z["lr"][0:16, :]], width=16, at=140)
                turned(6, two(Z["rq"]))
                turned(7, two(Z["rk"]))
                straight(8, Z["rv"], 256)
                turned(9, two(Z["rg"]), ACT.Silu)
                turned(10, [Z["gq"][:, :], Z["gk"][:, :]])
                straight(10, Z["gkt"], 128, 128)
                straight(11, Z["gv"], 256)
                turned(12, two(Z["gr"]), ACT.Silu)
                for i in range(16):
                    turned(13 + i, [mg[:, 2 * i, :], mg[:, 2 * i + 1, :]], ACT.Sigmoid)
                linear(C, "w_in2", [A["w_in2"][l_ * TILES2 + i, :, :] for i in range(TILES2)], jobs)
                hv.close()
                stick_breaking(C, A, Z, branch[0])
                nsa(C, A, l_, Z, branch[1])
                retention(C, A, Z, branch[2])
                head_norm(C, "ret_norm", branch[2], branch[2], 2, V["gn_g"], V["gn_b"], True, nt=2)
                gla(C, A, l_, Z, branch[3])
                head_norm(C, "gla_norm", branch[3], branch[3], 2, V["gla_g"], None, False, nt=2)
                times(C, "out_gates", [(branch[2], Z["rg"][:, :, :]), (branch[3], Z["gr"][:, :, :])])
            with ExitStack() as local:
                pr = local.enter_context(nc.sbuf_tensor("pr", [P, 4 * KT, SEQ], F32))
                os = local.enter_context(nc.sbuf_tensor("o_halves", [P, 2, KT, SEQ], F32R))
                split(C, "split_o", [(o[:, :, :], os[:, 0, :, :], os[:, 1, :, :])])
                jobs = [(i, m * P, P, True, tuple(os[:, q, 2 * i:2 * i + 2, :] for q in range(2)), 0, SEQ,
                         pr[:, i * KT + m, :], None, mg[:, i * KT + m, :]) for i in range(4) for m in range(KT)]

                def merge(S, dve):
                    for n, (a, b) in enumerate(((0, 2), (1, 3), (0, 1))):
                        ra, rb = slice(a * KT, (a + 1) * KT), slice(b * KT, (b + 1) * KT)
                        S.link(dve, dve.tensor_tensor(pr[:, ra, :], pr[:, ra, :], pr[:, rb, :], ALU.add), "merged")

                linear(C, "w_branch", [A["w_branch"][l_ * 4 + i, :, :] for i in range(4)], jobs, kt=2, extra=merge)
                split(C, "split_pr", [(pr[:, 0:KT, :], os[:, 0, :, :], os[:, 1, :, :])])
                jobs = [(m // 2, P * (m % 2), P, True, (os[:, 0, :, :], os[:, 1, :, :]), 0, SEQ, x1[:, m, :], None,
                         None) for m in range(KT)]

                def residual(S, dve):
                    S.link(dve, dve.scalar_tensor_tensor(out=x1[:, :, :], in0=xT[:, :, :], scalar=DN_ALPHA,
                                                         in1=x1[:, :, :], op0=ALU.mult, op1=ALU.add), "x")
                linear(C, "w_out2", [A["w_out2"][l_ * 4 + i, :, :] for i in range(4)], jobs, extra=residual)
        norm(C, "ln1", [(x1[:, :, :], x1[:, :, :], V["ln1_g"], V["ln1_b"], SEQ)], 2, centred=True)
        with ExitStack() as mid:
            sm = lambda name, shape, dt=F32: mid.enter_context(nc.sbuf_tensor(name, shape, dt))
            xtok = sm("xtok", [P, TT, D])
            gate = sm("peer_gate", [P, TT * PH, TOPK])
            index = sm("peer_index", [P, TT * PH, TOPK], U32)
            with ExitStack() as local:
                qv = local.enter_context(nc.sbuf_tensor("peer_q", [P, 2 * PH, SEQ], F32))
                hv = local.enter_context(ExitStack())
                xh = hv.enter_context(nc.sbuf_tensor("x1_halves", [P, 2, KT, SEQ], F32R))
                xs = (xh[:, 0, :, :], xh[:, 1, :, :])
                split(C, "split_x1", [(x1[:, :, :], *xs)])
                jobs = [(m // 2, P * (m % 2), P, True, xs, 0, SEQ, qv[:, m, :], None, None) for m in range(2 * PH)]
                linear(C, "peer_wq", [A["peer_wq"][l_ * 8 + i, :, :] for i in range(8)], jobs)
                hv.close()
                peer_search(C, A, l_, qv, x1, xtok, gate, index, V["offset"])
            peer_experts(C, A, xtok, gate, index, x1)
        norm(C, "ln2", [(x1[:, :, :], xT[:, :, :], V["ln2_g"], V["ln2_b"], SEQ)], 2, centred=True)


def second_block(C, A, xT):
    norm(C, "ln_in", [(xT[:, :, :], xT[:, :, :], C.v["lnin_g"], C.v["lnin_b"], SEQ)], 2, centred=True)
    with C.nc.Fori(0, 2) as l_:
        layer(C, A, l_, xT)


VEC2 = [("gn_g", 2), ("gn_b", 2), ("gla_g", 2), ("ln1_g", 8), ("ln1_b", 8), ("ln2_g", 8), ("ln2_b", 8), ("offset", 1)]
VEC2_AT, VEC2_COLS = {}, 0
for _name, _n in VEC2:
    VEC2_AT[_name] = (VEC2_COLS, _n)
    VEC2_COLS += _n


def build(nc, A, out):
    with ExitStack() as ctx:
        C = Core(nc, ctx)
        square = C.keep("square", [P, len(SQUARE), P])
        C.sq = {k: square[:, i, :] for i, k in enumerate(SQUARE)}
        epst = C.keep("eps", [P, len(EPS)])
        C.eps = [epst[:, i:i + 1] for i in range(len(EPS))]
        C.mask4 = C.keep("mask4", [P, 2, 4 * P])
        vec = C.keep("vec", [P, VEC_COLS])
        C.v = {}
        for name, (at, n) in VEC_AT.items():
            C.v[name] = vec[:, at:at + n]
        xT = C.keep("xT", [P, KT, SEQ])
        load_all(nc, "start", [(square[:, :, :], A["square"]), (epst[:, :], A["eps"]),
                               (C.mask4[:, :, :], A["mask4"]), (vec[:, :], A["vec"]), (xT[:, :, :], A["xT"])])
        S = Stage(nc, "one_minus")
        with nc.Block() as block:
            @block.vector
            def _(dve):
                S.link(dve, dve.tensor_scalar(C.v["one_minus_k_a"], C.v["k_a"], -1.0, 1.0, ALU.mult, ALU.add), "k_a")
        S.close()
        first_block(C, A, xT)
        second_block(C, A, xT)
        S = Stage(nc, "end")
        with nc.Block() as block:
            @block.sync
            def _(sp):
                sp.dma_start(out, xT[:, :, :]).then_inc(S["out"], 16)
                sp.wait_ge(S["out"], 16)
        S.close()


VEC = [("norm1_g", 8), ("norm2_g", 8), ("k_k", 4), ("k_a", 4), ("one_minus_k_a", 4), ("a0", 8), ("r_k", 4),
       ("ln_g", 4), ("ln_b", 4), ("q_g", 4), ("k_g", 4), ("lnin_g", 8), ("lnin_b", 8)]
VEC_AT, VEC_COLS = {}, 0
for _name, _n in VEC:
    VEC_AT[_name] = (VEC_COLS, _n)
    VEC_COLS += _n


def columns(a):
    return np.asarray(a).reshape(-1, P).T


def tiled(w, cols):
    K, N = w.shape
    return np.ascontiguousarray(w.reshape(K // P, P, N // cols, cols).transpose(2, 1, 0, 3)
                                .reshape(N // cols, P, K // P * cols))


def turn(x):
    return np.ascontiguousarray(x.T.reshape(-1, P, x.shape[0]).transpose(1, 0, 2))


def window_bias(rpb):
    W, rows = 64, SEQ // 64
    q, k = np.arange(SEQ)[:, None], np.arange(SEQ)[None, :]
    drow = k // W - q // W + 7
    dcol = np.clip(k % W - q % W, -15, 15) + 15
    return np.ascontiguousarray(rpb[:, drow, dcol].reshape(NH, TT, P, SEQ))


def window_mask():
    j = np.arange(64)
    start = np.clip(j - 8, 0, 64 - 16)
    inside = (j[None, :] >= start[:, None]) & (j[None, :] < start[:, None] + 16)
    m = np.where(inside, 0.0, NEG).astype(np.float32)
    return np.ascontiguousarray(np.tile(m, (4, 4)).reshape(TT, P, SEQ).transpose(1, 0, 2))


def lay_out(I):
    f = {k: np.asarray(v) for k, v in I.items()}
    A = {}
    A["square"], A["eps"] = square_array(), eps_array()
    c = constants_square()
    A["mask4"] = np.ascontiguousarray(np.stack(
        [np.concatenate([c["m_" + s + "_ex"], c["m_" + s + "_in"]] * 2, 1) for s in SIDES], 1))
    vec = {"norm1_g": f["norm1_g"][0], "norm2_g": f["norm2_g"][0], "k_k": f["rw_k_k"][0], "k_a": f["rw_k_a"][0],
           "a0": f["rw_a0"][0].reshape(-1), "r_k": f["rw_r_k"][0].reshape(-1), "ln_g": f["rw_ln_g"][0],
           "ln_b": f["rw_ln_b"][0], "q_g": np.tile(f["na_q_g"][0], NH), "k_g": np.tile(f["na_k_g"][0], NH),
           "lnin_g": f["ln_in_g_2"], "lnin_b": f["ln_in_b_2"]}
    v = np.zeros((P, VEC_COLS), np.float32)
    for name, (at, n) in VEC_AT.items():
        if name in vec:
            v[:, at:at + n] = columns(vec[name])
    A["vec"] = v
    A["xT"], A["ctxT"] = turn(f["x"][0]), turn(f["ctx"][0])
    A["cond"] = np.ascontiguousarray(np.stack([columns(f["c"][0]), columns(f["c_ctx"])], 2))
    A["mod_b"] = np.ascontiguousarray(columns(f["mod_b"][0]))
    A["mod_w"] = tiled(f["mod_w"][0], 256)
    w = f["w_in"][0]
    A["w_in"] = tiled(np.concatenate([w[:, :1920], np.zeros((D, 128), np.float32), w[:, 1920:]], 1), 256)
    A["rw_w_lora_b"] = np.ascontiguousarray(f["rw_w_lora_b"][0].reshape(P, -1))
    A["rw_a_lora_b"] = np.ascontiguousarray(f["rw_a_lora_b"][0].reshape(P, -1))
    w0 = np.zeros((P, NH * HD), np.float32)
    w0[0], w0[64] = f["rw_w0"][0, 0], f["rw_w0"][0, 1]
    A["rw_w0"] = w0
    A["rw_g_lora_b"] = np.ascontiguousarray(f["rw_g_lora_b"][0])
    A["na_bias"], A["na_mask"] = window_bias(f["na_rpb"][0]), window_mask()
    A["proj_ab"] = np.concatenate([tiled(f["proj_a"][0], 512), tiled(f["proj_b"][0], 512)], 0)
    A["w_out"] = tiled(f["w_out"][0], 256)
    A["router_w"] = np.ascontiguousarray(f["router_w"].reshape(KT, P, N_EXP).transpose(1, 0, 2))
    A["router_bias"] = np.ascontiguousarray(np.tile(f["router_bias"][None], (P, 1)))
    A["pick"] = np.ascontiguousarray(np.repeat(np.eye(N_EXP, dtype=np.float32)[:, :, None], P, 2))
    moe = []
    for e in range(N_EXP + 1):
        if e < N_EXP:
            w1, w3 = f["moe_w1"][0, e].reshape(D, 4, P), f["moe_w3"][0, e].reshape(D, 4, P)
            up = tiled(np.concatenate([w1, w3], 2).reshape(D, 8 * P), 256)
            moe.append(up[0:1])
        if e:
            moe.append(tiled(f["moe_w2"][0, e - 1], 512))
        if e < N_EXP:
            moe.append(up[1:4])
    A["moe"] = np.concatenate(moe, 0)
    L = 2
    s, t = np.arange(SEQ)[:, None], np.arange(SEQ)[None, :]
    halves = lambda a: np.ascontiguousarray(a.reshape(TT, P, SEQ).transpose(1, 0, 2).reshape(P, TT * SEQ))
    A["causal"] = halves((s < t).astype(np.float32))
    slopes = 2.0 ** (-8.0 * np.arange(1, H4 + 1) / H4)
    tok = np.arange(SEQ)[:, None]
    end = np.arange(N_CMP)[None, :] * 16 + 31
    cb = np.where(tok >= end, -slopes[:, None, None] * (tok - end), NEG)
    A["cmp_bias"] = np.ascontiguousarray(cb.reshape(H4, TT, P, N_CMP).transpose(2, 1, 0, 3)
                                         .reshape(P, TT * H4, N_CMP).astype(np.float32))
    A["cmp_seen"] = np.ascontiguousarray((np.arange(SEQ) >= 31).astype(np.float32).reshape(TT, P).T)
    lb = np.where(t <= s, -slopes[:, None, None] * (s - t), NEG)
    A["lin_bias"] = np.ascontiguousarray(lb.reshape(H4, TT, P, SEQ).transpose(2, 1, 0, 3)
                                         .reshape(P, TT * H4, SEQ).astype(np.float32))
    log_g = np.log1p(-(2.0 ** (-5.0 - np.arange(H4))))
    dec = np.where(s <= t, np.exp(log_g[:, None, None] * np.maximum(t - s, 0)), 0.0) * HD ** -0.5
    A["ret_decay"] = np.ascontiguousarray(np.stack([halves(d.astype(np.float32)) for d in dec], 1))
    A["gla_heads"] = (np.arange(P)[:, None] // 32 == np.arange(H4)[None, :]).astype(np.float32)
    A["gla_blocks"] = (np.arange(P)[:, None] // 32 == np.arange(MIX)[None, :] // HD).astype(np.float32)
    w = f["w_in_2"]
    cols = lambda a, n: w[:, :, a:a + n]
    w = np.concatenate([cols(0, 1024), cols(1024, 128), cols(1152, 64), cols(1280, 64), cols(1216, 64), cols(1344, 64),
                        cols(1408, 12), cols(3212, 16), np.zeros((L, D, 100), np.float32), cols(1420, 1792),
                        cols(3228, 4096)], 2)
    A["w_in2"] = np.concatenate([tiled(w[i], 256) for i in range(L)], 0)
    cw = np.stack([f["nsa_cmp_wk_2"], f["nsa_cmp_wv_2"]], 1).reshape(L, 2, 32, HD, HD)
    A["cmp_w"] = np.ascontiguousarray(cw.transpose(0, 3, 1, 2, 4))
    A["cmp_pos"] = np.ascontiguousarray(f["nsa_cmp_pos_2"].transpose(0, 2, 1))
    A["gla_wa"] = np.concatenate([f["gla_w_alpha_2"], f["gla_b_alpha_2"][:, None, :]], 1)
    A["w_branch"] = np.concatenate([tiled(f["w_branch_2"][i, j], 1024) for i in range(L) for j in range(4)], 0)
    A["w_out2"] = np.concatenate([tiled(f["w_out_2"][i], 256) for i in range(L)], 0)
    A["peer_wq"] = np.concatenate([tiled(f["peer_wq_2"][i], 256) for i in range(L)], 0)
    A["peer_keys"] = np.ascontiguousarray(f["peer_keys_2"].reshape(L, 2 * PH, KEYS, P).transpose(0, 3, 1, 2))
    A["peer_u"] = f["peer_u_2"].reshape(-1, D)
    A["peer_v"] = f["peer_v_2"].reshape(-1, D)
    vec2 = {"gn_g": "ret_gn_g_2", "gn_b": "ret_gn_b_2", "gla_g": "gla_norm_g_2", "ln1_g": "ln1_g_2",
            "ln1_b": "ln1_b_2", "ln2_g": "ln2_g_2", "ln2_b": "ln2_b_2"}
    v = np.zeros((L, P, VEC2_COLS), np.float32)
    for i in range(L):
        for name, (at, n) in VEC2_AT.items():
            v[i, :, at:at + n] = i * KEYS * KEYS if name == "offset" else columns(f[vec2[name]][i])
    A["vec2"] = v
    return A


def kernel(**inputs):
    import concourse.bacc as bacc
    from concourse.bass_utils import run_bass_kernel_spmd

    nc = bacc.Bacc("TRN2", target_bir_lowering=False, num_devices=1)
    arrays, A = {}, {}
    for name, a in lay_out(inputs).items():
        arrays[f"in_{name}"] = a
        A[name] = nc.dram_tensor(f"in_{name}", a.shape, mybir.dt.from_np(a.dtype), kind="ExternalInput").ap()
    out = nc.dram_tensor("out_xT", (P, KT, SEQ), F32, kind="ExternalOutput").ap()
    build(nc, A, out)
    r = run_bass_kernel_spmd(nc, [arrays], core_ids=[0])
    y = np.asarray(r.results[0]["out_xT"])
    return np.ascontiguousarray(y.transpose(2, 1, 0).reshape(1, SEQ, D))
```

```python
from contextlib import ExitStack

import numpy as np

import concourse.bass as bass
from concourse import mybir

F32 = mybir.dt.float32
F32R = mybir.dt.float32r
U32 = mybir.dt.uint32
I32 = mybir.dt.int32
ALU = mybir.AluOpType
ACT = mybir.ActivationFunctionType
AX = mybir.AxisListType.X

P = 128
D = 1024
KT = D // P
SEQ = 256
CTX = 256
ALL = CTX + SEQ
TT = SEQ // P
TILE = 2048
RING = 6
COLUMNS = (slice(0, TILE // 2), slice(TILE // 2, TILE))
NH = 8
HD = 64
PAIRS = NH // 2
CH = 64
RMS_EPS = 1e-6
GN_EPS = 64e-5
LN_EPS = 1e-5
N_EXP = 16
D_EXP = 512
DECAY = float(np.exp(-0.5))
NEG = -1e30


class Stage:

    def __init__(self, nc, name):
        self.nc, self.name, self.sems, self.count = nc, name, {}, {}

    def __getitem__(self, what):
        if what not in self.sems:
            self.sems[what] = self.nc.alloc_semaphore(f"{self.name}_{what}")
            self.count[what] = 0
        return self.sems[what]

    def wait(self, eng, what, n):
        if n > 0:
            eng.wait_ge(self[what], n)

    def link(self, eng, ins, what):
        ins.then_inc(self[what], 1)
        self.count[what] += 1
        eng.wait_ge(self[what], self.count[what])

    def close(self):
        self.nc.clear_and_free_semaphores(list(self.sems.values()))
        self.nc.all_engine_barrier()


class Core:

    def __init__(self, nc, ctx):
        self.nc, self.ctx = nc, ctx
        self.bank = [ctx.enter_context(nc.psum_tensor(f"bank{i}", [P, 512], F32)) for i in range(8)]
        self.ring = ctx.enter_context(nc.sbuf_tensor("ring", [P, RING, TILE], F32))

    def keep(self, name, shape, dt=F32):
        return self.ctx.enter_context(self.nc.sbuf_tensor(name, shape, dt))


def constants_square():
    i, j = np.arange(P)[:, None], np.arange(P)[None, :]
    same = (i // CH) == (j // CH)
    out = {}
    out["ident"] = (i == j)
    out["ones"] = np.ones((P, P))
    out["head_ones"] = same
    out["fwd_in"] = -DECAY * (same & (i <= j))
    out["fwd_ex"] = -DECAY * (same & (i < j))
    out["bwd_in"] = -DECAY * (same & (i >= j))
    out["bwd_ex"] = -DECAY * (same & (i > j))
    out["m_fwd_ex"] = same & (i < j)
    out["m_fwd_in"] = same & (i <= j)
    out["m_bwd_ex"] = same & (i > j)
    out["m_bwd_in"] = same & (i >= j)
    out["lt"] = i < j
    out["neg_ge"] = -1.0 * (i >= j)
    out["neg_ones"] = -np.ones((P, P))
    mid = same & ((i % CH) <= CH // 2 - 1)
    tau = 16.0
    out["gla_in"] = (same & (i <= j)) / tau
    out["gla_mid"] = ((same & (i <= j)) * 1.0 - mid) / tau
    out["gla_tail"] = (same & (i > j)) / tau
    return {k: v.astype(np.float32) for k, v in out.items()}


SQUARE = list(constants_square())
EPS = [RMS_EPS, GN_EPS, LN_EPS, 1.0]


def square_array():
    c = constants_square()
    return np.ascontiguousarray(np.stack([c[k] for k in SQUARE], 1))


def eps_array():
    return np.ascontiguousarray(np.tile(np.array(EPS, np.float32)[None], (P, 1)))


def load_all(nc, name, pairs):
    S = Stage(nc, name)
    with nc.Block() as block:
        @block.sync
        def _(sp):
            for dst, src in pairs:
                sp.dma_start(dst, src).then_inc(S["loaded"], 16)
            sp.wait_ge(S["loaded"], 16 * len(pairs))
    S.close()


def product(pe, out, terms):
    for n, (lhsT, rhs) in enumerate(terms):
        ins = pe.matmul(out, lhsT, rhs, start=(n == 0), stop=(n == len(terms) - 1))
    return ins


def split_product(pe, out, a, b, first, last):
    pe.matmul(out, a[0], b[0], start=first, stop=False)
    pe.matmul(out, a[0], b[1], start=False, stop=False)
    return pe.matmul(out, a[1], b[0], start=False, stop=last)


def split_high(S, act, pairs):
    for src, high, low in pairs:
        act.activation(high, src, ACT.Copy).then_inc(S["acts_high"], 1)


def split_low(S, dve, pairs):
    for n, (src, high, low) in enumerate(pairs):
        dve.wait_ge(S["acts_high"], n + 1)
        dve.tensor_tensor(low, src, high.bitcast(F32), ALU.subtract).then_inc(S["acts_low"], 1)


def split(C, name, pairs):
    S = Stage(C.nc, name)
    with C.nc.Block() as block:
        @block.scalar
        def _(act):
            split_high(S, act, pairs)

        @block.vector
        def _(dve):
            split_low(S, dve, pairs)
    S.close()


def channel_tiles(src, halves):
    return [(src[:, k, :], halves[:, 0, k, :], halves[:, 1, k, :]) for k in range(KT)]


def linear(C, name, tiles, jobs, kt=KT, extra=None, pairs=()):
    nc = C.nc
    S = Stage(nc, name)
    by = []
    for j, job in enumerate(jobs):
        by.append("v" if job[9] is not None or (job[8] is None and j % 2) else "a")
    upto = {e: [sum(b == e for b in by[:j + 1]) for j in range(len(jobs))] for e in "av"}
    last = {job[0]: j + 1 for j, job in enumerate(jobs)}
    of_tile = [[j for j, job in enumerate(jobs) if job[0] == n] for n in range(len(tiles))]
    halves = [any(isinstance(jobs[j][4], tuple) for j in of_tile[n]) for n in range(len(tiles))]
    plain = [any(not isinstance(jobs[j][4], tuple) for j in of_tile[n]) for n in range(len(tiles))]
    nth = [sum(halves[:n]) for n in range(len(tiles))]
    split_at = [n for n in range(len(tiles)) if halves[n]]
    out_of = {"a": "taken_by_act", "v": "taken_by_dve"}
    NB = 8

    def where(j):
        _, _, cols, turned, _, _, n, _, _, _ = jobs[j]
        return C.bank[j % NB][0:cols if turned else n, 0:n if turned else cols]

    with ExitStack() as local:
        w2 = local.enter_context(nc.sbuf_tensor(name + "_halves", [P, 2, 2, TILE], F32R)) if any(halves) else None
        with nc.Block() as block:
            @block.sync
            def _(sp):
                for n, src in enumerate(tiles):
                    old = n - RING
                    if old >= 0:
                        if halves[old]:
                            S.wait(sp, "low", nth[old] + 1)
                        if plain[old]:
                            S.wait(sp, "product", last[old])
                    sp.dma_start(C.ring[:, n % RING, :], src).then_inc(S[f"loaded{n % RING}"], 16)

            @block.tensor
            def _(pe):
                at = -1
                S.wait(pe, "acts_low", len(pairs))
                for j, (tile, c0, cols, turned, acts, t0, n, _, _, _) in enumerate(jobs):
                    if tile != at:
                        at = tile
                        pe.wait_ge(S[f"loaded{tile % RING}"], 16 * (tile // RING + 1))
                        if halves[tile]:
                            pe.wait_ge(S["low"], nth[tile] + 1)
                    if j >= NB:
                        S.wait(pe, out_of[by[j - NB]], upto[by[j - NB]][j - NB])
                    for k in range(kt):
                        if isinstance(acts, tuple):
                            w = [w2[:, nth[tile] % 2, i, :].rearrange("p (k c) -> p k c", k=kt)[:, k, c0:c0 + cols]
                                 for i in range(2)]
                            x = [acts[i][:, k, t0:t0 + n] for i in range(2)]
                            a, b = (w, x) if turned else (x, w)
                            ins = split_product(pe, where(j), a, b, k == 0, k == kt - 1)
                        else:
                            w = C.ring[:, tile % RING, :].rearrange("p (k c) -> p k c", k=kt)[:, k, c0:c0 + cols]
                            x = acts[:, k, t0:t0 + n]
                            a, b = (w, x) if turned else (x, w)
                            ins = pe.matmul(where(j), a, b, start=(k == 0), stop=(k == kt - 1))
                    ins.then_inc(S["product"], 1)

            @block.scalar
            def _(act):
                def high(i):
                    n = split_at[i]
                    act.wait_ge(S[f"loaded{n % RING}"], 16 * (n // RING + 1))
                    if i >= 2:
                        act.wait_ge(S["product"], last[split_at[i - 2]])
                    for c in COLUMNS:
                        act.activation(w2[:, i % 2, 0, c], C.ring[:, n % RING, c], ACT.Copy).then_inc(S["high"], 1)

                split_high(S, act, pairs)
                if split_at:
                    high(0)
                for n in range(len(tiles)):
                    if halves[n] and nth[n] + 1 < len(split_at):
                        high(nth[n] + 1)
                    for j in of_tile[n]:
                        if by[j] == "a":
                            act.wait_ge(S["product"], j + 1)
                            act.activation(jobs[j][7], where(j), jobs[j][8] or ACT.Copy).then_inc(S["taken_by_act"], 1)

            @block.vector
            def _(dve):
                def low(i):
                    n = split_at[i]
                    for q, c in enumerate(COLUMNS):
                        dve.wait_ge(S["high"], 2 * i + q + 1)
                        ins = dve.tensor_tensor(w2[:, i % 2, 1, c], C.ring[:, n % RING, c],
                                                w2[:, i % 2, 0, c].bitcast(F32), ALU.subtract)
                    ins.then_inc(S["low"], 1)

                split_low(S, dve, pairs)
                if split_at:
                    low(0)
                for n in range(len(tiles)):
                    if halves[n] and nth[n] + 1 < len(split_at):
                        low(nth[n] + 1)
                    for j in of_tile[n]:
                        if by[j] == "v":
                            dve.wait_ge(S["product"], j + 1)
                            if jobs[j][9] is None:
                                ins = dve.tensor_copy(jobs[j][7], where(j))
                            else:
                                ins = dve.tensor_tensor(jobs[j][7], where(j), jobs[j][9], ALU.mult)
                            ins.then_inc(S["taken_by_dve"], 1)
                if extra is not None:
                    S.wait(dve, "taken_by_act", upto["a"][-1])
                    S.wait(dve, "taken_by_dve", upto["v"][-1])
                    extra(S, dve)
    S.close()


def norm(C, name, rows, eps, centred=False):
    nc = C.nc
    S = Stage(nc, name)
    n = rows[0][4]
    with ExitStack() as local:
        work = local.enter_context(nc.sbuf_tensor(name + "_work", [P, KT, n], F32))
        cent = local.enter_context(nc.sbuf_tensor(name + "_cent", [P, KT, n], F32)) if centred else None
        mean = local.enter_context(nc.sbuf_tensor(name + "_mean", [P, n], F32))
        rstd = local.enter_context(nc.sbuf_tensor(name + "_rstd", [P, n], F32))
        with nc.Block() as block:
            @block.tensor
            def _(pe):
                for i, (src, dst, gain, shift, n) in enumerate(rows):
                    if centred:
                        S.wait(pe, "mean", i)
                        product(pe, C.bank[0][:, 0:n], [(C.sq["ones"], src[:, k, :]) for k in range(KT)])\
                            .then_inc(S["sum"], 1)
                    S.wait(pe, "root", i)
                    for k in range(KT):
                        pe.wait_ge(S["squares"], i * KT + k + 1)
                        ins = pe.matmul(C.bank[1][:, 0:n], C.sq["ones"], work[:, k, :], start=(k == 0),
                                        stop=(k == KT - 1))
                    ins.then_inc(S["square_sum"], 1)

            @block.scalar
            def _(act):
                for i, (src, dst, gain, shift, n) in enumerate(rows):
                    if centred:
                        act.wait_ge(S["sum"], i + 1)
                        act.activation(mean[:, :], C.bank[0][:, 0:n], ACT.Copy, scale=1.0 / D)\
                           .then_inc(S["mean"], 1)
                        src = cent
                    S.wait(act, "square_sum", i)
                    for k in range(KT):
                        if centred:
                            act.wait_ge(S["centred"], i * KT + k + 1)
                        act.activation(work[:, k, :], src[:, k, :], ACT.Square).then_inc(S["squares"], 1)
                    act.wait_ge(S["square_sum"], i + 1)
                    S.wait(act, "scaled", i * KT)
                    act.activation(rstd[:, :], C.bank[1][:, 0:n], ACT.Sqrt, scale=1.0 / D,
                                   bias=C.eps[eps]).then_inc(S["root"], 1)
                    for k in range(KT):
                        act.wait_ge(S["scaled"], i * KT + k + 1)
                        act.activation(dst[:, k, :], dst[:, k, :], ACT.Identity, bias=shift[:, k:k + 1])\
                           .then_inc(S["out"], 1)

            @block.vector
            def _(dve):
                for i, (src, dst, gain, shift, n) in enumerate(rows):
                    if centred:
                        dve.wait_ge(S["mean"], i + 1)
                        for k in range(KT):
                            dve.tensor_tensor(cent[:, k, :], src[:, k, :], mean[:, :], ALU.subtract)\
                               .then_inc(S["centred"], 1)
                        dve.wait_ge(S["centred"], (i + 1) * KT)
                        src = cent
                    dve.wait_ge(S["root"], i + 1)
                    S.link(dve, dve.reciprocal(rstd[:, :], rstd[:, :]), "inverse")
                    for k in range(KT):
                        dve.scalar_tensor_tensor(out=dst[:, k, :], in0=src[:, k, :], scalar=gain[:, k:k + 1],
                                                 in1=rstd[:, :], op0=ALU.mult, op1=ALU.mult)\
                           .then_inc(S["scaled"], 1)
        S.close()


def modulation(C, A, mod):
    nc = C.nc
    S = Stage(nc, "modulation")
    tiles = 6 * D // 256
    with ExitStack() as local:
        c = local.enter_context(nc.sbuf_tensor("cond", [P, KT, 2], F32))
        bias = local.enter_context(nc.sbuf_tensor("mod_bias", [P, 6 * KT], F32))
        row = local.enter_context(nc.sbuf_tensor("mod_rows", [2, 6 * D], F32))
        with nc.Block() as block:
            @block.sync
            def _(sp):
                sp.dma_start(c[:, :, :], A["cond"]).then_inc(S["small"], 16)
                sp.dma_start(bias[:, :], A["mod_b"]).then_inc(S["small"], 16)
                for n in range(tiles):
                    S.wait(sp, "product", n - RING + 1)
                    sp.dma_start(C.ring[:, n % RING, :], A["mod_w"][n]).then_inc(S[f"loaded{n % RING}"], 16)

            @block.scalar
            def _(act):
                act.wait_ge(S["small"], 32)
                act.activation(c[:, :, :], c[:, :, :], ACT.Silu).then_inc(S["silu"], 1)
                for n in range(tiles):
                    act.wait_ge(S["product"], n + 1)
                    act.activation(row[:, n * 256:(n + 1) * 256], C.bank[n % 4][0:2, 0:256], ACT.Copy)\
                       .then_inc(S["row"], 1)

            @block.tensor
            def _(pe):
                pe.wait_ge(S["silu"], 1)
                for n in range(tiles):
                    pe.wait_ge(S[f"loaded{n % RING}"], 16 * (n // RING + 1))
                    S.wait(pe, "row", n - 3)
                    w = C.ring[:, n % RING, :].rearrange("p (k c) -> p k c", k=KT)
                    product(pe, C.bank[n % 4][0:2, 0:256], [(c[:, k, :], w[:, k, :]) for k in range(KT)])\
                        .then_inc(S["product"], 1)
                for m in range(6 * KT):
                    pe.wait_ge(S["row"], m // 2 + 1)
                    ins = pe.transpose(C.bank[4][:, 2 * m:2 * m + 2], row[:, m * P:(m + 1) * P],
                                       C.sq["ident"][0:2, 0:2])
                ins.then_inc(S["turned"], 1)

            @block.vector
            def _(dve):
                dve.wait_ge(S["small"], 32)
                dve.wait_ge(S["turned"], 1)
                S.link(dve, dve.tensor_tensor(mod[:, :, :], C.bank[4][:, 0:12 * KT].rearrange("p (m c) -> p m c", c=2),
                                              bias[:, :].unsqueeze(2).broadcast_to([P, 6 * KT, 2]), ALU.add), "mod")
        S.close()


def gains(C, name, rows):
    nc = C.nc
    S = Stage(nc, name)
    with nc.Block() as block:
        @block.vector
        def _(dve):
            for out, gain, scale in rows:
                S.link(dve, dve.scalar_tensor_tensor(out=out, in0=scale, scalar=1.0, in1=gain,
                                                     op0=ALU.add, op1=ALU.mult), "gain")
    S.close()


def rwkv_prep(C, Z, W, weights):
    nc = C.nc
    S = Stage(nc, "rwkv_prep")
    kT, kk = Z["k"], W["kk"]
    with ExitStack() as local:
        sq = local.enter_context(nc.sbuf_tensor("kk_sq", [P, PAIRS, ALL], F32))
        nrm = local.enter_context(nc.sbuf_tensor("kk_norm", [P, PAIRS, ALL], F32))
        with nc.Block() as block:
            @block.sync
            def _(sp):
                for dst, src in weights:
                    sp.dma_start(dst, src).then_inc(S["weights"], 16)
                sp.wait_ge(S["weights"], 16 * len(weights))

            @block.tensor
            def _(pe):
                for p in range(PAIRS):
                    pe.wait_ge(S["squares"], p + 1)
                    product(pe, C.bank[p][:, :], [(C.sq["head_ones"], sq[:, p, :])]).then_inc(S["norm"], 1)

            @block.scalar
            def _(act):
                for p in range(PAIRS):
                    act.wait_ge(S["scaled"], p + 1)
                    act.activation(sq[:, p, :], kk[:, p, :], ACT.Square).then_inc(S["squares"], 1)
                for p in range(PAIRS):
                    act.wait_ge(S["clamped"], p + 1)
                    act.activation(nrm[:, p, :], nrm[:, p, :], ACT.Sqrt).then_inc(S["root"], 1)

            @block.vector
            def _(dve):
                for p in range(PAIRS):
                    dve.tensor_scalar(kk[:, p, :], kT[:, p, :], C.v["k_k"][:, p:p + 1], None, ALU.mult)\
                       .then_inc(S["scaled"], 1)
                for p in range(PAIRS):
                    dve.wait_ge(S["norm"], p + 1)
                    dve.tensor_scalar(nrm[:, p, :], C.bank[p][:, :], 1e-12, None, ALU.max)\
                       .then_inc(S["clamped"], 1)
                dve.wait_ge(S["scaled"], PAIRS)
                for p in range(PAIRS):
                    dve.wait_ge(S["root"], p + 1)
                    S.link(dve, dve.reciprocal(nrm[:, p, :], nrm[:, p, :]), "inverse")
                    dve.tensor_tensor(kk[:, p, :], kk[:, p, :], nrm[:, p, :], ALU.mult).then_inc(S["kk"], 1)
        S.close()


SIDES = ("fwd", "bwd")


def rwkv_tile(C, Z, W, step, B):
    nc = C.nc
    latent = step >= 2
    tile = [step, (1, 0, 3, 2)[step]]
    NCOL = 512 if latent else 256
    S = Stage(nc, f"delta{step}")

    def tok(d):
        return slice(P * tile[d], P * tile[d] + P)

    def lat(d):
        return slice(P * tile[d] - CTX, P * tile[d] - CTX + P)

    def rows(h):
        return slice(HD * (h % 2), HD * (h % 2) + HD)

    qr, bb, kn, btok, ktok = B["qr"], B["bb"], B["kn"], B["btok"], B["ktok"]
    ein, eex, eneg, tmp = B["ein"], B["eex"], B["eneg"], B["tmp"]
    X, PT, M = B["X"], B["PT"], B["M"]
    with nc.Block() as block:
        @block.tensor
        def _(pe):
            for d in range(2):
                r = slice(64 * d, 64 * d + 64)
                product(pe, C.bank[2 + d][:, :], [(Z["lw"][r, tok(d)], W["wb"][r, :]),
                                                  (C.sq["ones"][r, :], W["w0"][r, :])]).then_inc(S["wl"], 1)
                for p in range(PAIRS):
                    ins = product(pe, C.bank[6 + d][:, p * P:(p + 1) * P],
                                  [(W["ab"][r, p * P:(p + 1) * P], Z["la"][r, tok(d)])])
                ins.then_inc(S["al"], 1)
            for d, side in enumerate(SIDES):
                pe.wait_ge(S["sig"], d + 1)
                if d:
                    pe.wait_ge(S["decays"], 3 * d)
                for p in range(PAIRS):
                    out = C.bank[p // 2][:, (p % 2) * 256:(p % 2) * 256 + 256]
                    lhsT = W["sig"][:, d, p * P:(p + 1) * P]
                    pe.matmul(out[:, 0:P], lhsT, C.sq[side + "_in"], start=True, stop=True)
                    ins = pe.matmul(out[:, P:2 * P], lhsT, C.sq[side + "_ex"], start=True, stop=True)
                ins.then_inc(S["logs"], 1)
            for d in range(2):
                pe.wait_ge(S["operands"], d + 1)
                if d:
                    pe.wait_ge(S["tok"], 2 * d)
                for p in range(PAIRS):
                    pe.transpose(C.bank[4][:, p * P:(p + 1) * P], bb[:, d, p, :], C.sq["ident"])
                    ins = pe.transpose(C.bank[5][:, p * P:(p + 1) * P], kn[:, d, p, :], C.sq["ident"])
                ins.then_inc(S["turned"], 1)

        @block.scalar
        def _(act):
            for d in range(2):
                act.wait_ge(S["wl"], d + 1)
                act.activation(W["sig"][:, d, :], C.bank[2 + d][:, :], ACT.Sigmoid).then_inc(S["sig"], 1)
                act.wait_ge(S["al"], d + 1)
                for p in range(PAIRS):
                    ins = act.activation(W["a"][:, d, p, :], C.bank[6 + d][:, p * P:(p + 1) * P], ACT.Sigmoid,
                                         bias=C.v["a0"][:, 4 * d + p:4 * d + p + 1])
                ins.then_inc(S["a"], 1)
            for d in range(2):
                act.wait_ge(S["logs"], d + 1)
                for i, (dst, scale, half) in enumerate(((ein, 1.0, 0), (eneg, -1.0, 0), (eex, 1.0, 1))):
                    for q in range(2):
                        src = C.bank[q][:, :].rearrange("p (a c) -> p a c", a=2)[:, :, half * P:half * P + P]
                        ins = act.activation(dst[:, d, 2 * q:2 * q + 2, :], src, ACT.Exp, scale=scale)
                    ins.then_inc(S["decays"], 1)
            for d in range(2):
                act.wait_ge(S["turned"], d + 1)
                for dst, bank in ((btok, 4), (ktok, 5)):
                    act.activation(dst[:, d, :], C.bank[bank][:, :], ACT.Copy).then_inc(S["tok"], 1)

        @block.vector
        def _(dve):
            for d in range(2):
                a = W["a"][:, d, :, :]
                dve.wait_ge(S["a"], d + 1)
                kk = W["kk"][:, :, tok(d)]
                for p in range(PAIRS):
                    dve.tensor_scalar(tmp[:, d, p, :], a[:, p, :], C.v["k_a"][:, p:p + 1],
                                      C.v["one_minus_k_a"][:, p:p + 1], ALU.mult, ALU.add).then_inc(S["rate"], 1)
                dve.wait_ge(S["rate"], PAIRS * (d + 1))
                S.link(dve, dve.tensor_tensor(kn[:, d, :, :], tmp[:, d, :, :], Z["k"][:, :, tok(d)], ALU.mult), "kdir")
                S.link(dve, dve.tensor_tensor(bb[:, d, :, :], a, kk, ALU.mult), "kka")
                dve.wait_ge(S["decays"], 3 * d + 3)
                dve.tensor_tensor(qr[:, d, :, 0:P], kk, eex[:, d, :, :], ALU.mult).then_inc(S["q"], 1)
                if latent:
                    dve.tensor_tensor(qr[:, d, :, P:2 * P], Z["r"][:, :, lat(d)], ein[:, d, :, :], ALU.mult)\
                       .then_inc(S["r"], 1)
                dve.tensor_tensor(kn[:, d, :, :], kn[:, d, :, :], eneg[:, d, :, :], ALU.mult).then_inc(S["k"], 1)
                dve.wait_ge(S["k"], d + 1)
                dve.wait_ge(S["q"], d + 1)
                S.link(dve, dve.tensor_tensor(bb[:, d, :, :], bb[:, d, :, :], eneg[:, d, :, :], ALU.mult), "operands")
    S.close()

    S = Stage(nc, f"inverse{step}")
    UN = 2 * NH
    SQ = 5
    with nc.Block() as block:
        @block.tensor
        def _(pe):
            for u in range(UN):
                d, h = u // NH, u % NH
                r, p = rows(h), h // 2
                if u >= 3:
                    pe.wait_ge(S["masked"], u - 2)
                b1, b2 = C.bank[2 * (u % 3)], C.bank[2 * (u % 3) + 1]
                w = 2 * P if latent else P
                pe.matmul(b1[:, 0:w], bb[r, d, p, :], qr[r, d, p, 0:w], start=True, stop=True)
                pe.matmul(b1[:, 256:256 + w], kn[r, d, p, :], qr[r, d, p, 0:w], start=True, stop=True)
                pe.matmul(b2[:, 0:P], qr[r, d, p, 0:P], bb[r, d, p, :], start=True, stop=True)\
                  .then_inc(S["pairs"], 1)
            pe.wait_ge(S["masked"], UN)
            for s in range(SQ + 1):
                for u in range(UN):
                    n = s * UN + u
                    if s == 0:
                        pe.wait_ge(S["first"], u + 1)
                    else:
                        pe.wait_ge(S["power"], n - UN + 1)
                    m, mt = M[:, u, 0:P], M[:, u, P:2 * P]
                    if s >= 1:
                        q = n - UN
                        S.wait(pe, "summed", max(q - 3, q - UN + 1))
                        pe.matmul(C.bank[4 + q % 4][:, 0:P], m, PT[:, u, :], start=True, stop=True)\
                          .then_inc(S["corrected"], 1)
                    if s < SQ:
                        S.wait(pe, "power", n - 3)
                        ins = pe.matmul(C.bank[n % 4][:, 0:P], mt, m, start=True, stop=True)
                        if s < SQ - 1:
                            ins = pe.matmul(C.bank[n % 4][:, P:2 * P], m, mt, start=True, stop=True)
                        ins.then_inc(S["squared"], 1)

        @block.scalar
        def _(act):
            for s in range(SQ):
                for u in range(UN):
                    n = s * UN + u
                    act.wait_ge(S["squared"], n + 1)
                    w = 2 * P if s < SQ - 1 else P
                    act.activation(M[:, u, 0:w], C.bank[n % 4][:, 0:w], ACT.Copy).then_inc(S["power"], 1)

        @block.vector
        def _(dve):
            for u in range(UN):
                d = u // NH
                dve.wait_ge(S["pairs"], u + 1)
                mask = C.mask4[:, d, :] if latent else C.mask4[:, d, :].rearrange("p (a c) -> p a c", a=2)[:, :, 0:P]
                b1, b2 = C.bank[2 * (u % 3)], C.bank[2 * (u % 3) + 1]
                x = X[:, u, :].rearrange("p (a c) -> p a c", a=2)
                if latent:
                    dve.tensor_tensor(X[:, u, :], b1[:, :], mask, ALU.mult).then_inc(S["x"], 1)
                else:
                    dve.tensor_tensor(x[:, :, 0:P], b1[:, :].rearrange("p (a c) -> p a c", a=2)[:, :, 0:P], mask,
                                      ALU.mult).then_inc(S["x"], 1)
                dve.tensor_tensor(M[:, u, 0:P], b2[:, 0:P], C.sq["m_" + SIDES[1 - d] + "_ex"], ALU.mult)\
                   .then_inc(S["masked"], 1)
            for u in range(UN):
                dve.wait_ge(S["x"], u + 1)
                dve.tensor_tensor(PT[:, u, :], C.sq["ident"], X[:, u, 0:P], ALU.subtract).then_inc(S["start"], 1)
                dve.tensor_copy(M[:, u, P:2 * P], X[:, u, 0:P]).then_inc(S["first"], 1)
            for q in range(SQ * UN):
                u = q % UN
                dve.wait_ge(S["corrected"], q + 1)
                if q < UN:
                    dve.wait_ge(S["start"], u + 1)
                else:
                    dve.wait_ge(S["summed"], q - UN + 1)
                dve.tensor_tensor(PT[:, u, :], PT[:, u, :], C.bank[4 + q % 4][:, 0:P], ALU.add)\
                   .then_inc(S["summed"], 1)
    S.close()

    S = Stage(nc, f"chain{step}")
    R, nU, S0, SW, yT, V = B["R"], B["nU"], W["S0"], B["SW"], W["y"], Z["v"]
    units = [(c, d) for c in range(2) for d in range(2)]

    def chunk(c, d):
        a = CH * (c if d == 0 else 1 - c)
        return slice(a, a + CH)

    def cols(h):
        return slice(HD * h, HD * h + HD)

    with nc.Block() as block:
        @block.tensor
        def _(pe):
            for n, (c, d) in enumerate(units):
                t, B0 = chunk(c, d), 4 * d
                if c:
                    pe.wait_ge(S["state"], n - 1)
                for p in range(PAIRS):
                    pe.matmul(C.bank[B0][t, p * P:(p + 1) * P], qr[:, d, p, t], S0[:, d, p, :],
                              start=True, stop=False, skip_group_check=True)
                    for h in (2 * p, 2 * p + 1):
                        ins = pe.matmul(C.bank[B0][t, cols(h)], X[:, d * NH + h, 256 + t.start:256 + t.stop],
                                        V[:, tile[d], cols(h)], start=False, stop=True, skip_group_check=True)
                ins.then_inc(S["right_side"], 1)
                pe.wait_ge(S["right"], n + 1)
                for h in range(NH):
                    ins = pe.matmul(C.bank[B0 + 1][t, cols(h)], PT[:, d * NH + h, t], R[:, d, cols(h)],
                                    start=True, stop=True)
                ins.then_inc(S["solved"], 1)
                pe.wait_ge(S["u"], n + 1)
                for p in range(PAIRS):
                    c2 = slice(p * P, (p + 1) * P)
                    pe.matmul(C.bank[B0 + 2][:, c2], btok[t, d, c2], nU[t, d, c2], start=True, stop=False)
                    ins = pe.matmul(C.bank[B0 + 2][:, c2], ktok[t, d, c2], V[t, tile[d], c2], start=False, stop=True)
                ins.then_inc(S["update"], 1)
                if latent:
                    if c:
                        pe.wait_ge(S["y"], n - 1)
                    for p in range(PAIRS):
                        out = C.bank[B0 + 3][:, p * CH:(p + 1) * CH]
                        pe.matmul(out, S0[:, d, p, :], qr[:, d, p, P + t.start:P + t.stop], start=True, stop=False,
                                  skip_group_check=True)
                        for h in (2 * p, 2 * p + 1):
                            r, u = rows(h), d * NH + h
                            out = C.bank[B0 + 3][r, p * CH:(p + 1) * CH]
                            pe.matmul(out, nU[:, d, cols(h)], X[:, u, P + t.start:P + t.stop], start=False, stop=False,
                                      skip_group_check=True)
                            ins = pe.matmul(out, V[:, tile[d], cols(h)], X[:, u, 384 + t.start:384 + t.stop],
                                            start=False, stop=True, skip_group_check=True)
                    ins.then_inc(S["y_product"], 1)

        @block.scalar
        def _(act):
            for n, (c, d) in enumerate(units):
                t, B0 = chunk(c, d), 4 * d
                act.wait_ge(S["right_side"], n + 1)
                act.activation(R[t, d, :], C.bank[B0][t, :], ACT.Copy).then_inc(S["right"], 1)
                act.wait_ge(S["solved"], n + 1)
                act.activation(nU[t, d, :], C.bank[B0 + 1][t, :], ACT.Copy, scale=-1.0).then_inc(S["u"], 1)

        @block.vector
        def _(dve):
            for n, (c, d) in enumerate(units):
                t, B0 = chunk(c, d), 4 * d
                last = t.stop - 1 if d == 0 else t.start
                for p in range(PAIRS):
                    dve.tensor_scalar(SW[:, p, :], C.sq["head_ones"], ein[:, d, p, last:last + 1], None, ALU.mult)\
                       .then_inc(S["whole"], 1)
                dve.wait_ge(S["whole"], PAIRS * (n + 1))
                dve.wait_ge(S["update"], n + 1)
                if latent:
                    dve.wait_ge(S["y_product"], n + 1)
                S.link(dve, dve.tensor_tensor(S0[:, d, :, :], S0[:, d, :, :], C.bank[B0 + 2][:, :].rearrange(
                    "p (a c) -> p a c", a=PAIRS), ALU.add), "sum")
                S.link(dve, dve.tensor_tensor(S0[:, d, :, :], S0[:, d, :, :], SW[:, :, :], ALU.mult), "state")
                if latent:
                    at = P * tile[d] - CTX + t.start
                    out = yT[:, d, :, at:at + CH]
                    dve.tensor_copy(out, C.bank[B0 + 3][:, 0:256].rearrange("p (a c) -> p a c", a=PAIRS))\
                       .then_inc(S["y"], 1)
    S.close()


def head_norm(C, name, src, dst, eps, gain, shift, centred, nt=PAIRS, cols=SEQ):
    nc = C.nc
    S = Stage(nc, name)
    half = nt * cols // 512
    with ExitStack() as local:
        work = local.enter_context(nc.sbuf_tensor(name + "_w", [P, nt * cols], F32))
        root = local.enter_context(nc.sbuf_tensor(name + "_r", [P, nt * cols], F32))
        s2 = src[:, :, :].rearrange("p a c -> p (a c)")
        d2 = dst[:, :, :].rearrange("p a c -> p (a c)")
        with nc.Block() as block:
            @block.tensor
            def _(pe):
                if centred:
                    for i in range(half):
                        product(pe, C.bank[i][:, :], [(C.sq["head_ones"], s2[:, i * 512:(i + 1) * 512])])\
                            .then_inc(S["sum"], 1)
                for i in range(half):
                    pe.wait_ge(S["squares"], i + 1)
                    product(pe, C.bank[4 + i][:, :], [(C.sq["head_ones"], work[:, i * 512:(i + 1) * 512])])\
                        .then_inc(S["square_sum"], 1)

            @block.scalar
            def _(act):
                for i in range(half):
                    c = slice(i * 512, (i + 1) * 512)
                    if centred:
                        act.wait_ge(S["centred"], i + 1)
                    act.activation(work[:, c], (d2 if centred else s2)[:, c], ACT.Square).then_inc(S["squares"], 1)
                for i in range(half):
                    act.wait_ge(S["square_sum"], i + 1)
                    act.activation(root[:, i * 512:(i + 1) * 512], C.bank[4 + i][:, :], ACT.Sqrt, scale=1.0 / HD,
                                   bias=C.eps[eps]).then_inc(S["root"], 1)

            @block.vector
            def _(dve):
                if centred:
                    for i in range(half):
                        c = slice(i * 512, (i + 1) * 512)
                        dve.wait_ge(S["sum"], i + 1)
                        dve.scalar_tensor_tensor(out=d2[:, c], in0=C.bank[i][:, :], scalar=-1.0 / HD, in1=s2[:, c],
                                                 op0=ALU.mult, op1=ALU.add).then_inc(S["centred"], 1)
                    dve.wait_ge(S["centred"], half)
                per = nt // half
                for i in range(half):
                    c = slice(i * 512, (i + 1) * 512)
                    dve.wait_ge(S["root"], i + 1)
                    S.link(dve, dve.reciprocal(root[:, c], root[:, c]), "inverse")
                    for p in range(i * per, (i + 1) * per):
                        dve.scalar_tensor_tensor(out=dst[:, p, :], in0=(dst if centred else src)[:, p, :],
                                                 scalar=gain[:, p:p + 1], in1=root[:, p * cols:(p + 1) * cols],
                                                 op0=ALU.mult, op1=ALU.mult).then_inc(S["scaled"], 1)
                if shift is not None:
                    for p in range(nt):
                        dve.wait_ge(S["scaled"], p + 1)
                        dve.tensor_scalar(dst[:, p, :], dst[:, p, :], shift[:, p:p + 1], None, ALU.add)\
                           .then_inc(S["out"], 1)
        S.close()


def rwkv_bonus(C, A, Z, W, ya):
    nc = C.nc
    S = Stage(nc, "bonus")
    with ExitStack() as local:
        rk = local.enter_context(nc.sbuf_tensor("rk", [P, PAIRS, SEQ], F32))
        vT = local.enter_context(nc.sbuf_tensor("vT", [P, PAIRS, SEQ], F32))
        gb = local.enter_context(nc.sbuf_tensor("g_lora", [P, NH * HD], F32))
        flat = rk[:, :, :].rearrange("p a c -> p (a c)")
        with nc.Block() as block:
            @block.sync
            def _(sp):
                sp.dma_start(gb[:, :], A["rw_g_lora_b"]).then_inc(S["lora"], 16)

            @block.tensor
            def _(pe):
                for p in range(PAIRS):
                    for t in range(TT):
                        ins = pe.transpose(C.bank[p // 2][:, (p % 2) * SEQ + t * P:(p % 2) * SEQ + (t + 1) * P],
                                           Z["v"][:, TT + t, p * P:(p + 1) * P], C.sq["ident"])
                ins.then_inc(S["v_turned"], 1)
                pe.wait_ge(S["lora"], 16)
                for p in range(PAIRS):
                    ins = product(pe, C.bank[2 + p // 2][:, (p % 2) * SEQ:(p % 2) * SEQ + SEQ],
                                  [(gb[:, p * P:(p + 1) * P], Z["lg"][:, :])])
                ins.then_inc(S["gate"], 1)
                pe.wait_ge(S["rk"], PAIRS)
                for i in range(2):
                    ins = product(pe, C.bank[4 + i][:, :], [(C.sq["head_ones"], flat[:, i * 512:(i + 1) * 512])])
                ins.then_inc(S["rk_sum"], 1)

            @block.scalar
            def _(act):
                act.wait_ge(S["v_turned"], 1)
                for i in range(2):
                    act.activation(vT[:, 2 * i:2 * i + 2, :], C.bank[i][:, :].rearrange("p (a c) -> p a c", a=2),
                                   ACT.Copy).then_inc(S["v"], 1)

            @block.vector
            def _(dve):
                for p in range(PAIRS):
                    dve.scalar_tensor_tensor(out=rk[:, p, :], in0=Z["r"][:, p, :], scalar=C.v["r_k"][:, p:p + 1],
                                             in1=Z["k"][:, p, CTX:ALL], op0=ALU.mult, op1=ALU.mult)\
                       .then_inc(S["rk"], 1)
                dve.wait_ge(S["v"], 2)
                dve.wait_ge(S["rk_sum"], 1)
                for i in range(2):
                    c = slice(2 * i, 2 * i + 2)
                    S.link(dve, dve.tensor_tensor(vT[:, c, :], vT[:, c, :], C.bank[4 + i][:, :].rearrange(
                        "p (a c) -> p a c", a=2), ALU.mult), "bonus")
                S.link(dve, dve.tensor_tensor(ya[:, :, :], ya[:, :, :], vT[:, :, :], ALU.add), "added")
                dve.wait_ge(S["gate"], 1)
                for i in range(2):
                    c = slice(2 * i, 2 * i + 2)
                    S.link(dve, dve.tensor_tensor(ya[:, c, :], ya[:, c, :], C.bank[2 + i][:, :].rearrange(
                        "p (a c) -> p a c", a=2), ALU.mult), "gated")
        S.close()


def na_attention(C, A, Z, qn, kn, yb):
    nc = C.nc
    S = Stage(nc, "na")
    units = [(h, t) for h in range(NH) for t in range(TT)]
    N = len(units)
    scale = HD ** -0.5
    with ExitStack() as local:
        sb = lambda name, shape: local.enter_context(nc.sbuf_tensor(name, shape, F32))
        bias = sb("na_bias", [P, 3, SEQ])
        mask = sb("na_mask", [P, TT, SEQ])
        sc = sb("na_scores", [P, 3, ALL])
        pT = sb("na_probsT", [P, 2, ALL])
        mx = sb("na_max", [P, N])
        rs = sb("na_sum", [P, N])
        with nc.Block() as block:
            @block.sync
            def _(sp):
                sp.dma_start(mask[:, :, :], A["na_mask"]).then_inc(S["mask"], 16)
                for n, (h, t) in enumerate(units):
                    S.wait(sp, "biased", n - 2)
                    sp.dma_start(bias[:, n % 3, :], A["na_bias"][h, t]).then_inc(S[f"bias{n % 3}"], 16)

            @block.gpsimd
            def _(pool):
                pool.wait_ge(S["mask"], 16)
                for n, (h, t) in enumerate(units):
                    pool.wait_ge(S[f"bias{n % 3}"], 16 * (n // 3 + 1))
                    pool.tensor_tensor(bias[:, n % 3, :], bias[:, n % 3, :], mask[:, t, :], ALU.add)\
                        .then_inc(S["bias_masked"], 1)

            @block.tensor
            def _(pe):
                def scores(n):
                    h, t = units[n]
                    r, p = slice(HD * (h % 2), HD * (h % 2) + HD), h // 2
                    if n >= 2:
                        pe.wait_ge(S["biased"], n - 1)
                    pe.matmul(C.bank[n % 2][:, :], qn[r, p, t * P:(t + 1) * P], kn[r, p, :],
                              start=True, stop=True).then_inc(S["scores"], 1)

                def mix(n):
                    h, t = units[n]
                    r = slice(HD * (h % 2), HD * (h % 2) + HD)
                    pe.wait_ge(S["turned_out"], n + 1)
                    if n >= 2:
                        pe.wait_ge(S["out"], n - 1)
                    product(pe, C.bank[4 + n % 2][r, 0:P],
                            [(Z["vb"][:, k, h * HD:(h + 1) * HD], pT[:, n % 2, k * P:(k + 1) * P])
                             for k in range(4)]).then_inc(S["mixed"], 1)

                scores(0)
                scores(1)
                for n, (h, t) in enumerate(units):
                    r, p = slice(HD * (h % 2), HD * (h % 2) + HD), h // 2
                    if n + 2 < N:
                        scores(n + 2)
                    pe.wait_ge(S["probs"], n + 1)
                    if n >= 2:
                        pe.wait_ge(S["turned_out"], n - 1)
                    for k in range(4):
                        ins = pe.transpose(C.bank[2 + n % 2][:, k * P:(k + 1) * P],
                                           sc[:, n % 3, k * P:(k + 1) * P], C.sq["ident"])
                    ins.then_inc(S["turned"], 1)
                    if n:
                        mix(n - 1)
                mix(N - 1)

            @block.scalar
            def _(act):
                def exp(n):
                    act.wait_ge(S["max"], n + 1)
                    act.activation(sc[:, n % 3, :], sc[:, n % 3, :], ACT.Exp, bias=mx[:, n:n + 1],
                                   accum_out=rs[:, n:n + 1]).then_inc(S["exp"], 1)

                exp(0)
                for n in range(N):
                    if n + 1 < N:
                        exp(n + 1)
                    act.wait_ge(S["turned"], n + 1)
                    S.wait(act, "mixed", n - 1)
                    act.activation(pT[:, n % 2, :], C.bank[2 + n % 2][:, :], ACT.Copy).then_inc(S["turned_out"], 1)

            @block.vector
            def _(dve):
                def begin(n):
                    h, t = units[n]
                    dve.wait_ge(S["scores"], n + 1)
                    S.wait(dve, "turned", n - 2)
                    dve.wait_ge(S["bias_masked"], n + 1)
                    dve.tensor_scalar(sc[:, n % 3, 0:CTX], C.bank[n % 2][:, 0:CTX], scale, None, ALU.mult)\
                       .then_inc(S["ctx_scores"], 1)
                    S.link(dve, dve.scalar_tensor_tensor(out=sc[:, n % 3, CTX:ALL], in0=C.bank[n % 2][:, CTX:ALL],
                                                         scalar=scale, in1=bias[:, n % 3, :], op0=ALU.mult,
                                                         op1=ALU.add), "biased")
                    S.link(dve, dve.tensor_reduce(mx[:, n:n + 1], sc[:, n % 3, :], AX, ALU.max), "reduced")
                    dve.tensor_scalar(mx[:, n:n + 1], mx[:, n:n + 1], -1.0, None, ALU.mult).then_inc(S["max"], 1)

                def take(n):
                    h, t = units[n]
                    dve.wait_ge(S["mixed"], n + 1)
                    r, p = slice(HD * (h % 2), HD * (h % 2) + HD), h // 2
                    dve.tensor_copy(yb[r, p, t * P:(t + 1) * P], C.bank[4 + n % 2][r, 0:P]).then_inc(S["out"], 1)

                begin(0)
                begin(1)
                for n, (h, t) in enumerate(units):
                    dve.wait_ge(S["exp"], n + 1)
                    S.link(dve, dve.reciprocal(rs[:, n:n + 1], rs[:, n:n + 1]), "inverse")
                    dve.tensor_scalar(sc[:, n % 3, :], sc[:, n % 3, :], rs[:, n:n + 1], None, ALU.mult)\
                       .then_inc(S["probs"], 1)
                    if n + 2 < N:
                        begin(n + 2)
                    if n >= 2:
                        take(n - 2)
                take(N - 2)
                take(N - 1)
        S.close()


def router(C, A, h2, gate_all, mod, m5, pairs):
    nc = C.nc
    S = Stage(nc, "router")
    with ExitStack() as local:
        sb = lambda name, shape: local.enter_context(nc.sbuf_tensor(name, shape, F32))
        rw = sb("router_w", [P, KT, N_EXP])
        rb = sb("router_b", [P, N_EXP])
        pick = sb("pick", [N_EXP, N_EXP, P])
        sc = sb("r_scores", [P, TT, N_EXP])
        sel = sb("r_sel", [P, TT, N_EXP])
        pair = sb("r_pair", [P, TT, 4, 6])
        grp = sb("r_grp", [P, TT, 4])
        top = sb("r_top", [P, TT, 8])
        den = sb("r_den", [P, TT])
        gT = sb("r_gateT", [N_EXP, SEQ])
        with nc.Block() as block:
            @block.sync
            def _(sp):
                for dst, src in ((rw[:, :, :], "router_w"), (rb[:, :], "router_bias"), (pick[:, :, :], "pick")):
                    sp.dma_start(dst, A[src]).then_inc(S["loaded"], 16)

            @block.tensor
            def _(pe):
                pe.wait_ge(S["loaded"], 48)
                for t in range(TT):
                    ins = product(pe, C.bank[0][:, t * N_EXP:(t + 1) * N_EXP],
                                  [(h2[:, k, t * P:(t + 1) * P], rw[:, k, :]) for k in range(KT)])
                ins.then_inc(S["logits"], 1)
                pe.wait_ge(S["gates"], TT)
                for t in range(TT):
                    ins = pe.transpose(C.bank[1][0:N_EXP, t * P:(t + 1) * P], sel[:, t, :], C.sq["ident"])
                ins.then_inc(S["turned"], 1)
                pe.wait_ge(S["gateT"], 1)
                for e in range(N_EXP):
                    if e >= 4:
                        pe.wait_ge(S["spread_out"], e - 3)
                    pe.matmul(C.bank[2 + e % 4][:, 0:SEQ], pick[:, e, :], gT[:, :], start=True, stop=True)\
                      .then_inc(S["spread"], 1)

            @block.scalar
            def _(act):
                split_high(S, act, pairs)
                act.wait_ge(S["logits"], 1)
                act.activation(sc[:, :, :], C.bank[0][:, 0:TT * N_EXP].rearrange("p (t e) -> p t e", t=TT),
                               ACT.Sigmoid).then_inc(S["scores"], 1)
                act.wait_ge(S["turned"], 1)
                act.activation(gT[:, :], C.bank[1][0:N_EXP, 0:SEQ], ACT.Copy).then_inc(S["gateT"], 1)
                for e in range(N_EXP):
                    act.wait_ge(S["spread"], e + 1)
                    act.activation(gate_all[:, e, :], C.bank[2 + e % 4][:, 0:SEQ], ACT.Copy)\
                       .then_inc(S["spread_out"], 1)

            @block.vector
            def _(dve):
                L = lambda ins: S.link(dve, ins, "vector")
                split_low(S, dve, pairs)
                L(dve.tensor_copy(m5[:, :], mod[:, 5 * KT:6 * KT, 0]))
                dve.wait_ge(S["loaded"], 48)
                dve.wait_ge(S["scores"], 1)
                L(dve.tensor_tensor(sel[:, :, :], sc[:, :, :], rb[:, :].unsqueeze(1).broadcast_to([P, TT, N_EXP]), ALU.add))
                for t in range(TT):
                    s = sel[:, t, :].rearrange("p (g e) -> p g e", g=4)
                    at = 0
                    for gap in (1, 2, 3):
                        L(dve.tensor_tensor(pair[:, t, :, at:at + 4 - gap], s[:, :, 0:4 - gap], s[:, :, gap:4], ALU.add))
                        at += 4 - gap
                    L(dve.tensor_reduce(grp[:, t, :], pair[:, t, :, :], AX, ALU.max))
                    L(dve.tensor_reduce(den[:, t:t + 1], grp[:, t, :], AX, ALU.max))
                    L(dve.tensor_scalar(grp[:, t, :], grp[:, t, :], den[:, t:t + 1], None, ALU.is_ge))
                    g = grp[:, t, :].unsqueeze(2).broadcast_to([P, 4, 4])
                    L(dve.tensor_tensor(s, s, g, ALU.mult))
                    L(dve.tensor_scalar(grp[:, t, :], grp[:, t, :], 1.0, -NEG, ALU.subtract, ALU.mult))
                    L(dve.tensor_tensor(s, s, g, ALU.add))
                    L(dve.max(top[:, t, :], sel[:, t, :]))
                    L(dve.tensor_scalar(sel[:, t, :], sel[:, t, :], top[:, t, 1:2], None, ALU.is_ge))
                    L(dve.tensor_tensor(sel[:, t, :], sel[:, t, :], sc[:, t, :], ALU.mult))
                    L(dve.tensor_reduce(den[:, t:t + 1], sel[:, t, :], AX, ALU.add))
                    L(dve.reciprocal(den[:, t:t + 1], den[:, t:t + 1]))
                    S.link(dve, dve.tensor_scalar(sel[:, t, :], sel[:, t, :], den[:, t:t + 1], None, ALU.mult), "gates")
        S.close()


def experts(C, A, h2, gate_all, xT, m5):
    nc = C.nc
    S = Stage(nc, "experts")
    HT = D_EXP // P
    NT = 6
    FIRST_UP = 4
    with ExitStack() as local:
        act_h = local.enter_context(nc.sbuf_tensor("silu_h", [P, HT, SEQ], F32))
        hid = local.enter_context(nc.sbuf_tensor("hid", [P, 2, HT, SEQ], F32R))
        w2 = local.enter_context(nc.sbuf_tensor("moe_halves", [P, 2, 2, TILE], F32R))
        zero = local.enter_context(nc.sbuf_tensor("zero_row", [1, 512], F32))
        up = lambda m: C.bank[m]
        body = ("up0", "down0", "down1", "up1", "up2", "up3")

        def number(e, i):
            return FIRST_UP + NT * (e - 1) + i

        def arrivals(e, i):
            return 16 * (e - 1) + 16 * ((FIRST_UP + i) // NT + 1)

        with nc.Block() as block:
            @block.sync
            def _(sp):
                for n in range(NT):
                    sp.dma_start(C.ring[:, n, :], A["moe"][n, :, :]).then_inc(S[f"loaded{n}"], 16)
                with sp.Fori(1, N_EXP) as e:
                    for i in range(NT):
                        sp.wait_ge(S["low"], NT * (e - 1) + i + 1)
                        sp.dma_start(C.ring[:, i, :], A["moe"][NT * e + i, :, :]).then_inc(S[f"loaded{i}"], 16)

            @block.tensor
            def _(pe):
                def halves(n2, k):
                    return [w2[:, n2, i, :].rearrange("p (k c) -> p k c", k=k) for i in range(2)]

                def up_tile(m, n2):
                    w = halves(n2, KT)
                    for i in range(2):
                        for k in range(KT):
                            ins = split_product(pe, up(m)[:, i * SEQ:(i + 1) * SEQ],
                                                [x[:, k, i * P:(i + 1) * P] for x in w],
                                                [x[:, k, :] for x in h2], k == 0, k == KT - 1)
                    ins.then_inc(S["tile"], 1)

                def down_tile(j, n2):
                    w = halves(n2, HT)
                    for q in range(4):
                        dt = 4 * j + q
                        out = C.bank[4 + dt // 2][:, (dt % 2) * SEQ:(dt % 2) * SEQ + SEQ]
                        for m in range(HT):
                            a = [x[:, m, q * P:(q + 1) * P] for x in w]
                            b = [hid[:, i, m, :] for i in range(2)]
                            for x, y in ((a[0], b[0]), (a[0], b[1]), (a[1], b[0])):
                                ins = pe.matmul(out, x, y, start=False, stop=False, skip_group_check=True)
                    ins.then_inc(S["tile"], 1)

                pe.wait_ge(S["zero"], 1)
                for b in range(4):
                    pe.matmul(C.bank[4 + b][:, :], zero[:, 0:P], zero[:, :], start=True, stop=False,
                              skip_group_check=True)
                for m in range(HT):
                    pe.wait_ge(S["low"], m + 1)
                    up_tile(m, m % 2)
                with pe.Fori(1, N_EXP) as e:
                    for i, what in enumerate(body):
                        if what == "down0":
                            pe.wait_ge(S["hid"], e * HT)
                        pe.wait_ge(S["low"], number(e, i) + 1)
                        if what.startswith("up"):
                            up_tile(int(what[-1]), i % 2)
                        else:
                            down_tile(int(what[-1]), i % 2)
                pe.wait_ge(S["hid"], N_EXP * HT)
                for j in range(2):
                    pe.wait_ge(S["low"], N_EXP * NT - 1 + j)
                    down_tile(j, j % 2)
                pe.matmul(C.bank[4][:, 0:P], zero[:, 0:P], zero[:, 0:P], start=False, stop=True,
                          skip_group_check=True).then_inc(S["done"], 1)

            @block.scalar
            def _(act):
                def high(slot, arrived, n2, used):
                    act.wait_ge(S[f"loaded{slot}"], arrived)
                    if used is not None:
                        act.wait_ge(S["tile"], used)
                    for c in COLUMNS:
                        act.activation(w2[:, n2, 0, c], C.ring[:, slot, c], ACT.Copy).then_inc(S["high"], 1)

                def silu(m, n):
                    act.wait_ge(S["tile"], n + 1)
                    act.activation(act_h[:, m, :], up(m)[:, 0:SEQ], ACT.Silu).then_inc(S["silu"], 1)

                def hidden_high(m, count):
                    act.wait_ge(S["hidden"], count)
                    act.activation(hid[:, 0, m, :], act_h[:, m, :], ACT.Copy).then_inc(S["hid_high"], 1)

                high(0, 16, 0, None)
                for m in range(HT):
                    high(m + 1, 16, (m + 1) % 2, m if m else None)
                    silu(m, m)
                    hidden_high(m, m + 1)
                with act.Fori(1, N_EXP) as e:
                    for i in range(NT):
                        high((FIRST_UP + i + 1) % NT, arrivals(e, i + 1), (i + 1) % 2, number(e, i))
                        if i == 2:
                            silu(0, number(e, 0))
                            act.wait_ge(S["tile"], number(e, 2) + 1)
                            hidden_high(0, e * HT + 1)
                        elif i > 2:
                            silu(i - 2, number(e, i))
                            hidden_high(i - 2, e * HT + i - 1)
                high(5, 16 * N_EXP, 1, N_EXP * NT - 2)

            @block.vector
            def _(dve):
                def low(slot, n2, n):
                    for i, c in enumerate(COLUMNS):
                        dve.wait_ge(S["high"], 2 * n + i + 1)
                        ins = dve.tensor_tensor(w2[:, n2, 1, c], C.ring[:, slot, c], w2[:, n2, 0, c].bitcast(F32),
                                                ALU.subtract)
                    ins.then_inc(S["low"], 1)

                def hidden(m, e, count):
                    dve.wait_ge(S["silu"], count)
                    dve.tensor_tensor(act_h[:, m, :], act_h[:, m, :], gate_all[:, e, :], ALU.mult)\
                       .then_inc(S["gated"], 1)
                    dve.wait_ge(S["gated"], count)
                    dve.tensor_tensor(act_h[:, m, :], act_h[:, m, :], up(m)[:, SEQ:2 * SEQ], ALU.mult)\
                       .then_inc(S["hidden"], 1)
                    dve.wait_ge(S["hid_high"], count)
                    dve.tensor_tensor(hid[:, 1, m, :], act_h[:, m, :], hid[:, 0, m, :].bitcast(F32), ALU.subtract)\
                       .then_inc(S["hid"], 1)

                dve.memset(zero[:, :], 0.0).then_inc(S["zero"], 1)
                low(0, 0, 0)
                for m in range(HT):
                    low(m + 1, (m + 1) % 2, m + 1)
                    hidden(m, 0, m + 1)
                with dve.Fori(1, N_EXP) as e:
                    for i in range(NT):
                        low((FIRST_UP + i + 1) % NT, (i + 1) % 2, number(e, i + 1))
                        if i == 2:
                            hidden(0, e, e * HT + 1)
                        elif i > 2:
                            hidden(i - 2, e, e * HT + i - 1)
                low(5, 1, N_EXP * NT - 1)
                dve.wait_ge(S["done"], 1)
                for k in range(KT):
                    S.link(dve, dve.scalar_tensor_tensor(
                        out=xT[:, k, :], in0=C.bank[4 + k // 2][:, (k % 2) * SEQ:(k % 2) * SEQ + SEQ],
                        scalar=m5[:, k:k + 1], in1=xT[:, k, :], op0=ALU.mult, op1=ALU.add), "x")
        S.close()


def first_block(C, A, xT):
    nc = C.nc
    with ExitStack() as outer:
        sb = lambda name, shape: outer.enter_context(nc.sbuf_tensor(name, shape, F32))
        mod = sb("mod", [P, 6 * KT, 2])
        g1 = sb("gain_x", [P, KT])
        gc = sb("gain_c", [P, KT])
        g2 = sb("gain_2", [P, KT])
        modulation(C, A, mod)
        gains(C, "gains", [(g1[:, :], C.v["norm1_g"], mod[:, KT:2 * KT, 0]),
                           (gc[:, :], C.v["norm1_g"], mod[:, KT:2 * KT, 1]),
                           (g2[:, :], C.v["norm2_g"], mod[:, 4 * KT:5 * KT, 0])])
        upper = outer.enter_context(ExitStack())
        su = lambda name, shape: upper.enter_context(nc.sbuf_tensor(name, shape, F32))
        gates = su("gates", [P, 2 * KT, SEQ])
        yab = su("yab", [P, 2 * PAIRS, SEQ])
        ya, yb = yab[:, 0:PAIRS, :], yab[:, PAIRS:2 * PAIRS, :]
        with ExitStack() as mid:
            sm = lambda name, shape: mid.enter_context(nc.sbuf_tensor(name, shape, F32))
            Z = {"r": sm("z_r", [P, PAIRS, SEQ]), "k": sm("z_k", [P, PAIRS, ALL]),
                 "v": sm("z_v", [P, 4, NH * HD]), "lw": sm("z_lw", [P, ALL]), "la": sm("z_la", [P, ALL]),
                 "lg": sm("z_lg", [P, SEQ]), "q": sm("z_q", [P, PAIRS, SEQ]), "kb": sm("z_kb", [P, PAIRS, ALL]),
                 "vb": sm("z_vb", [P, 4, NH * HD])}
            with ExitStack() as local:
                hs = local.enter_context(nc.sbuf_tensor("h1_halves", [P, 2, KT, ALL], F32R))
                h = (hs[:, 0, :, :], hs[:, 1, :, :])
                h1 = C.ring[:, 0:2, :].rearrange("p a (b c) -> p (a b) c", c=ALL)
                xc = C.ring[:, 2, :].rearrange("p (b c) -> p b c", c=CTX)
                load_all(nc, "context", [(xc, A["ctxT"])])
                norm(C, "norm1", [(xc, h1[:, :, 0:CTX], gc, mod[:, 0:KT, 1], CTX),
                                  (xT[:, :, :], h1[:, :, CTX:ALL], g1, mod[:, 0:KT, 0], SEQ)], 0)
                split(C, "split1", [(h1[:, k, :], h[0][:, k, :], h[1][:, k, :]) for k in range(KT)])
                jobs = []

                def turned(col, n, dst, lo, func=None):
                    for m in range(n // P):
                        c = col + m * P
                        jobs.append((c // 256, c % 256, P, True, h, lo, ALL - lo, dst[m], func, None))

                def straight(col, n, dst):
                    for m in range(n // 256):
                        for t in range(ALL // P):
                            jobs.append(((col + m * 256) // 256, 0, 256, False, h, t * P, P,
                                         dst[:, t, m * 256:(m + 1) * 256], None, None))

                per = lambda t, n: [t[:, i, :] for i in range(n)]
                turned(0, 512, per(Z["r"], PAIRS), CTX)
                turned(512, 512, per(Z["k"], PAIRS), 0)
                straight(1024, 512, Z["v"])
                turned(1536, 128, [Z["lw"][:, :]], 0, ACT.Tanh)
                turned(1664, 128, [Z["la"][:, :]], 0)
                turned(1792, 128, [Z["lg"][:, :]], CTX, ACT.Sigmoid)
                turned(2048, 512, per(Z["q"], PAIRS), CTX)
                turned(2560, 512, per(Z["kb"], PAIRS), 0)
                straight(3072, 512, Z["vb"])
                turned(3584, 2048, per(gates, 2 * KT), CTX, ACT.Sigmoid)
                linear(C, "w_in", [A["w_in"][i] for i in range(22)], jobs)
            head_norm(C, "q_norm", Z["q"], Z["q"], 0, C.v["q_g"], None, False)
            head_norm(C, "k_norm", Z["kb"], Z["kb"], 0, C.v["k_g"], None, False, cols=ALL)
            na_attention(C, A, Z, Z["q"], Z["kb"], yb)
            with ExitStack() as local:
                sl = lambda name, shape: local.enter_context(nc.sbuf_tensor(name, shape, F32))
                W = {"kk": Z["kb"], "a": sl("w_a", [P, 2, PAIRS, P]), "sig": sl("w_sig", [P, 2, NH * HD]),
                     "S0": sl("w_S0", [P, 2, PAIRS, P]),
                     "y": Z["vb"][:, :, :].rearrange("p a (b c) -> p (a b) c", c=SEQ)
                                          .rearrange("p (d a) c -> p d a c", d=2),
                     "wb": sl("lora_w", [P, NH * HD]), "ab": sl("lora_a", [P, NH * HD]),
                     "w0": sl("w0", [P, NH * HD])}
                rwkv_prep(C, Z, W, [(W["wb"][:, :], A["rw_w_lora_b"]), (W["ab"][:, :], A["rw_a_lora_b"]),
                                    (W["w0"][:, :], A["rw_w0"])])
                with ExitStack() as inner:
                    si = lambda name, shape: inner.enter_context(nc.sbuf_tensor(name, shape, F32))
                    B = {"qr": si("b_qr", [P, 2, PAIRS, 2 * P]), "bb": C.ring[:, 5, 0:8 * P].rearrange("p (d a c) -> p d a c", d=2, a=PAIRS),
                         "kn": C.ring[:, 5, 8 * P:16 * P].rearrange("p (d a c) -> p d a c", d=2, a=PAIRS), "btok": si("b_btok", [P, 2, NH * HD]),
                         "ktok": si("b_ktok", [P, 2, NH * HD]), "ein": si("b_ein", [P, 2, PAIRS, P]),
                         "eex": si("b_eex", [P, 2, PAIRS, P]), "eneg": si("b_eneg", [P, 2, PAIRS, P]),
                         "tmp": Z["q"][:, :, :].rearrange("p a (d c) -> p d a c", d=2),
                         "X": C.ring[:, 0:4, :].rearrange("p a (b c) -> p (a b) c", c=4 * P),
                         "PT": C.ring[:, 4, :].rearrange("p (b c) -> p b c", c=P),
                         "M": si("b_m", [P, 2 * NH, 2 * P])}
                    B["R"] = B["eex"][:, :, :, :].rearrange("p d a c -> p d (a c)")
                    B["nU"] = B["eneg"][:, :, :, :].rearrange("p d a c -> p d (a c)")
                    B["SW"] = si("b_sw", [P, PAIRS, P])
                    S = Stage(nc, "delta")
                    with nc.Block() as block:
                        @block.vector
                        def _(dve):
                            S.link(dve, dve.memset(W["S0"][:, :, :, :], 0.0), "state")
                    S.close()
                    for step in range(4):
                        rwkv_tile(C, Z, W, step, B)
                S = Stage(nc, "directions")
                with nc.Block() as block:
                    @block.vector
                    def _(dve):
                        S.link(dve, dve.tensor_tensor(ya[:, :, :], W["y"][:, 0, :, :], W["y"][:, 1, :, :], ALU.add), "y")
                S.close()
            head_norm(C, "y_norm", ya, ya, 1, C.v["ln_g"], C.v["ln_b"], True)
            rwkv_bonus(C, A, Z, None, ya)
        with ExitStack() as local:
            sl = lambda name, shape, dt=F32: local.enter_context(nc.sbuf_tensor(name, shape, dt))
            pab = sl("p_ab", [P, 2 * KT, SEQ])
            ys = sl("y_halves", [P, 2, KT, SEQ], F32R)
            jobs = []
            for i in range(2):
                y = (ys[:, 0, i * PAIRS:(i + 1) * PAIRS, :], ys[:, 1, i * PAIRS:(i + 1) * PAIRS, :])
                for m in range(KT):
                    jobs.append((2 * i + m // 4, P * (m % 4), P, True, y, 0, SEQ,
                                 pab[:, i * KT + m, :], None, gates[:, i * KT + m, :]))

            def merge(S, dve):
                S.link(dve, dve.tensor_tensor(pab[:, 0:KT, :], pab[:, 0:KT, :], pab[:, KT:2 * KT, :], ALU.add), "merged")

            linear(C, "proj", [A["proj_ab"][i] for i in range(4)], jobs, kt=4, extra=merge, pairs=channel_tiles(yab, ys))
            jobs = [(m // 2, P * (m % 2), P, True, (ys[:, 0, :, :], ys[:, 1, :, :]), 0, SEQ, pab[:, KT + m, :], None,
                     None) for m in range(KT)]

            def residual(S, dve):
                for k in range(KT):
                    S.link(dve, dve.scalar_tensor_tensor(out=xT[:, k, :], in0=pab[:, KT + k, :],
                                                         scalar=mod[:, 2 * KT + k:2 * KT + k + 1, 0],
                                                         in1=xT[:, k, :], op0=ALU.mult, op1=ALU.add), "x")
            linear(C, "w_out", [A["w_out"][i] for i in range(4)], jobs, extra=residual,
                   pairs=channel_tiles(pab, ys))
        upper.close()
        with ExitStack() as local:
            sl = lambda name, shape, dt=F32: local.enter_context(nc.sbuf_tensor(name, shape, dt))
            h2 = sl("h2", [P, KT, SEQ])
            hs = sl("h2_halves", [P, 2, KT, SEQ], F32R)
            gate_all = sl("gate_all", [P, N_EXP, SEQ])
            m5 = sl("m5", [P, KT])
            norm(C, "norm2", [(xT[:, :, :], h2[:, :, :], g2, mod[:, 3 * KT:4 * KT, 0], SEQ)], 0)
            router(C, A, h2, gate_all, mod, m5, channel_tiles(h2, hs))
            experts(C, A, (hs[:, 0, :, :], hs[:, 1, :, :]), gate_all, xT, m5)


H4 = 4
MIX = H4 * HD
N_CMP = (SEQ - 32) // 16 + 1
GATHERED = 8
TOPK = 16
PH = 8
KEYS = 128
DN_ALPHA = 4.0 ** 0.25
TILES2 = 29


def stick_breaking(C, A, Z, out):
    nc = C.nc
    S = Stage(nc, "stick")
    scale = HD ** -0.5
    with ExitStack() as local:
        sb = lambda name: local.enter_context(nc.sbuf_tensor(name, [P, H4, TT * SEQ], F32))
        z, l = sb("sb_z"), sb("sb_l")
        mask = local.enter_context(nc.sbuf_tensor("sb_mask", [P, TT * SEQ], F32))
        with nc.Block() as block:
            @block.sync
            def _(sp):
                sp.dma_start(mask[:, :], A["causal"]).then_inc(S["mask"], 16)

            @block.tensor
            def _(pe):
                for h in range(H4):
                    r, p = slice(HD * (h % 2), HD * (h % 2) + HD), h // 2
                    for s in range(TT):
                        ins = pe.matmul(C.bank[h][:, s * SEQ:(s + 1) * SEQ], Z["sk"][r, p, s * P:(s + 1) * P],
                                        Z["sq"][r, p, :], start=True, stop=True)
                    ins.then_inc(S["z"], 1)
                for h in range(H4):
                    pe.wait_ge(S["softplus"], h + 1)
                    lo, hi = l[:, h, 0:SEQ], l[:, h, SEQ:2 * SEQ]
                    product(pe, C.bank[4 + h][:, 0:SEQ], [(C.sq["neg_ge"], lo), (C.sq["neg_ones"], hi)])
                    product(pe, C.bank[4 + h][:, SEQ:2 * SEQ], [(C.sq["neg_ge"], hi)]).then_inc(S["sums"], 1)
                for h in range(H4):
                    pe.wait_ge(S["weights"], h + 1)
                    r = slice(HD * (h % 2), HD * (h % 2) + HD)
                    product(pe, C.bank[h][r, 0:SEQ], [(Z["sv"][:, s, h * HD:(h + 1) * HD],
                                                       l[:, h, s * SEQ:(s + 1) * SEQ]) for s in range(TT)])\
                        .then_inc(S["o"], 1)

            @block.scalar
            def _(act):
                for h in range(H4):
                    act.wait_ge(S["z"], h + 1)
                    act.activation(z[:, h, :], C.bank[h][:, :], ACT.Copy, scale=scale).then_inc(S["z_out"], 1)
                    S.link(act, act.activation(l[:, h, :], C.bank[h][:, :], ACT.Abs, scale=scale), "abs")
                for h in range(H4):
                    S.link(act, act.activation(l[:, h, :], l[:, h, :], ACT.Exp, scale=-1.0), "exp")
                for h in range(H4):
                    act.activation(l[:, h, :], l[:, h, :], ACT.Ln, bias=C.eps[3]).then_inc(S["log"], 1)
                for h in range(H4):
                    act.wait_ge(S["log_w"], h + 1)
                    act.activation(l[:, h, :], z[:, h, :], ACT.Exp).then_inc(S["w"], 1)
                for h in range(H4):
                    r, p = slice(HD * (h % 2), HD * (h % 2) + HD), h // 2
                    act.wait_ge(S["o"], h + 1)
                    act.activation(out[r, p, :], C.bank[h][r, 0:SEQ], ACT.Copy).then_inc(S["out"], 1)

            @block.vector
            def _(dve):
                dve.wait_ge(S["mask"], 16)
                for h in range(H4):
                    dve.wait_ge(S["log"], h + 1)
                    S.link(dve, dve.scalar_tensor_tensor(out=l[:, h, :], in0=z[:, h, :], scalar=0.0, in1=l[:, h, :],
                                                         op0=ALU.max, op1=ALU.add), "sp")
                    dve.tensor_tensor(l[:, h, :], l[:, h, :], mask[:, :], ALU.mult).then_inc(S["softplus"], 1)
                for h in range(H4):
                    dve.wait_ge(S["sums"], h + 1)
                    S.link(dve, dve.tensor_tensor(z[:, h, :], z[:, h, :], C.bank[4 + h][:, :], ALU.add), "added")
                    dve.tensor_scalar(z[:, h, :], z[:, h, :], 0.0, None, ALU.min).then_inc(S["log_w"], 1)
                for h in range(H4):
                    dve.wait_ge(S["w"], h + 1)
                    dve.tensor_tensor(l[:, h, :], l[:, h, :], mask[:, :], ALU.mult).then_inc(S["weights"], 1)
        S.close()


def nsa(C, A, l_, Z, out):
    nc = C.nc
    S = Stage(nc, "nsa")
    scale = HD ** -0.5
    units = [(t, h) for t in range(TT) for h in range(H4)]
    N = len(units)
    NC = N_CMP
    with ExitStack() as local:
        sb = lambda name, shape: local.enter_context(nc.sbuf_tensor(name, shape, F32))
        wkv = sb("cmp_w", [HD, 2, 32, HD])
        pos = sb("cmp_pos", [HD, 32])
        blk = sb("cmp_blocks", [HD, 2, 32, NC])
        kc = sb("cmp_k", [HD, NC])
        vc = sb("cmp_v", [NC, HD])
        cb = sb("cmp_bias", [P, N, NC])
        seen = sb("cmp_seen", [P, TT])
        lb = sb("lin_bias", [P, N, SEQ])
        pc = sb("cmp_p", [P, N, NC])
        cm = sb("cmp_max", [P, N])
        pcT = sb("cmp_pT", [NC, N * P])
        sc = sb("nsa_s", [P, 3, 2 * SEQ])
        pT = sb("nsa_pT", [P, 2, 4 * P])
        mx = sb("nsa_max", [P, N, 2])
        rs = sb("nsa_sum", [P, N, 2])
        with nc.Block() as block:
            @block.sync
            def _(sp):
                for dst, src in ((wkv[:, :, :, :], A["cmp_w"][l_, :, :, :, :]), (pos[:, :], A["cmp_pos"][l_, :, :]),
                                 (cb[:, :, :], A["cmp_bias"]), (seen[:, :], A["cmp_seen"]), (lb[:, :, :], A["lin_bias"])):
                    sp.dma_start(dst, src).then_inc(S["loaded"], 16)

            @block.tensor
            def _(pe):
                pe.wait_ge(S["loaded"], 80)
                pe.wait_ge(S["blocks"], 4)
                product(pe, C.bank[6][0:HD, 0:NC], [(wkv[:, 0, i, :], blk[:, 0, i, :]) for i in range(32)])\
                    .then_inc(S["kc"], 1)
                product(pe, C.bank[7][0:NC, 0:HD], [(blk[:, 1, i, :], wkv[:, 1, i, :]) for i in range(32)])\
                    .then_inc(S["vc"], 1)
                pe.wait_ge(S["kv_out"], 2)
                for n, (t, h) in enumerate(units):
                    ins = pe.matmul(C.bank[6][:, n * NC:(n + 1) * NC], Z["nq"][:, h, t * P:(t + 1) * P], kc[:, :],
                                    start=True, stop=True)
                ins.then_inc(S["cmp_scores"], 1)
                pe.wait_ge(S["cmp_p"], 1)
                for n in range(N):
                    ins = pe.transpose(C.bank[6 + n // 4][0:NC, (n % 4) * P:(n % 4) * P + P], pc[:, n, :], C.sq["ident"])
                ins.then_inc(S["cmp_turned"], 1)
                pe.wait_ge(S["cmp_pT"], 1)

                def scores(n):
                    t, h = units[n]
                    if n >= 2:
                        pe.wait_ge(S["biased"], n - 1)
                    for b in range(2):
                        ins = pe.matmul(C.bank[n % 2][:, b * SEQ:(b + 1) * SEQ], Z["nq"][:, h, t * P:(t + 1) * P],
                                        Z["nk"][:, b, :], start=True, stop=True)
                    ins.then_inc(S["scores"], 1)

                def mix(n):
                    t, h = units[n]
                    r = slice(HD * (h % 2), HD * (h % 2) + HD)
                    pe.wait_ge(S["turned_out"], n + 1)
                    if n >= 2:
                        pe.wait_ge(S["out"], n - 1)
                    product(pe, C.bank[4 + n % 2][r, 0:P],
                            [(vc[:, :], pcT[:, n * P:(n + 1) * P])] +
                            [(Z["nv"][:, k % 2, (k // 2) * HD:(k // 2 + 1) * HD], pT[:, n % 2, k * P:(k + 1) * P])
                             for k in range(4)]).then_inc(S["mixed"], 1)

                scores(0)
                scores(1)
                for n, (t, h) in enumerate(units):
                    r = slice(HD * (h % 2), HD * (h % 2) + HD)
                    if n + 2 < N:
                        scores(n + 2)
                    pe.wait_ge(S["probs"], 2 * n + 2)
                    if n >= 2:
                        pe.wait_ge(S["turned_out"], n - 1)
                    for k in range(4):
                        ins = pe.transpose(C.bank[2 + n % 2][:, k * P:(k + 1) * P], sc[:, n % 3, k * P:(k + 1) * P],
                                           C.sq["ident"])
                    ins.then_inc(S["turned"], 1)
                    if n:
                        mix(n - 1)
                mix(N - 1)

            @block.scalar
            def _(act):
                act.wait_ge(S["kc"], 1)
                act.activation(kc[:, :], C.bank[6][0:HD, 0:NC], ACT.Copy).then_inc(S["kv_out"], 1)
                act.wait_ge(S["vc"], 1)
                act.activation(vc[:, :], C.bank[7][0:NC, 0:HD], ACT.Copy).then_inc(S["kv_out"], 1)
                act.wait_ge(S["cmp_s"], 1)
                act.activation(pc[:, :, :], pc[:, :, :], ACT.Exp).then_inc(S["cmp_exp"], 1)
                act.wait_ge(S["cmp_turned"], 1)
                for i in range(2):
                    ins = act.activation(pcT[:, i * 512:(i + 1) * 512], C.bank[6 + i][0:NC, :], ACT.Copy)
                ins.then_inc(S["cmp_pT"], 1)
                def exp(n):
                    act.wait_ge(S["max"], n + 1)
                    for b in range(2):
                        half = sc[:, n % 3, b * SEQ:(b + 1) * SEQ]
                        ins = act.activation(half, half, ACT.Exp, bias=mx[:, n, b:b + 1], accum_out=rs[:, n, b:b + 1])
                    ins.then_inc(S["exp"], 1)

                exp(0)
                for n in range(N):
                    if n + 1 < N:
                        exp(n + 1)
                    act.wait_ge(S["turned"], n + 1)
                    S.wait(act, "mixed", n - 1)
                    act.activation(pT[:, n % 2, :], C.bank[2 + n % 2][:, :], ACT.Copy).then_inc(S["turned_out"], 1)

            @block.vector
            def _(dve):
                L = lambda ins: S.link(dve, ins, "vector")
                dve.wait_ge(S["loaded"], 80)
                for b in range(2):
                    rows = Z["kcv"][:, b, :].rearrange("d (c i) -> d i c", i=16)
                    for a in range(2):
                        i = slice(16 * a, 16 * a + 16)
                        dve.tensor_tensor(blk[:, b, i, :], rows[:, :, a:a + NC],
                                          pos[:, i].unsqueeze(2).broadcast_to([HD, 16, NC]), ALU.add)\
                           .then_inc(S["blocks"], 1)
                dve.wait_ge(S["cmp_scores"], 1)
                wide = lambda a: a.unsqueeze(2).broadcast_to([P, N, NC])
                L(dve.scalar_tensor_tensor(out=pc[:, :, :].rearrange("p n c -> p (n c)"), in0=C.bank[6][:, 0:N * NC], scalar=scale, in1=cb[:, :, :].rearrange("p n c -> p (n c)"), op0=ALU.mult, op1=ALU.add))
                L(dve.tensor_reduce(cm[:, :], pc[:, :, :], AX, ALU.max))
                dve.tensor_tensor(pc[:, :, :], pc[:, :, :], wide(cm[:, :]), ALU.subtract).then_inc(S["cmp_s"], 1)
                dve.wait_ge(S["cmp_exp"], 1)
                L(dve.tensor_reduce(cm[:, :], pc[:, :, :], AX, ALU.add))
                L(dve.reciprocal(cm[:, :], cm[:, :]))
                for t in range(TT):
                    g = Z["ng"][:, t, 0:12].rearrange("p (h b) -> p h b", b=3)[:, :, 0]
                    c4 = cm[:, 4 * t:4 * t + 4]
                    L(dve.scalar_tensor_tensor(out=c4, in0=c4, scalar=seen[:, t:t + 1], in1=g, op0=ALU.mult, op1=ALU.mult))
                dve.tensor_tensor(pc[:, :, :], pc[:, :, :], wide(cm[:, :]), ALU.mult).then_inc(S["cmp_p"], 1)

                def begin(n):
                    dve.wait_ge(S["scores"], n + 1)
                    S.wait(dve, "turned", n - 2)
                    s2 = sc[:, n % 3, :].rearrange("p (b k) -> p b k", b=2)
                    S.link(dve, dve.scalar_tensor_tensor(
                        out=s2, in0=C.bank[n % 2][:, :].rearrange("p (b k) -> p b k", b=2), scalar=scale,
                        in1=lb[:, n, :].unsqueeze(1).broadcast_to([P, 2, SEQ]), op0=ALU.mult, op1=ALU.add), "biased")
                    S.link(dve, dve.tensor_reduce(mx[:, n, :], s2, AX, ALU.max), "reduced")
                    dve.tensor_scalar(mx[:, n, :], mx[:, n, :], -1.0, None, ALU.mult).then_inc(S["max"], 1)

                def take(n):
                    t, h = units[n]
                    dve.wait_ge(S["mixed"], n + 1)
                    r = slice(HD * (h % 2), HD * (h % 2) + HD)
                    dve.tensor_copy(out[r, h // 2, t * P:(t + 1) * P], C.bank[4 + n % 2][r, 0:P]).then_inc(S["out"], 1)

                begin(0)
                begin(1)
                for n, (t, h) in enumerate(units):
                    dve.wait_ge(S["exp"], n + 1)
                    L(dve.reciprocal(rs[:, n, :], rs[:, n, :]))
                    L(dve.tensor_tensor(rs[:, n, :], rs[:, n, :], Z["ng"][:, t, 3 * h + 1:3 * h + 3], ALU.mult))
                    for b in range(2):
                        half = sc[:, n % 3, b * SEQ:(b + 1) * SEQ]
                        dve.tensor_scalar(half, half, rs[:, n, b:b + 1], None, ALU.mult).then_inc(S["probs"], 1)
                    if n + 2 < N:
                        begin(n + 2)
                    if n >= 2:
                        take(n - 2)
                take(N - 2)
                take(N - 1)
        S.close()


def retention(C, A, Z, out):
    nc = C.nc
    S = Stage(nc, "retention")
    with ExitStack() as local:
        dec = local.enter_context(nc.sbuf_tensor("ret_decay", [P, H4, TT * SEQ], F32))
        w = local.enter_context(nc.sbuf_tensor("ret_w", [P, H4, TT * SEQ], F32))
        with nc.Block() as block:
            @block.sync
            def _(sp):
                sp.dma_start(dec[:, :, :], A["ret_decay"]).then_inc(S["decay"], 16)

            @block.tensor
            def _(pe):
                for h in range(H4):
                    r, p = slice(HD * (h % 2), HD * (h % 2) + HD), h // 2
                    for s in range(TT):
                        ins = pe.matmul(C.bank[h][:, s * SEQ:(s + 1) * SEQ], Z["rk"][r, p, s * P:(s + 1) * P],
                                        Z["rq"][r, p, :], start=True, stop=True)
                    ins.then_inc(S["scores"], 1)
                for h in range(H4):
                    pe.wait_ge(S["weights"], h + 1)
                    r = slice(HD * (h % 2), HD * (h % 2) + HD)
                    product(pe, C.bank[4 + h][r, 0:SEQ], [(Z["rv"][:, s, h * HD:(h + 1) * HD],
                                                           w[:, h, s * SEQ:(s + 1) * SEQ]) for s in range(TT)])\
                        .then_inc(S["o"], 1)

            @block.vector
            def _(dve):
                dve.wait_ge(S["decay"], 16)
                for h in range(H4):
                    dve.wait_ge(S["scores"], h + 1)
                    dve.tensor_tensor(w[:, h, :], C.bank[h][:, :], dec[:, h, :], ALU.mult).then_inc(S["weights"], 1)

            @block.scalar
            def _(act):
                for h in range(H4):
                    r, p = slice(HD * (h % 2), HD * (h % 2) + HD), h // 2
                    act.wait_ge(S["o"], h + 1)
                    act.activation(out[r, p, :], C.bank[4 + h][r, 0:SEQ], ACT.Copy).then_inc(S["out"], 1)
        S.close()


def gla(C, A, l_, Z, out):
    nc = C.nc
    S = Stage(nc, "gla")
    NCH = SEQ // CH
    dk = 32
    with ExitStack() as local:
        sb = lambda name, shape: local.enter_context(nc.sbuf_tensor(name, shape, F32))
        wa = sb("gla_wa", [17, P])
        hm = sb("gla_heads", [P, H4])
        bd = sb("gla_blocks", [P, MIX])
        la = sb("gla_log", [P, TT, P])
        lt = sb("gla_tmp", [P, TT, P])
        e1, en, eb, et = (sb(f"gla_e{i}", [P, SEQ]) for i in range(4))
        k1 = sb("gla_k", [P, H4, SEQ])
        att = sb("gla_att", [P, TT, H4, P])
        st = sb("gla_state", [P, NCH, MIX])
        up = sb("gla_update", [P, MIX])
        with nc.Block() as block:
            @block.sync
            def _(sp):
                for dst, src in ((wa[:, :], A["gla_wa"][l_, :, :]), (hm[:, :], A["gla_heads"]), (bd[:, :], A["gla_blocks"])):
                    sp.dma_start(dst, src).then_inc(S["loaded"], 16)

            @block.tensor
            def _(pe):
                pe.wait_ge(S["loaded"], 48)
                for t in range(TT):
                    ins = pe.matmul(C.bank[0][:, t * P:(t + 1) * P], Z["lr"][0:17, t * P:(t + 1) * P], wa[:, :],
                                    start=True, stop=True)
                ins.then_inc(S["alpha"], 1)
                pe.wait_ge(S["log_a"], 1)
                for t in range(TT):
                    c = slice(t * P, (t + 1) * P)
                    pe.matmul(C.bank[1][:, c], la[:, t, :], C.sq["gla_mid"], start=True, stop=True)
                    pe.matmul(C.bank[2][:, c], la[:, t, :], C.sq["gla_in"], start=True, stop=True)
                    ins = pe.matmul(C.bank[3][:, c], C.sq["gla_tail"], la[:, t, :], start=True, stop=True)
                ins.then_inc(S["sums"], 1)
                pe.wait_ge(S["k1"], H4)
                for t in range(TT):
                    for h in range(H4):
                        ins = pe.matmul(C.bank[4 + t][:, h * P:(h + 1) * P], k1[:, h, t * P:(t + 1) * P],
                                        e1[:, t * P:(t + 1) * P], start=True, stop=True)
                ins.then_inc(S["pairs"], 1)
                for c in range(NCH - 1):
                    t, r = c // 2, slice(CH * (c % 2), CH * (c % 2) + CH)
                    if c >= 2:
                        pe.wait_ge(S["update"], c - 1)
                    pe.matmul(C.bank[6 + c % 2][:, 0:MIX], et[r, t * P:(t + 1) * P], Z["gv"][r, t, :],
                              start=True, stop=True).then_inc(S["outer"], 1)
                pe.wait_ge(S["att"], TT)
                for c in range(NCH):
                    t, off = c // 2, CH * (c % 2)
                    S.wait(pe, "state", c + 1)
                    for h in range(H4):
                        r, p = slice(HD * (h % 2), HD * (h % 2) + HD), h // 2
                        o = C.bank[0][r, p * SEQ + c * CH:p * SEQ + (c + 1) * CH]
                        ins = product(pe, o, [(st[:, c, h * HD:(h + 1) * HD], eb[:, c * CH:(c + 1) * CH]),
                                              (Z["gv"][:, t, h * HD:(h + 1) * HD], att[:, t, h, off:off + CH])])
                ins.then_inc(S["o"], 1)

            @block.scalar
            def _(act):
                flat = lt[:, :, :].rearrange("p t c -> p (t c)")
                act.wait_ge(S["alpha"], 1)
                S.link(act, act.activation(flat, C.bank[0][:, 0:SEQ], ACT.Abs), "a")
                S.link(act, act.activation(flat, flat, ACT.Exp, scale=-1.0), "a")
                act.activation(flat, flat, ACT.Ln, bias=C.eps[3]).then_inc(S["softplus"], 1)
                act.wait_ge(S["sums"], 1)
                for dst, b, scale in ((e1, 1, 1.0), (en, 1, -1.0), (eb, 2, 1.0), (et, 3, 1.0)):
                    act.activation(dst[:, :], C.bank[b][:, 0:SEQ], ACT.Exp, scale=scale).then_inc(S["exps"], 1)
                act.wait_ge(S["o"], 1)
                act.activation(out[:, :, :].rearrange("p a t -> p (a t)"), C.bank[0][:, :], ACT.Copy).then_inc(S["out"], 1)

            @block.vector
            def _(dve):
                L = lambda ins: S.link(dve, ins, "vector")
                flat = lambda a: a[:, :, :].rearrange("p t c -> p (t c)")
                L(dve.memset(st[:, 0, :], 0.0))
                dve.wait_ge(S["loaded"], 48)
                dve.wait_ge(S["softplus"], 1)
                dve.scalar_tensor_tensor(out=flat(la), in0=C.bank[0][:, 0:SEQ], scalar=0.0, in1=flat(lt),
                                         op0=ALU.min, op1=ALU.subtract).then_inc(S["log_a"], 1)
                dve.wait_ge(S["exps"], 4)
                L(dve.tensor_copy(lt[:, 0, 0:NCH], eb[:, CH - 1:SEQ:CH]))
                L(dve.tensor_tensor(en[:, :], en[:, :], Z["gk"][:, :], ALU.mult))
                L(dve.scalar_tensor_tensor(out=e1[:, :], in0=e1[:, :], scalar=dk ** -0.5, in1=Z["gq"][:, :],
                                           op0=ALU.mult, op1=ALU.mult))
                L(dve.scalar_tensor_tensor(out=eb[:, :], in0=eb[:, :], scalar=dk ** -0.5, in1=Z["gq"][:, :],
                                           op0=ALU.mult, op1=ALU.mult))
                L(dve.tensor_tensor(et[:, :], et[:, :], Z["gkt"][:, :, :].rearrange("p t c -> p (t c)"), ALU.mult))
                for h in range(H4):
                    dve.tensor_scalar(k1[:, h, :], en[:, :], hm[:, h:h + 1], None, ALU.mult).then_inc(S["k1"], 1)
                dve.wait_ge(S["pairs"], 1)
                for t in range(TT):
                    dve.tensor_tensor(att[:, t, :, :], C.bank[4 + t][:, :].rearrange("p (h c) -> p h c", h=H4),
                                      C.sq["m_fwd_in"].unsqueeze(1).broadcast_to([P, H4, P]), ALU.mult)\
                       .then_inc(S["att"], 1)
                S.link(dve, dve.tensor_copy(st[:, 0, :], st[:, 0, :]), "state")
                for c in range(NCH - 1):
                    dve.wait_ge(S["outer"], c + 1)
                    S.link(dve, dve.tensor_tensor(up[:, :], C.bank[6 + c % 2][:, 0:MIX], bd[:, :], ALU.mult), "update")
                    S.link(dve, dve.scalar_tensor_tensor(out=st[:, c + 1, :], in0=st[:, c, :], scalar=lt[:, 0, c:c + 1],
                                                         in1=up[:, :], op0=ALU.mult, op1=ALU.add), "state")
        S.close()


def times(C, name, rows):
    S = Stage(C.nc, name)
    with C.nc.Block() as block:
        @block.vector
        def _(dve):
            for a, b in rows:
                S.link(dve, dve.tensor_tensor(a, a, b, ALU.mult), "product")
    S.close()


def peer(C, A, l_, qv, x1, offset):
    nc = C.nc
    S = Stage(nc, "peer")
    U = TT * PH
    U2 = 2 * U
    GROUPS = U2 // 4
    NG = GATHERED
    PER = TOPK // NG
    DIAGONALS = (0, 4)
    CLEARED = 1
    flat = lambda n: C.ring[:, n, :]
    keys = flat(0).rearrange("p (h c) -> p h c", c=KEYS)
    s = C.ring[:, 1:3, :].rearrange("p a (u c) -> p (a u) c", c=KEYS)
    xtok = flat(3).rearrange("p (t c) -> p t c", t=TT)
    y = flat(4).rearrange("p (t c) -> p t c", t=TT)
    diag = flat(5).rearrange("p (k c) -> p k c", k=TOPK)
    with ExitStack() as local:
        sb = lambda name, shape, dt=F32: local.enter_context(nc.sbuf_tensor(name, shape, dt))
        ub = sb("u_rows", [P, NG, D])
        vb = sb("v_rows", [P, NG, D])
        junk = sb("u_junk", [P, D])
        zero = sb("peer_zero", [1, 512])
        top = sb("peer_top", [P, 2, TOPK])
        ti = sb("peer_ti", [P, 2, TOPK], U32)
        tf = sb("peer_tf", [P, 2, TOPK])
        cand = sb("peer_cand", [P, TOPK * TOPK])
        bi = sb("peer_bi", [P, TOPK], U32)
        part = sb("peer_part", [P, 2, TOPK], U32)
        pf = sb("peer_pf", [P, 2, TOPK])
        iota = sb("peer_iota", [P, TOPK])
        gate = sb("peer_gate", [P, U, TOPK])
        score = sb("peer_score", [P, 2, KEYS])
        chosen = sb("peer_chosen", [P, TOPK])
        den = sb("peer_den", [P, 1])
        still = sb("search_still", [1, 64])
        index = sb("peer_index", [P, U, TOPK], U32)
        acts = sb("peer_act", [P, 2, TOPK])
        wts = sb("peer_wts", [P, TOPK])
        gi = sb("peer_gi", [P, 2, TOPK], U32)
        idle = sb("gather_idle", [1, 1 + 2 * TOPK])
        with nc.Block() as block:
            @block.sync
            def _(sp):
                sp.dma_start(keys, A["peer_keys"][l_, :, :, :]).then_inc(S["keys"], 16)

            @block.gpsimd
            def _(pool):
                def gather(name, table, rows, done, first_done, i, k, first):
                    slot = k % NG
                    if not (first and k < NG):
                        pool.wait_ge(S[done], first_done + (k - NG + 1))
                        cell = 1 + k + (TOPK if name == "v" else 0)
                        pool.tensor_tensor(idle[:, cell:cell + 1], idle[:, 0:1], idle[:, 0:1], ALU.mult)
                    pool.indirect_dma_start(
                        out=rows[:, slot, :], out_offset=None, in_=table,
                        in_offset=bass.IndirectOffsetOnAxis(ap=gi[:, i, k:k + 1], axis=0))\
                        .then_inc(S[f"{name}{slot}"], 16)

                def head(g, i, first):
                    pool.wait_ge(S["found"], g + 1)
                    pool.tensor_copy(gi[:, i, :], index[:, g, :]).then_inc(S["index"], 1)
                    pool.wait_ge(S["index"], g + 1)
                    for k in range(TOPK):
                        gather("u", A["peer_u"], ub, "dots", TOPK * g, i, k, first)
                    for k in range(TOPK):
                        gather("v", A["peer_v"], vb, "sums", TOPK * g + CLEARED, i, k, first)

                pool.iota(iota[:, :], pattern=[[1, TOPK]], base=0, channel_multiplier=0,
                          allow_small_or_imprecise_dtypes=True).then_inc(S["iota"], 1)
                S.link(pool, pool.memset(idle[:, :], 0.0), "idle")
                head(0, 0, True)
                head(1, 1, False)
                with pool.Fori(1, U // 2) as m:
                    head(2 * m, 0, False)
                    head(2 * m + 1, 1, False)

            @block.tensor
            def _(pe):
                pe.wait_ge(S["keys"], 16)
                for g in range(GROUPS):
                    if g >= 4:
                        pe.wait_ge(S["scores_out"], g - 3)
                    for i in range(4):
                        u = 4 * g + i
                        t, hp = u // (2 * PH), u % (2 * PH)
                        ins = pe.matmul(C.bank[g % 4][:, i * P:(i + 1) * P], qv[:, hp, t * P:(t + 1) * P],
                                        keys[:, hp, :], start=True, stop=True)
                    ins.then_inc(S["scores"], 1)
                for t in range(TT):
                    for k in range(KT):
                        ins = pe.transpose(C.bank[4 + 2 * t + k // 4][:, (k % 4) * P:(k % 4) * P + P],
                                           x1[:, k, t * P:(t + 1) * P], C.sq["ident"])
                ins.then_inc(S["x_turned"], 1)
                pe.wait_ge(S["scores_out"], GROUPS)
                pe.wait_ge(S["zero"], 1)
                for b in range(2 * TT):
                    ins = pe.matmul(C.bank[b][:, :], zero[:, 0:P], zero[:, :], start=True, stop=False,
                                    skip_group_check=True)
                ins.then_inc(S["sums"], CLEARED)
                for t in range(TT):
                    with pe.Fori(t * PH, (t + 1) * PH) as g:
                        for k in range(TOPK):
                            if k in DIAGONALS:
                                pe.wait_ge(S["diag"], 2 * g + DIAGONALS.index(k) + 1)
                            pe.wait_ge(S[f"v{k % NG}"], PER * 16 * g + 16 * (k // NG + 1))
                            for c in range(2):
                                ins = pe.matmul(C.bank[2 * t + c][:, :], diag[:, k, :],
                                                vb[:, k % NG, c * 512:(c + 1) * 512], start=False, stop=False,
                                                skip_group_check=True)
                            ins.then_inc(S["sums"], 1)
                    ins = pe.matmul(C.bank[2 * t][:, 0:P], zero[:, 0:P], zero[:, 0:P], start=False, stop=True,
                                    skip_group_check=True)
                    ins.then_inc(S["tile"], 1)
                    pe.wait_ge(S["x_out"], 4)
                    pe.wait_ge(S["y"], 2 * t + 2)
                    for k in range(KT):
                        ins = pe.transpose(C.bank[4 + k // 2][:, (k % 2) * SEQ + t * P:(k % 2) * SEQ + (t + 1) * P],
                                           y[:, t, k * P:(k + 1) * P], C.sq["ident"])
                ins.then_inc(S["y_turned"], 1)

            @block.scalar
            def _(act):
                for g in range(GROUPS):
                    act.wait_ge(S["scores"], g + 1)
                    act.activation(s[:, 4 * g:4 * g + 4, :].rearrange("p a c -> p (a c)"), C.bank[g % 4][:, :], ACT.Copy)\
                       .then_inc(S["scores_out"], 1)
                act.wait_ge(S["x_turned"], 1)
                for i in range(4):
                    act.activation(xtok[:, i // 2, (i % 2) * 512:(i % 2) * 512 + 512], C.bank[4 + i][:, :], ACT.Copy)\
                       .then_inc(S["x_out"], 1)
                for t in range(TT):
                    with act.Fori(t * PH, (t + 1) * PH) as g:
                        act.wait_ge(S["found"], g + 1)
                        act.activation(gate[:, g, :], gate[:, g, :], ACT.Exp).then_inc(S["exp"], 1)
                        act.wait_ge(S["dots"], TOPK * g + TOPK)
                        act.activation(acts[:, 1, :], acts[:, 0, :], ACT.Gelu).then_inc(S["gelu"], 1)
                    act.wait_ge(S["tile"], t + 1)
                    for c in range(2):
                        act.activation(y[:, t, c * 512:(c + 1) * 512], C.bank[2 * t + c][:, :], ACT.Copy)\
                           .then_inc(S["y"], 1)

            @block.vector
            def _(dve):
                steps = {}

                def search(g):
                    count = [0]

                    def step(ins):
                        ins.then_inc(S["search"], 1)
                        count[0] += 1

                    def settle():
                        dve.wait_ge(S["search"], steps.get("unit", 0) * g + count[0])

                    def pause():
                        settle()
                        dve.tensor_tensor(still[:, count[0]:count[0] + 1], still[:, 0:1], still[:, 0:1], ALU.mult)

                    def best(rows):
                        a, b = slice(0, 8), slice(8, 16)
                        for score, value, place in rows:
                            step(dve.max(value[:, a], score))
                        pause()
                        for score, value, place in rows:
                            step(dve.max_index(place[:, a], value[:, a], score))
                        pause()
                        for score, value, place in rows:
                            step(dve.match_replace(score, value[:, a], score, NEG))
                        pause()
                        for score, value, place in rows:
                            step(dve.max(value[:, b], score))
                        pause()
                        for score, value, place in rows:
                            step(dve.max_index(place[:, b], value[:, b], score))
                        settle()

                    for q in range(2):
                        step(dve.tensor_copy(score[:, q, :], s[:, 2 * g + q, :]))
                    pause()
                    best([(score[:, q, :], top[:, q, :], ti[:, q, :]) for q in range(2)])
                    step(dve.tensor_copy(tf[:, :, :], ti[:, :, :]))
                    square = [P, TOPK, TOPK]
                    c3 = cand[:, :].rearrange("p (a b) -> p a b", a=TOPK)
                    step(dve.tensor_tensor(c3, top[:, 0, :].unsqueeze(2).broadcast_to(square),
                                           top[:, 1, :].unsqueeze(1).broadcast_to(square), ALU.add))
                    pause()
                    best([(cand[:, :], chosen[:, :], bi[:, :])])
                    step(dve.tensor_scalar(part[:, 0, :], bi[:, :], 4, None, ALU.logical_shift_right))
                    step(dve.tensor_scalar(part[:, 1, :], bi[:, :], 15, None, ALU.bitwise_and))
                    step(dve.tensor_scalar(gate[:, g, :], chosen[:, :], chosen[:, 0:1], None, ALU.subtract))
                    settle()
                    step(dve.tensor_copy(pf[:, :, :], part[:, :, :]))
                    settle()
                    for q in range(2):
                        step(dve.tensor_tensor(c3, pf[:, q, :].unsqueeze(2).broadcast_to(square),
                                               iota[:, :].unsqueeze(1).broadcast_to(square), ALU.is_equal))
                        settle()
                        step(dve.tensor_tensor(c3, c3, tf[:, q, :].unsqueeze(1).broadcast_to(square), ALU.mult))
                        settle()
                        step(dve.tensor_reduce(pf[:, q, :], c3, AX, ALU.add))
                        settle()
                    step(dve.scalar_tensor_tensor(out=pf[:, 0, :], in0=pf[:, 0, :], scalar=float(KEYS), in1=pf[:, 1, :],
                                                  op0=ALU.mult, op1=ALU.add))
                    settle()
                    step(dve.tensor_scalar(pf[:, 0, :], pf[:, 0, :], offset, None, ALU.add))
                    settle()
                    dve.tensor_copy(index[:, g, :], pf[:, 0, :]).then_inc(S["found"], 1)
                    steps["unit"] = count[0]

                def dots(g, t):
                    for k in range(TOPK):
                        dve.wait_ge(S[f"u{k % NG}"], PER * 16 * g + 16 * (k // NG + 1))
                        if k:
                            dve.wait_ge(S["dots"], TOPK * g + k)
                        dve.tensor_tensor_reduce(junk[:, :], ub[:, k % NG, :], xtok[:, t, :], 1.0, 0.0, ALU.mult,
                                                 ALU.add, acts[:, 0, k:k + 1]).then_inc(S["dots"], 1)

                def weigh(g):
                    dve.wait_ge(S["exp"], g + 1)
                    dve.tensor_reduce(den[:, :], gate[:, g, :], AX, ALU.add).then_inc(S["total"], 1)
                    dve.wait_ge(S["total"], g + 1)
                    dve.tensor_tensor(still[:, 63:64], still[:, 0:1], still[:, 0:1], ALU.mult)
                    dve.reciprocal(den[:, :], den[:, :]).then_inc(S["inverse"], 1)
                    dve.wait_ge(S["inverse"], g + 1)
                    dve.tensor_scalar(gate[:, g, :], gate[:, g, :], den[:, :], None, ALU.mult)\
                       .then_inc(S["gates"], 1)
                    dve.wait_ge(S["gates"], g + 1)
                    dve.wait_ge(S["gelu"], g + 1)
                    dve.tensor_tensor(wts[:, :], acts[:, 1, :], gate[:, g, :], ALU.mult).then_inc(S["weights"], 1)
                    dve.wait_ge(S["weights"], g + 1)
                    dve.wait_ge(S["sums"], TOPK * g + CLEARED)
                    for a, b in zip(DIAGONALS, DIAGONALS[1:] + (TOPK,)):
                        wide = [P, b - a, P]
                        dve.tensor_tensor(diag[:, a:b, :], C.sq["ident"].unsqueeze(1).broadcast_to(wide),
                                          wts[:, a:b].unsqueeze(2).broadcast_to(wide), ALU.mult)\
                           .then_inc(S["diag"], 1)

                dve.memset(zero[:, :], 0.0).then_inc(S["zero"], 1)
                S.link(dve, dve.memset(still[:, :], 0.0), "still")
                dve.wait_ge(S["scores_out"], 1)
                dve.wait_ge(S["iota"], 1)
                search(0)
                dve.wait_ge(S["scores_out"], GROUPS)
                dve.wait_ge(S["x_out"], 4)
                for t in range(TT):
                    with dve.Fori(t * PH, (t + 1) * PH - (t == TT - 1)) as g:
                        dots(g, t)
                        weigh(g)
                        search(g + 1)
                dots(U - 1, TT - 1)
                weigh(U - 1)
                dve.wait_ge(S["y_turned"], 1)
                for i in range(4):
                    c = slice(2 * i, 2 * i + 2)
                    dve.scalar_tensor_tensor(out=x1[:, c, :], in0=x1[:, c, :], scalar=DN_ALPHA,
                                             in1=C.bank[4 + i][:, :].rearrange("p (a c) -> p a c", a=2),
                                             op0=ALU.mult, op1=ALU.add).then_inc(S["x"], 1)
        S.close()


def layer(C, A, l_, xT):
    nc = C.nc
    with ExitStack() as outer:
        so = lambda name, shape: outer.enter_context(nc.sbuf_tensor(name, shape, F32))
        v2 = so("vec2", [P, VEC2_COLS])
        x1 = so("x1", [P, KT, SEQ])
        V = {name: v2[:, at:at + n] for name, (at, n) in VEC2_AT.items()}
        load_all(nc, "vec2", [(v2[:, :], A["vec2"][l_, :, :])])
        with ExitStack() as mid:
            sm = lambda name, shape: mid.enter_context(nc.sbuf_tensor(name, shape, F32))
            mg = sm("z_mg", [P, 4 * KT, SEQ])
            o = sm("z_o", [P, 8, SEQ])
            branch = [o[:, 2 * i:2 * i + 2, :] for i in range(4)]
            with ExitStack() as local:
                sl = lambda name, shape: local.enter_context(nc.sbuf_tensor(name, shape, F32))
                Z = {n: sl("z2_" + n, [P, 2, SEQ]) for n in ("sq", "sk", "sv", "rq", "rk", "rv", "rg", "gv", "gr")}
                Z["nq"], Z["kcv"], Z["nk"] = sl("z2_nq", [HD, 4, SEQ]), sl("z2_kcv", [HD, 2, SEQ]), sl("z2_nk", [HD, 2, SEQ])
                Z["nv"], Z["ng"], Z["lr"] = sl("z2_nv", [P, 2, P]), sl("z2_ng", [P, 2, 12]), sl("z2_lr", [32, SEQ])
                Z["gq"], Z["gk"], Z["gkt"] = sl("z2_gq", [P, SEQ]), sl("z2_gk", [P, SEQ]), sl("z2_gkt", [P, 2, P])
                S = Stage(nc, "lr_ones")
                with nc.Block() as block:
                    @block.vector
                    def _(dve):
                        S.link(dve, dve.memset(Z["lr"][:, :], 1.0), "ones")
                S.close()
                hv = local.enter_context(ExitStack())
                xh = hv.enter_context(nc.sbuf_tensor("x_halves", [P, 2, KT, SEQ], F32R))
                xs = (xh[:, 0, :, :], xh[:, 1, :, :])
                jobs = []

                def turned(tile, dst, func=None, width=P, at=0):
                    for i, d in enumerate(dst):
                        acts = xs if width == P else xT
                        jobs.append((tile, at + i * width, width, True, acts, 0, SEQ, d, func, None))

                def straight(tile, dst, width, at=0, func=None):
                    for t in range(TT):
                        jobs.append((tile, at, width, False, xs, t * P, P, dst[:, t, 0:width], func, None))

                two = lambda a: [a[:, 0, :], a[:, 1, :]]
                turned(0, two(Z["sq"]))
                turned(1, two(Z["sk"]))
                straight(2, Z["sv"], 256)
                turned(3, [Z["nq"][:, i, :] for i in range(4)], width=HD)
                turned(4, two(Z["kcv"]) + two(Z["nk"]), width=HD)
                straight(5, Z["nv"], 128)
                straight(5, Z["ng"], 12, 128, ACT.Sigmoid)
                turned(5, [Z["lr"][0:16, :]], width=16, at=140)
                turned(6, two(Z["rq"]))
                turned(7, two(Z["rk"]))
                straight(8, Z["rv"], 256)
                turned(9, two(Z["rg"]), ACT.Silu)
                turned(10, [Z["gq"][:, :], Z["gk"][:, :]])
                straight(10, Z["gkt"], 128, 128)
                straight(11, Z["gv"], 256)
                turned(12, two(Z["gr"]), ACT.Silu)
                for i in range(16):
                    turned(13 + i, [mg[:, 2 * i, :], mg[:, 2 * i + 1, :]], ACT.Sigmoid)
                linear(C, "w_in2", [A["w_in2"][l_ * TILES2 + i, :, :] for i in range(TILES2)], jobs,
                       pairs=channel_tiles(xT, xh))
                hv.close()
                stick_breaking(C, A, Z, branch[0])
                nsa(C, A, l_, Z, branch[1])
                retention(C, A, Z, branch[2])
                head_norm(C, "ret_norm", branch[2], branch[2], 2, V["gn_g"], V["gn_b"], True, nt=2)
                gla(C, A, l_, Z, branch[3])
                head_norm(C, "gla_norm", branch[3], branch[3], 2, V["gla_g"], None, False, nt=2)
                times(C, "out_gates", [(branch[2], Z["rg"][:, :, :]), (branch[3], Z["gr"][:, :, :])])
            with ExitStack() as local:
                pr = local.enter_context(nc.sbuf_tensor("pr", [P, 4 * KT, SEQ], F32))
                os = local.enter_context(nc.sbuf_tensor("o_halves", [P, 2, KT, SEQ], F32R))
                jobs = [(i, m * P, P, True, tuple(os[:, q, 2 * i:2 * i + 2, :] for q in range(2)), 0, SEQ,
                         pr[:, i * KT + m, :], None, mg[:, i * KT + m, :]) for i in range(4) for m in range(KT)]

                def merge(S, dve):
                    for n, (a, b) in enumerate(((0, 2), (1, 3), (0, 1))):
                        ra, rb = slice(a * KT, (a + 1) * KT), slice(b * KT, (b + 1) * KT)
                        S.link(dve, dve.tensor_tensor(pr[:, ra, :], pr[:, ra, :], pr[:, rb, :], ALU.add), "merged")

                linear(C, "w_branch", [A["w_branch"][l_ * 4 + i, :, :] for i in range(4)], jobs, kt=2, extra=merge,
                       pairs=channel_tiles(o, os))
                jobs = [(m // 2, P * (m % 2), P, True, (os[:, 0, :, :], os[:, 1, :, :]), 0, SEQ, x1[:, m, :], None,
                         None) for m in range(KT)]

                def residual(S, dve):
                    S.link(dve, dve.scalar_tensor_tensor(out=x1[:, :, :], in0=xT[:, :, :], scalar=DN_ALPHA,
                                                         in1=x1[:, :, :], op0=ALU.mult, op1=ALU.add), "x")
                linear(C, "w_out2", [A["w_out2"][l_ * 4 + i, :, :] for i in range(4)], jobs, extra=residual,
                       pairs=channel_tiles(pr, os))
        norm(C, "ln1", [(x1[:, :, :], x1[:, :, :], V["ln1_g"], V["ln1_b"], SEQ)], 2, centred=True)
        with ExitStack() as local:
            qv = local.enter_context(nc.sbuf_tensor("peer_q", [P, 2 * PH, SEQ], F32))
            hv = local.enter_context(ExitStack())
            xh = hv.enter_context(nc.sbuf_tensor("x1_halves", [P, 2, KT, SEQ], F32R))
            xs = (xh[:, 0, :, :], xh[:, 1, :, :])
            jobs = [(m // 2, P * (m % 2), P, True, xs, 0, SEQ, qv[:, m, :], None, None) for m in range(2 * PH)]
            linear(C, "peer_wq", [A["peer_wq"][l_ * 8 + i, :, :] for i in range(8)], jobs,
                   pairs=channel_tiles(x1, xh))
            hv.close()
            peer(C, A, l_, qv, x1, V["offset"])
        norm(C, "ln2", [(x1[:, :, :], xT[:, :, :], V["ln2_g"], V["ln2_b"], SEQ)], 2, centred=True)


def second_block(C, A, xT):
    norm(C, "ln_in", [(xT[:, :, :], xT[:, :, :], C.v["lnin_g"], C.v["lnin_b"], SEQ)], 2, centred=True)
    with C.nc.Fori(0, 2) as l_:
        layer(C, A, l_, xT)


VEC2 = [("gn_g", 2), ("gn_b", 2), ("gla_g", 2), ("ln1_g", 8), ("ln1_b", 8), ("ln2_g", 8), ("ln2_b", 8), ("offset", 1)]
VEC2_AT, VEC2_COLS = {}, 0
for _name, _n in VEC2:
    VEC2_AT[_name] = (VEC2_COLS, _n)
    VEC2_COLS += _n


def build(nc, A, out):
    with ExitStack() as ctx:
        C = Core(nc, ctx)
        square = C.keep("square", [P, len(SQUARE), P])
        C.sq = {k: square[:, i, :] for i, k in enumerate(SQUARE)}
        epst = C.keep("eps", [P, len(EPS)])
        C.eps = [epst[:, i:i + 1] for i in range(len(EPS))]
        C.mask4 = C.keep("mask4", [P, 2, 4 * P])
        vec = C.keep("vec", [P, VEC_COLS])
        C.v = {}
        for name, (at, n) in VEC_AT.items():
            C.v[name] = vec[:, at:at + n]
        xT = C.keep("xT", [P, KT, SEQ])
        load_all(nc, "start", [(square[:, :, :], A["square"]), (epst[:, :], A["eps"]),
                               (C.mask4[:, :, :], A["mask4"]), (vec[:, :], A["vec"]), (xT[:, :, :], A["xT"])])
        S = Stage(nc, "one_minus")
        with nc.Block() as block:
            @block.vector
            def _(dve):
                S.link(dve, dve.tensor_scalar(C.v["one_minus_k_a"], C.v["k_a"], -1.0, 1.0, ALU.mult, ALU.add), "k_a")
        S.close()
        first_block(C, A, xT)
        second_block(C, A, xT)
        S = Stage(nc, "end")
        with nc.Block() as block:
            @block.sync
            def _(sp):
                sp.dma_start(out, xT[:, :, :]).then_inc(S["out"], 16)
                sp.wait_ge(S["out"], 16)
        S.close()


VEC = [("norm1_g", 8), ("norm2_g", 8), ("k_k", 4), ("k_a", 4), ("one_minus_k_a", 4), ("a0", 8), ("r_k", 4),
       ("ln_g", 4), ("ln_b", 4), ("q_g", 4), ("k_g", 4), ("lnin_g", 8), ("lnin_b", 8)]
VEC_AT, VEC_COLS = {}, 0
for _name, _n in VEC:
    VEC_AT[_name] = (VEC_COLS, _n)
    VEC_COLS += _n


def columns(a):
    return np.asarray(a).reshape(-1, P).T


def tiled(w, cols):
    K, N = w.shape
    return np.ascontiguousarray(w.reshape(K // P, P, N // cols, cols).transpose(2, 1, 0, 3)
                                .reshape(N // cols, P, K // P * cols))


def turn(x):
    return np.ascontiguousarray(x.T.reshape(-1, P, x.shape[0]).transpose(1, 0, 2))


def window_bias(rpb):
    W, rows = 64, SEQ // 64
    q, k = np.arange(SEQ)[:, None], np.arange(SEQ)[None, :]
    drow = k // W - q // W + 7
    dcol = np.clip(k % W - q % W, -15, 15) + 15
    return np.ascontiguousarray(rpb[:, drow, dcol].reshape(NH, TT, P, SEQ))


def window_mask():
    j = np.arange(64)
    start = np.clip(j - 8, 0, 64 - 16)
    inside = (j[None, :] >= start[:, None]) & (j[None, :] < start[:, None] + 16)
    m = np.where(inside, 0.0, NEG).astype(np.float32)
    return np.ascontiguousarray(np.tile(m, (4, 4)).reshape(TT, P, SEQ).transpose(1, 0, 2))


def lay_out(I):
    f = {k: np.asarray(v) for k, v in I.items()}
    A = {}
    A["square"], A["eps"] = square_array(), eps_array()
    c = constants_square()
    A["mask4"] = np.ascontiguousarray(np.stack(
        [np.concatenate([c["m_" + s + "_ex"], c["m_" + s + "_in"]] * 2, 1) for s in SIDES], 1))
    vec = {"norm1_g": f["norm1_g"][0], "norm2_g": f["norm2_g"][0], "k_k": f["rw_k_k"][0], "k_a": f["rw_k_a"][0],
           "a0": f["rw_a0"][0].reshape(-1), "r_k": f["rw_r_k"][0].reshape(-1), "ln_g": f["rw_ln_g"][0],
           "ln_b": f["rw_ln_b"][0], "q_g": np.tile(f["na_q_g"][0], NH), "k_g": np.tile(f["na_k_g"][0], NH),
           "lnin_g": f["ln_in_g_2"], "lnin_b": f["ln_in_b_2"]}
    v = np.zeros((P, VEC_COLS), np.float32)
    for name, (at, n) in VEC_AT.items():
        if name in vec:
            v[:, at:at + n] = columns(vec[name])
    A["vec"] = v
    A["xT"], A["ctxT"] = turn(f["x"][0]), turn(f["ctx"][0])
    A["cond"] = np.ascontiguousarray(np.stack([columns(f["c"][0]), columns(f["c_ctx"])], 2))
    A["mod_b"] = np.ascontiguousarray(columns(f["mod_b"][0]))
    A["mod_w"] = tiled(f["mod_w"][0], 256)
    w = f["w_in"][0]
    A["w_in"] = tiled(np.concatenate([w[:, :1920], np.zeros((D, 128), np.float32), w[:, 1920:]], 1), 256)
    A["rw_w_lora_b"] = np.ascontiguousarray(f["rw_w_lora_b"][0].reshape(P, -1))
    A["rw_a_lora_b"] = np.ascontiguousarray(f["rw_a_lora_b"][0].reshape(P, -1))
    w0 = np.zeros((P, NH * HD), np.float32)
    w0[0], w0[64] = f["rw_w0"][0, 0], f["rw_w0"][0, 1]
    A["rw_w0"] = w0
    A["rw_g_lora_b"] = np.ascontiguousarray(f["rw_g_lora_b"][0])
    A["na_bias"], A["na_mask"] = window_bias(f["na_rpb"][0]), window_mask()
    A["proj_ab"] = np.concatenate([tiled(f["proj_a"][0], 512), tiled(f["proj_b"][0], 512)], 0)
    A["w_out"] = tiled(f["w_out"][0], 256)
    A["router_w"] = np.ascontiguousarray(f["router_w"].reshape(KT, P, N_EXP).transpose(1, 0, 2))
    A["router_bias"] = np.ascontiguousarray(np.tile(f["router_bias"][None], (P, 1)))
    A["pick"] = np.ascontiguousarray(np.repeat(np.eye(N_EXP, dtype=np.float32)[:, :, None], P, 2))
    moe = []
    for e in range(N_EXP + 1):
        if e < N_EXP:
            w1, w3 = f["moe_w1"][0, e].reshape(D, 4, P), f["moe_w3"][0, e].reshape(D, 4, P)
            up = tiled(np.concatenate([w1, w3], 2).reshape(D, 8 * P), 256)
            moe.append(up[0:1])
        if e:
            moe.append(tiled(f["moe_w2"][0, e - 1], 512))
        if e < N_EXP:
            moe.append(up[1:4])
    A["moe"] = np.concatenate(moe, 0)
    L = 2
    s, t = np.arange(SEQ)[:, None], np.arange(SEQ)[None, :]
    halves = lambda a: np.ascontiguousarray(a.reshape(TT, P, SEQ).transpose(1, 0, 2).reshape(P, TT * SEQ))
    A["causal"] = halves((s < t).astype(np.float32))
    slopes = 2.0 ** (-8.0 * np.arange(1, H4 + 1) / H4)
    tok = np.arange(SEQ)[:, None]
    end = np.arange(N_CMP)[None, :] * 16 + 31
    cb = np.where(tok >= end, -slopes[:, None, None] * (tok - end), NEG)
    A["cmp_bias"] = np.ascontiguousarray(cb.reshape(H4, TT, P, N_CMP).transpose(2, 1, 0, 3)
                                         .reshape(P, TT * H4, N_CMP).astype(np.float32))
    A["cmp_seen"] = np.ascontiguousarray((np.arange(SEQ) >= 31).astype(np.float32).reshape(TT, P).T)
    lb = np.where(t <= s, -slopes[:, None, None] * (s - t), NEG)
    A["lin_bias"] = np.ascontiguousarray(lb.reshape(H4, TT, P, SEQ).transpose(2, 1, 0, 3)
                                         .reshape(P, TT * H4, SEQ).astype(np.float32))
    log_g = np.log1p(-(2.0 ** (-5.0 - np.arange(H4))))
    dec = np.where(s <= t, np.exp(log_g[:, None, None] * np.maximum(t - s, 0)), 0.0) * HD ** -0.5
    A["ret_decay"] = np.ascontiguousarray(np.stack([halves(d.astype(np.float32)) for d in dec], 1))
    A["gla_heads"] = (np.arange(P)[:, None] // 32 == np.arange(H4)[None, :]).astype(np.float32)
    A["gla_blocks"] = (np.arange(P)[:, None] // 32 == np.arange(MIX)[None, :] // HD).astype(np.float32)
    w = f["w_in_2"]
    cols = lambda a, n: w[:, :, a:a + n]
    w = np.concatenate([cols(0, 1024), cols(1024, 128), cols(1152, 64), cols(1280, 64), cols(1216, 64), cols(1344, 64),
                        cols(1408, 12), cols(3212, 16), np.zeros((L, D, 100), np.float32), cols(1420, 1792),
                        cols(3228, 4096)], 2)
    A["w_in2"] = np.concatenate([tiled(w[i], 256) for i in range(L)], 0)
    cw = np.stack([f["nsa_cmp_wk_2"], f["nsa_cmp_wv_2"]], 1).reshape(L, 2, 32, HD, HD)
    A["cmp_w"] = np.ascontiguousarray(cw.transpose(0, 3, 1, 2, 4))
    A["cmp_pos"] = np.ascontiguousarray(f["nsa_cmp_pos_2"].transpose(0, 2, 1))
    A["gla_wa"] = np.concatenate([f["gla_w_alpha_2"], f["gla_b_alpha_2"][:, None, :]], 1)
    A["w_branch"] = np.concatenate([tiled(f["w_branch_2"][i, j], 1024) for i in range(L) for j in range(4)], 0)
    A["w_out2"] = np.concatenate([tiled(f["w_out_2"][i], 256) for i in range(L)], 0)
    A["peer_wq"] = np.concatenate([tiled(f["peer_wq_2"][i], 256) for i in range(L)], 0)
    A["peer_keys"] = np.ascontiguousarray(f["peer_keys_2"].reshape(L, 2 * PH, KEYS, P).transpose(0, 3, 1, 2))
    A["peer_u"] = f["peer_u_2"].reshape(-1, D)
    A["peer_v"] = f["peer_v_2"].reshape(-1, D)
    vec2 = {"gn_g": "ret_gn_g_2", "gn_b": "ret_gn_b_2", "gla_g": "gla_norm_g_2", "ln1_g": "ln1_g_2",
            "ln1_b": "ln1_b_2", "ln2_g": "ln2_g_2", "ln2_b": "ln2_b_2"}
    v = np.zeros((L, P, VEC2_COLS), np.float32)
    for i in range(L):
        for name, (at, n) in VEC2_AT.items():
            v[i, :, at:at + n] = i * KEYS * KEYS if name == "offset" else columns(f[vec2[name]][i])
    A["vec2"] = v
    return A


def kernel(**inputs):
    import concourse.bacc as bacc
    from concourse.bass_utils import run_bass_kernel_spmd

    nc = bacc.Bacc("TRN2", target_bir_lowering=False, num_devices=1)
    arrays, A = {}, {}
    for name, a in lay_out(inputs).items():
        arrays[f"in_{name}"] = a
        A[name] = nc.dram_tensor(f"in_{name}", a.shape, mybir.dt.from_np(a.dtype), kind="ExternalInput").ap()
    out = nc.dram_tensor("out_xT", (P, KT, SEQ), F32, kind="ExternalOutput").ap()
    build(nc, A, out)
    r = run_bass_kernel_spmd(nc, [arrays], core_ids=[0])
    y = np.asarray(r.results[0]["out_xT"])
    return np.ascontiguousarray(y.transpose(2, 1, 0).reshape(1, SEQ, D))
```
